# Optimizing a Trainium2 kernel written in Bass

```python
import math
import jax, jax.numpy as jnp
from jax import lax
import numpy as np

D_MODEL = 1024
BATCH = 1
SEQ = 512
DEPTH = 1
DEC_BATCH = 8
DEC_SEQ = 4
PAST_LEN = 4096
PAGE_SIZE = 128

SSD_INNER = D_MODEL
SSD_HEADDIM = 64
SSD_HEADS = SSD_INNER // SSD_HEADDIM
SSD_GROUPS = 2
SSD_REP = SSD_HEADS // SSD_GROUPS
SSD_STATE = 128
SSD_CONV = 4
SSD_CONV_DIM = SSD_INNER + 2 * SSD_GROUPS * SSD_STATE
CHUNK = 128
M_HEADS = 4
M_INNER = D_MODEL
M_HEADDIM = M_INNER // M_HEADS
POOL_WINDOWS = (2, 4, 8, 16)
POOL_GROUPS = len(POOL_WINDOWS)
POOL_WIDTH = D_MODEL
POOL_GW = POOL_WIDTH // POOL_GROUPS
POOL_BUF = max(POOL_WINDOWS) - 1
N_BRANCH = 3
N_EGROUPS = 4
EXP_PER_GROUP = 4
N_EXPERTS = N_EGROUPS * EXP_PER_GROUP
TOP_K = 2
D_FF_E = D_MODEL // 4
ALPHA = (2 * DEPTH) ** 0.25
BETA = (8 * DEPTH) ** -0.25
LN_EPS = 1e-5
RMS_EPS = 1e-6

_IN_SIZES = (SSD_INNER, SSD_CONV_DIM, SSD_HEADS,
             M_INNER, M_INNER, M_INNER, M_HEADS, M_HEADS, M_INNER,
             POOL_WIDTH,
             N_BRANCH * D_MODEL)
IN_DIM = sum(_IN_SIZES)
_IN_OFFSETS = tuple(int(v) for v in np.cumsum(_IN_SIZES)[:-1])

kernel_name = "hybrid_ssd_mlstm_pool_hmoe_decoder_step"

def layer_norm(x, g, b):
    xf = x.astype(jnp.float32)
    mu = xf.mean(-1, keepdims=True)
    var = jnp.square(xf - mu).mean(-1, keepdims=True)
    return ((xf - mu) * lax.rsqrt(var + LN_EPS) * g + b).astype(x.dtype)

def rms_norm(x, g):
    xf = x.astype(jnp.float32)
    return (xf * lax.rsqrt(jnp.square(xf).mean(-1, keepdims=True) + RMS_EPS) * g).astype(x.dtype)

def head_norm(h):
    mu = h.mean(-1, keepdims=True)
    var = jnp.square(h - mu).mean(-1, keepdims=True)
    return (h - mu) * lax.rsqrt(var + LN_EPS)

def ada_mod(c, w, b):
    m = c @ w + b
    shift, scale, gate = jnp.split(m, 3, axis=-1)
    return shift[:, None], scale[:, None], gate[:, None]

def _chunks(a, nc, L):
    return jnp.moveaxis(a.reshape(a.shape[0], nc, L, *a.shape[2:]), 1, 0)

def causal_conv(u, buf, w, b):
    t = u.shape[1]
    z = jnp.concatenate([buf.astype(u.dtype), u], axis=1)
    y = sum(z[:, k:k + t] * w[k] for k in range(SSD_CONV)) + b
    return jax.nn.silu(y), z[:, -(SSD_CONV - 1):]

def ssd_scan(x, dt, A, Bm, Cm, s0):
    t = x.shape[1]
    L = math.gcd(t, CHUNK)
    nc = t // L
    causal = jnp.tril(jnp.ones((L, L), bool))

    def step(s, inp):
        xc, dtc, Bc, Cc = inp
        cum = jnp.cumsum(dtc * A, axis=1)
        cum_h = jnp.moveaxis(cum, 1, -1)
        seg = jnp.where(causal, cum_h[..., :, None] - cum_h[..., None, :], -jnp.inf)
        cb = jnp.einsum('blgn,bsgn->bgls', Cc, Bc)
        w = cb[:, :, None] * jnp.exp(seg) * jnp.moveaxis(dtc, 1, -1)[..., None, :]
        y = jnp.einsum('bgrls,bsgrp->blgrp', w, xc)
        y = y + jnp.einsum('blgn,bgrpn->blgrp', Cc, s) * jnp.exp(cum)[..., None]
        last = cum[:, -1]
        ws = jnp.exp(last[:, None] - cum) * dtc
        s = jnp.exp(last)[..., None, None] * s + jnp.einsum('bsgr,bsgn,bsgrp->bgrpn', ws, Bc, xc)
        return s, y

    s, ys = lax.scan(step, s0, (_chunks(x, nc, L), _chunks(dt, nc, L), _chunks(Bm, nc, L), _chunks(Cm, nc, L)))
    return jnp.moveaxis(ys, 0, 1).reshape(x.shape), s

def mlstm_scan(q, k, v, logi, logf, C0, n0, m0):
    t = q.shape[1]
    L = math.gcd(t, CHUNK)
    nc = t // L
    causal = jnp.tril(jnp.ones((L, L), bool))

    def step(carry, inp):
        C, n, mp = carry
        qc, kc, vc, ic, fc = inp
        bcum = jnp.moveaxis(jnp.cumsum(fc, axis=1), 1, -1)
        ih = jnp.moveaxis(ic, 1, -1)
        dmat = jnp.where(causal, bcum[..., :, None] - bcum[..., None, :] + ih[..., None, :], -jnp.inf)
        m_st = bcum + mp[..., None]
        m = jnp.maximum(m_st, dmat.max(-1))
        wts = jnp.exp(dmat - m[..., None]) * jnp.einsum('blhk,bshk->bhls', qc, kc)
        ws = jnp.exp(m_st - m)
        num = jnp.einsum('bhls,bshv->bhlv', wts, vc) + ws[..., None] * jnp.einsum('bhvk,blhk->bhlv', C, qc)
        den = wts.sum(-1) + ws * jnp.einsum('bhk,blhk->bhl', n, qc)
        hc = num / jnp.maximum(jnp.abs(den), jnp.exp(-m))[..., None]
        last_b = bcum[..., -1]
        m_new = m[..., -1]
        wsrc = jnp.exp(last_b[..., None] - bcum + ih - m_new[..., None])
        wprev = jnp.exp(last_b + mp - m_new)
        C = wprev[..., None, None] * C + jnp.einsum('bhs,bshv,bshk->bhvk', wsrc, vc, kc)
        n = wprev[..., None] * n + jnp.einsum('bhs,bshk->bhk', wsrc, kc)
        return (C, n, m_new), jnp.moveaxis(hc, 2, 1)

    (C, n, m), hs = lax.scan(step, (C0, n0, m0),
                             (_chunks(q, nc, L), _chunks(k, nc, L), _chunks(v, nc, L),
                              _chunks(logi, nc, L), _chunks(logf, nc, L)))
    return jnp.moveaxis(hs, 0, 1).reshape(q.shape[0], t, q.shape[2], v.shape[3]), C, n, m

def pool_mix(u, buf, pool_valid, pool_w, pool_scale):
    b, t, _ = u.shape
    z = jnp.concatenate([buf.astype(u.dtype), u], axis=1)
    zf = z.astype(jnp.float32)
    cs = jnp.concatenate([jnp.zeros_like(zf[:, :1]), jnp.cumsum(zf, axis=1)], axis=1)
    n_avail = jnp.arange(t) + 1 + pool_valid
    means = []
    for g, w in enumerate(POOL_WINDOWS):
        sl = slice(g * POOL_GW, (g + 1) * POOL_GW)
        wsum = cs[:, POOL_BUF + 1:, sl] - cs[:, POOL_BUF + 1 - w:POOL_BUF + 1 - w + t, sl]
        cnt = jnp.minimum(n_avail, w).astype(jnp.float32)[None, :, None]
        means.append(wsum / cnt)
    mean = jnp.stack(means, axis=2)
    d = (mean - u.astype(jnp.float32).reshape(b, t, POOL_GROUPS, POOL_GW)).astype(u.dtype)
    y = jnp.einsum('btgc,gcd->btgd', d, pool_w).reshape(b, t, POOL_WIDTH) * pool_scale
    return y, z[:, -POOL_BUF:]

def token_mixers(u, states, pool_valid, lw):
    ssd_s, conv_s, C_s, n_s, m_s, pool_s = states
    b, t, _ = u.shape
    f32 = jnp.float32
    z, xbc, dt, q, k, v, ig, fg, og, up, gl = jnp.split(u @ lw['w_in'], _IN_OFFSETS, axis=-1)
    xbc, conv_new = causal_conv(xbc, conv_s, lw['conv_w'], lw['conv_b'])
    xs, bm, cm = jnp.split(xbc, [SSD_INNER, SSD_INNER + SSD_GROUPS * SSD_STATE], axis=-1)
    dtp = jax.nn.softplus((dt + lw['ssd_dt_bias']).astype(f32)).reshape(b, t, SSD_GROUPS, SSD_REP)
    A = -jnp.exp(lw['ssd_A_log'].astype(f32)).reshape(SSD_GROUPS, SSD_REP)
    x5 = xs.astype(f32).reshape(b, t, SSD_GROUPS, SSD_REP, SSD_HEADDIM)
    y, ssd_new = ssd_scan(x5, dtp, A,
                          bm.astype(f32).reshape(b, t, SSD_GROUPS, SSD_STATE),
                          cm.astype(f32).reshape(b, t, SSD_GROUPS, SSD_STATE),
                          ssd_s.astype(f32).reshape(b, SSD_GROUPS, SSD_REP, SSD_HEADDIM, SSD_STATE))
    y = y + lw['ssd_D'].astype(f32).reshape(SSD_GROUPS, SSD_REP)[..., None] * x5
    y_ssd = rms_norm(y.reshape(b, t, SSD_INNER).astype(u.dtype) * jax.nn.silu(z), lw['ssd_norm_w'])
    qh = q.astype(f32).reshape(b, t, M_HEADS, M_HEADDIM)
    kh = k.astype(f32).reshape(b, t, M_HEADS, M_HEADDIM) * (M_HEADDIM ** -0.5)
    vh = v.astype(f32).reshape(b, t, M_HEADS, M_HEADDIM)
    logi = (ig + lw['mlstm_gate_b'][:M_HEADS]).astype(f32)
    logf = jax.nn.log_sigmoid((fg + lw['mlstm_gate_b'][M_HEADS:]).astype(f32))
    h, C_new, n_new, m_new = mlstm_scan(qh, kh, vh, logi, logf,
                                        C_s.astype(f32), n_s.astype(f32), m_s.astype(f32))
    hn = head_norm(h) * lw['mlstm_norm_w'].reshape(M_HEADS, M_HEADDIM)
    y_m = hn.reshape(b, t, M_INNER).astype(u.dtype) * jax.nn.sigmoid(og)
    y_pool, pool_new = pool_mix(up, pool_s, pool_valid, lw['pool_w'], lw['pool_scale'])
    g = jax.nn.sigmoid(gl + lw['gate_b']).reshape(b, t, N_BRANCH, D_MODEL)
    merged = (g[:, :, 0] * (y_ssd @ lw['w_br_ssd'])
              + g[:, :, 1] * (y_m @ lw['w_br_mlstm'])
              + g[:, :, 2] * (y_pool @ lw['w_br_pool']))
    out = merged @ lw['w_out']
    new_states = (ssd_new.reshape(b, SSD_HEADS, SSD_HEADDIM, SSD_STATE).astype(ssd_s.dtype),
                  conv_new.astype(conv_s.dtype), C_new.astype(C_s.dtype), n_new.astype(n_s.dtype),
                  m_new.astype(m_s.dtype), pool_new.astype(pool_s.dtype))
    return out, new_states

def hier_moe(u, lw):
    f32 = jnp.float32
    p_grp = jax.nn.softmax((u @ lw['w_rt_group'] + lw['b_rt_group']).astype(f32), axis=-1)
    gp, gi = lax.top_k(p_grp, 1)
    le = (u @ lw['w_rt_expert'] + lw['b_rt_expert']).astype(f32)
    le = le.reshape(*u.shape[:-1], N_EGROUPS, EXP_PER_GROUP)
    le_g = jnp.take_along_axis(le, gi[..., None], axis=-2)[..., 0, :]
    lk, ik = lax.top_k(le_g, TOP_K)
    pk = jax.nn.softmax(lk, axis=-1) * gp
    eidx = gi * EXP_PER_GROUP + ik
    wts = jnp.sum(jax.nn.one_hot(eidx, N_EXPERTS, dtype=f32) * pk[..., None], axis=-2)
    h = jax.nn.silu(jnp.einsum('btd,edf->btef', u, lw['w_e_gate'])) * jnp.einsum('btd,edf->btef', u, lw['w_e_up'])
    h = h * wts.astype(h.dtype)[..., None]
    return jnp.einsum('btef,efd->btd', h, lw['w_e_down'])

def decoder_layer(x, c, states, pool_valid, lw):
    shift, scale, gate = ada_mod(c, lw['w_ada_mix'], lw['b_ada_mix'])
    mix, new_states = token_mixers(x * (1 + scale) + shift, states, pool_valid, lw)
    x = layer_norm(ALPHA * x + (1 + gate) * mix, lw['ln1_g'], lw['ln1_b'])
    shift, scale, gate = ada_mod(c, lw['w_ada_ffn'], lw['b_ada_ffn'])
    ffn = hier_moe(x * (1 + scale) + shift, lw)
    x = layer_norm(ALPHA * x + (1 + gate) * ffn, lw['ln2_g'], lw['ln2_b'])
    return x, new_states

def setup_inputs(seed: int = 0) -> dict:
    key = jax.random.key(seed)
    ks = jax.random.split(key, 40)
    f32 = jnp.float32

    def nrm(i, shape, scale):
        return jax.random.normal(ks[i], shape, f32) * scale

    dt0 = jnp.exp(jax.random.uniform(ks[30], (DEPTH, SSD_HEADS), f32, math.log(1e-3), math.log(1e-1)))
    mlstm_gate_b = jnp.concatenate(
        [nrm(31, (DEPTH, M_HEADS), 0.1),
         jnp.linspace(3.0, 6.0, M_HEADS, dtype=f32)[None] + nrm(32, (DEPTH, M_HEADS), 0.1)], axis=-1)
    return {
        "x_prompt": nrm(0, (BATCH, SEQ, D_MODEL), 1.0),
        "x_sample": nrm(1, (DEC_BATCH, DEC_SEQ, D_MODEL), 1.0),
        "state_ssd": nrm(2, (DEPTH, DEC_BATCH, SSD_HEADS, SSD_HEADDIM, SSD_STATE), 0.1),
        "state_conv": nrm(3, (DEPTH, DEC_BATCH, SSD_CONV - 1, SSD_CONV_DIM), 1.0),
        "state_mlstm_C": nrm(4, (DEPTH, DEC_BATCH, M_HEADS, M_HEADDIM, M_HEADDIM), 0.1),
        "state_mlstm_n": jnp.abs(nrm(5, (DEPTH, DEC_BATCH, M_HEADS, M_HEADDIM), 1.0)),
        "state_mlstm_m": nrm(6, (DEPTH, DEC_BATCH, M_HEADS), 1.0),
        "state_pool": nrm(7, (DEPTH, DEC_BATCH, POOL_BUF, POOL_WIDTH), 1.0),
        "c_prompt": nrm(8, (BATCH, D_MODEL), 1.0),
        "c_sample": nrm(9, (DEC_BATCH, D_MODEL), 1.0),
        "w_ada_mix": nrm(10, (DEPTH, D_MODEL, 3 * D_MODEL), 0.1 * D_MODEL ** -0.5),
        "b_ada_mix": nrm(11, (DEPTH, 3 * D_MODEL), 0.01),
        "w_in": nrm(12, (DEPTH, D_MODEL, IN_DIM), D_MODEL ** -0.5),
        "conv_w": nrm(13, (DEPTH, SSD_CONV, SSD_CONV_DIM), SSD_CONV ** -0.5),
        "conv_b": nrm(14, (DEPTH, SSD_CONV_DIM), 0.01),
        "ssd_A_log": jnp.log(jax.random.uniform(ks[15], (DEPTH, SSD_HEADS), f32, 1.0, 16.0)),
        "ssd_dt_bias": dt0 + jnp.log(-jnp.expm1(-dt0)),
        "ssd_D": 1.0 + nrm(16, (DEPTH, SSD_HEADS), 0.1),
        "ssd_norm_w": 1.0 + nrm(17, (DEPTH, SSD_INNER), 0.1),
        "mlstm_gate_b": mlstm_gate_b,
        "mlstm_norm_w": 1.0 + nrm(18, (DEPTH, M_INNER), 0.1),
        "pool_w": nrm(19, (DEPTH, POOL_GROUPS, POOL_GW, POOL_GW), POOL_GW ** -0.5),
        "pool_scale": 1.0 + nrm(20, (DEPTH, POOL_WIDTH), 0.1),
        "gate_b": nrm(21, (DEPTH, N_BRANCH * D_MODEL), 0.01),
        "w_br_ssd": nrm(22, (DEPTH, SSD_INNER, D_MODEL), SSD_INNER ** -0.5),
        "w_br_mlstm": nrm(23, (DEPTH, M_INNER, D_MODEL), M_INNER ** -0.5),
        "w_br_pool": nrm(24, (DEPTH, POOL_WIDTH, D_MODEL), POOL_WIDTH ** -0.5),
        "w_out": nrm(25, (DEPTH, D_MODEL, D_MODEL), BETA * D_MODEL ** -0.5),
        "ln1_g": 1.0 + nrm(26, (DEPTH, D_MODEL), 0.1),
        "ln1_b": nrm(27, (DEPTH, D_MODEL), 0.01),
        "w_ada_ffn": nrm(28, (DEPTH, D_MODEL, 3 * D_MODEL), 0.1 * D_MODEL ** -0.5),
        "b_ada_ffn": nrm(29, (DEPTH, 3 * D_MODEL), 0.01),
        "w_rt_group": nrm(33, (DEPTH, D_MODEL, N_EGROUPS), D_MODEL ** -0.5),
        "b_rt_group": nrm(34, (DEPTH, N_EGROUPS), 0.01),
        "w_rt_expert": nrm(35, (DEPTH, D_MODEL, N_EXPERTS), D_MODEL ** -0.5),
        "b_rt_expert": nrm(36, (DEPTH, N_EXPERTS), 0.01),
        "w_e_gate": nrm(37, (DEPTH, N_EXPERTS, D_MODEL, D_FF_E), D_MODEL ** -0.5),
        "w_e_up": nrm(38, (DEPTH, N_EXPERTS, D_MODEL, D_FF_E), D_MODEL ** -0.5),
        "w_e_down": nrm(39, (DEPTH, N_EXPERTS, D_FF_E, D_MODEL), BETA * D_FF_E ** -0.5),
        "ln2_g": 1.0 + jax.random.normal(jax.random.fold_in(key, 101), (DEPTH, D_MODEL), f32) * 0.1,
        "ln2_b": jax.random.normal(jax.random.fold_in(key, 102), (DEPTH, D_MODEL), f32) * 0.01,
    }

def reference(x_prompt, x_sample, state_ssd, state_conv, state_mlstm_C, state_mlstm_n, state_mlstm_m,
              state_pool, c_prompt, c_sample, w_ada_mix, b_ada_mix, w_in, conv_w, conv_b, ssd_A_log,
              ssd_dt_bias, ssd_D, ssd_norm_w, mlstm_gate_b, mlstm_norm_w, pool_w, pool_scale, gate_b,
              w_br_ssd, w_br_mlstm, w_br_pool, w_out, ln1_g, ln1_b, w_ada_ffn, b_ada_ffn, w_rt_group,
              b_rt_group, w_rt_expert, b_rt_expert, w_e_gate, w_e_up, w_e_down, ln2_g, ln2_b):
    bp = x_prompt.shape[0]
    dt_p = x_prompt.dtype
    st_dt = state_ssd.dtype
    prompt_init = (jnp.zeros((bp, SSD_HEADS, SSD_HEADDIM, SSD_STATE), st_dt),
                   jnp.zeros((bp, SSD_CONV - 1, SSD_CONV_DIM), dt_p),
                   jnp.zeros((bp, M_HEADS, M_HEADDIM, M_HEADDIM), st_dt),
                   jnp.zeros((bp, M_HEADS, M_HEADDIM), st_dt),
                   jnp.zeros((bp, M_HEADS), st_dt),
                   jnp.zeros((bp, POOL_BUF, POOL_WIDTH), dt_p))
    xp, xs = x_prompt, x_sample
    p_new, s_new = [], []
    for l in range(DEPTH):
        lw = dict(w_ada_mix=w_ada_mix[l], b_ada_mix=b_ada_mix[l], w_in=w_in[l], conv_w=conv_w[l],
                  conv_b=conv_b[l], ssd_A_log=ssd_A_log[l], ssd_dt_bias=ssd_dt_bias[l], ssd_D=ssd_D[l],
                  ssd_norm_w=ssd_norm_w[l], mlstm_gate_b=mlstm_gate_b[l], mlstm_norm_w=mlstm_norm_w[l],
                  pool_w=pool_w[l], pool_scale=pool_scale[l], gate_b=gate_b[l], w_br_ssd=w_br_ssd[l],
                  w_br_mlstm=w_br_mlstm[l], w_br_pool=w_br_pool[l], w_out=w_out[l], ln1_g=ln1_g[l],
                  ln1_b=ln1_b[l], w_ada_ffn=w_ada_ffn[l], b_ada_ffn=b_ada_ffn[l], w_rt_group=w_rt_group[l],
                  b_rt_group=b_rt_group[l], w_rt_expert=w_rt_expert[l], b_rt_expert=b_rt_expert[l],
                  w_e_gate=w_e_gate[l], w_e_up=w_e_up[l], w_e_down=w_e_down[l], ln2_g=ln2_g[l],
                  ln2_b=ln2_b[l])
        xp, sp = decoder_layer(xp, c_prompt, prompt_init, 0, lw)
        sample_states = (state_ssd[l], state_conv[l], state_mlstm_C[l], state_mlstm_n[l],
                         state_mlstm_m[l], state_pool[l])
        xs, ss = decoder_layer(xs, c_sample, sample_states, POOL_BUF, lw)
        p_new.append(sp)
        s_new.append(ss)
    ssd_p, conv_p, mC_p, mn_p, mm_p, pool_p = [jnp.stack(a) for a in zip(*p_new)]
    ssd_s, conv_s, mC_s, mn_s, mm_s, pool_s = [jnp.stack(a) for a in zip(*s_new)]
    return (xp, xs, ssd_p, conv_p, mC_p, mn_p, mm_p, pool_p, ssd_s, conv_s, mC_s, mn_s, mm_s, pool_s)


_drawn_inputs = setup_inputs


def setup_inputs(seed=0):
    import zlib

    import numpy as np

    out = dict(_drawn_inputs(seed))
    spreads = {}
    factors = {'conv_b': 3.513,
     'mlstm_norm_w': 3.02,
     'gate_b': 22.145,
     'ln1_b': 4.57,
     'b_ada_ffn': 2.848,
     'b_rt_group': 12.632,
     'b_rt_expert': 26.372,
     'ln2_b': 5.515}
    for name, (base, spread) in spreads.items():
        noise = np.random.default_rng([zlib.crc32(name.encode()), seed]).standard_normal(out[name].shape)
        drawn = base * np.exp(spread * noise) if base else spread * noise
        out[name] = __import__('jax').numpy.asarray(drawn.astype(out[name].dtype))
    for name, factor in factors.items():
        out[name] = (out[name] * factor).astype(out[name].dtype)
    return out
```

```python
from contextlib import ExitStack

import concourse.bass as bass
from concourse import mybir

F32 = mybir.dt.float32
ALU = mybir.AluOpType
ACT = mybir.ActivationFunctionType
AX = mybir.AxisListType

P = 128
D = 1024
KT = D // P
TP, NSEQ, TS = 512, 8, 4
NT = TP + NSEQ * TS
HALF = NT // 2
RING = 4
CHUNKS = [(c * P, P) for c in range(TP // P)] + [(TP, NSEQ * TS)]
NSEG = TP // P + NSEQ
ALPHA = 2 ** 0.25
BIG = 3.0e38

PHASES = {}


def plan():
    b = g = a = 0
    for name, nb, ng, na in (("ada_mix", 12, 24, 0), ("xbcz", 10, 20, 20), ("merge0", 8, 16, 16),
                             ("qkvo", 16, 32, 32), ("merge1", 8, 16, 16), ("up", 4, 8, 8), ("poolw", 1, 8, 8),
                             ("merge2", 8, 16, 16), ("out", 4, 8, 8), ("ada_ffn", 12, 24, 0),
                             ("experts", 32, 64, 64), ("down", 16, 32, 8)):
        PHASES[name] = (b, g, a)
        b, g, a = b + nb, g + ng, a + na
    return b


NBLOCKS = plan()

CST = {}
_at = 0
for _n, _w in (("ident", P), ("one", P), ("mean", P), ("mask", P), ("mask16", P), ("smask", 32), ("smask16", 32),
               ("tokseq", NSEQ), ("seqcol", NSEQ * 32), ("rank", 4), ("invcnt", 64), ("eps", 2), ("sel", 16 * P)):
    CST[_n] = (_at, _w)
    _at += _w
NCST = _at

VEC = {}
_at = 0
for _n, _w in (("b_ada_mix", 24), ("b_ada_ffn", 24), ("gate_b", 24), ("conv_b", 12), ("conv_w", 48), ("ssd_norm_w", 8),
               ("mlstm_norm_w", 8), ("pool_scale", 8), ("ln1_g", 8), ("ln1_b", 8), ("ln2_g", 8), ("ln2_b", 8),
               ("ssd_D", 8), ("row_bias", 1), ("a_log", 1), ("b_rt", 20)):
    VEC[_n] = (_at, _w)
    _at += _w
NVEC = _at


def program(nc, wstream, xT, cT, cst, vec, wgate, segm, wrt, ssd0, conv0, caug0, m0, pool0, pool_raw,
            yT, ssd_p, conv_p, cm_p, mm_p, pool_p, ssd_s, conv_s, cm_s, mm_s, pool_s, pool_old):
    with ExitStack() as ctx:
        def sb(name, shape):
            return ctx.enter_context(nc.sbuf_tensor(name, shape, F32))

        def sem(name):
            return ctx.enter_context(nc.semaphore(name))

        C = sb("C", [P, NCST])
        V = sb("V", [P, NVEC])
        cTs = sb("cTs", [P, KT, 9])
        wr = sb("wr", [P, KT, 20])
        uT = sb("uT", [P, KT, NT])
        ring = sb("ring", [P, RING, 2048])
        proj = sb("proj", [P, 32, NT])
        merged = sb("merged", [P, KT, NT])
        G = sb("G", [P, 7, NT])
        tg = sb("tg", [P, 5, 80])
        exl = sb("exl", [P, 16, NSEG])
        wpb = sb("wpb", [P, 4, NSEG])
        adaM = sb("adaM", [P, 24, 9])
        adaF = sb("adaF", [P, 24, 9])
        gs = sb("gs", [P, 2, NT])
        mp = sb("mp", [P, NSEG])
        rt = sb("rt", [P, 5, 96])
        work = sb("work", [P, 8704])
        PS = ctx.enter_context(nc.psum_tensor("PS", [P, 8, 512], F32))

        def cc(name, rows=P):
            a, w = CST[name]
            return C[0:rows, a:a + w]

        def vv(name, i, n=1):
            a, _ = VEC[name]
            return V[:, a + i:a + i + n]

        ident, one, mean = cc("ident"), cc("one"), cc("mean")
        sel = cc("sel").rearrange("p (h m) -> p h m", h=16)
        seqcol = cc("seqcol").rearrange("p (j t) -> p j t", j=NSEQ)
        wg = gs[:, 0, :].rearrange("p (k m) -> p k m", k=KT)
        seg0 = gs[:, 1, :]

        def carve(sizes):
            out, at = [], 0
            for n in sizes:
                out.append(work[:, at:at + n])
                at += n
            return out

        xdt, xw, Es, cbm, Bt, ytok, sT, CTm = carve([1024, 1024, 2048, 256, 256, 1024, 1024, 512])
        s0g = [proj[:, 20:28, :].rearrange("p a t -> p (a t)")[:, 0:4096],
               merged[:].rearrange("p a t -> p (a t)")[:, 0:4096]]
        Btm = proj[:, 28:32, :].rearrange("p a t -> p (a t)")[:, 0:2048]
        cpad = proj[:, 20:28, :].rearrange("p a t -> p (a t)")
        vaug_, kw, Em, qs, CT_, kwm_, qm_, caug_ = carve([1028, 1024, 512, 1024, 2056, 512, 128, 2056])
        vaug = vaug_.rearrange("p (h v) -> p h v", h=4)
        CT = CT_.rearrange("p (h k v) -> p h k v", h=4, k=2)
        caug = caug_.rearrange("p (b j v) -> p b j v", b=2, j=4)
        hbuf = gs[:].rearrange("p a t -> p (a t)")[:, 0:1024]
        hstat = gs[:].rearrange("p a t -> p (a t)")[:, 1024:1088]

        pf = proj[:].rearrange("p a t -> p (a t)")
        at = 8 * NT
        padP, padS = [], []
        for _ in range(2):
            padP.append(pf[:, at:at + 8 * 527].rearrange("p (i t) -> p i t", i=8))
            at += 8 * 527
            padS.append(pf[:, at:at + 8 * 152].rearrange("p (i j t) -> p i j t", i=8, j=NSEQ))
            at += 8 * 152
        dpool = work[:, 0:4352].rearrange("p (i t) -> p i t", i=8)
        pool_hist_dst = padS[0][:, :, :, 0:15]

        def acc(p):
            return PS[:, 2 * p:2 * p + 2, 0:HALF]

        def banks(b, n):
            return PS[:, b:b + n, :].rearrange("p b f -> p (b f)")

        def halves(t):
            return t.rearrange("p (h t) -> p h t", h=2)

        w_loaded = [sem(f"w_loaded{i}") for i in range(RING)]
        group_done = sem("group_done")
        acc_free = [sem("acc_free0"), sem("acc_free1")]
        small_loaded, x_loaded, rows_in_loaded = sem("small_loaded"), sem("x_loaded"), sem("rows_in_loaded")
        dve_step, act_step = sem("dve_step"), sem("act_step")
        ada_ready, u_ready, gates_psum, xrow_ready, rabs_ready = (
            sem("ada_ready"), sem("u_ready"), sem("gates_psum"), sem("xrow_ready"), sem("rabs_ready"))
        rexp_ready, rw_ready, rln_ready, cumd_ready, rowexp_ready, rows_ready = (
            sem("rexp_ready"), sem("rw_ready"), sem("rln_ready"), sem("cumd_ready"), sem("rowexp_ready"),
            sem("rows_ready"))
        tok_psum, tok_ready, m_ready = sem("tok_psum"), sem("tok_ready"), sem("m_ready")
        evac_xz, conv_in_loaded, conv_pre, conv_silu, z_silu = (
            sem("evac_xz"), sem("conv_in_loaded"), sem("conv_pre"), sem("conv_silu"), sem("z_silu"))
        ssd_xb, ssd_bc, ssd_bt, ssd_x, ssd_seg, ssd_exp, ssd_w, ssd_yp, ssd_ytok, ssd_st, ssd_stdone, ssd_yTp, ssd_out = (
            sem(n) for n in ("ssd_xb", "ssd_bc", "ssd_bt", "ssd_x", "ssd_seg", "ssd_exp", "ssd_w", "ssd_yp", "ssd_ytok",
                             "ssd_st", "ssd_stdone", "ssd_yTp", "ssd_out"))
        ssd_masks, s0_loaded, ssd_upd, ssd_updone = sem("ssd_masks"), sem("s0_loaded"), sem("ssd_upd"), sem("ssd_updone")
        sq_ready, ssq_psum, sd_ready, br_ready, gate_ready, gate_used = (
            sem("sq_ready"), sem("ssq_psum"), sem("sd_ready"), sem("br_ready"), sem("gate_ready"), sem("gate_used"))
        evac_qk, og_ready = sem("evac_qk"), sem("og_ready")
        ml_kv, ml_sc, ml_kw, ml_va, ml_d, ml_exp, ml_w, ml_qs, ml_num, ml_h, ml_sd, ml_hn, ml_hT, ml_out = (
            sem(n) for n in ("ml_kv", "ml_sc", "ml_kw", "ml_va", "ml_d", "ml_exp", "ml_w", "ml_qs", "ml_num", "ml_h",
                             "ml_sd", "ml_hn", "ml_hT", "ml_out"))
        ml_st, ml_stdone, ml_qm, caug_loaded, ml_intra, ml_upd, ml_updone, caug_stored = (
            sem(n) for n in ("ml_st", "ml_stdone", "ml_qm", "caug_loaded0", "ml_intra", "ml_upd", "ml_updone",
                             "caug_stored0"))
        caug_l = [caug_loaded, sem("caug_loaded1")]
        caug_s = [caug_stored, sem("caug_stored1")]
        evac_up, pool_loaded, pool_d, evac_pool, evac_out, xr_loaded, r_ready = (
            sem(n) for n in ("evac_up", "pool_loaded", "pool_d", "evac_pool", "evac_out", "xr_loaded", "r_ready"))
        ln_mu, ln_cen, ln_sq, ln_var, ln_sd, ln_done = (
            sem(n) for n in ("ln_mu", "ln_cen", "ln_sq", "ln_var", "ln_sd", "ln_done"))
        u2_ready, rt_psum, rt_d, rt_e, rt_dd, rt_e2, wts_ready, wtsT_psum, wtsT_ready = (
            sem(n) for n in ("u2_ready", "rt_psum", "rt_d", "rt_e", "rt_dd", "rt_e2", "wts_ready", "wtsT_psum",
                             "wtsT_ready"))
        wm_ready, wbc_psum, silu_ready, h_used, evac_down, r2_ready = (
            sem(n) for n in ("wm_ready", "wbc_psum", "silu_ready", "h_used", "evac_down", "r2_ready"))
        stored, pool_stored = sem("stored"), sem("pool_stored")

        block = ctx.enter_context(nc.Block())

        def groups_before(b):
            pw = PHASES["poolw"][0]
            return 2 * (b + 1) + (6 if b >= pw else 0)

        @block.sync
        def _(sp):
            sp.dma_start(C[:], cst).then_inc(small_loaded, 16)
            sp.dma_start(V[:], vec).then_inc(small_loaded, 16)
            sp.dma_start(cTs[:], cT).then_inc(small_loaded, 16)
            for i in range(RING):
                sp.dma_start(ring[:, i, :], wstream[i]).then_inc(w_loaded[i], 16)

            def stream(first, last):
                base = groups_before(first - RING)
                with sp.Fori(0, (last - first) // RING) as it:
                    for i in range(RING):
                        sp.wait_ge(group_done, it * (2 * RING) + base + 2 * i)
                        sp.dma_start(ring[:, (first + i) % RING, :],
                                     wstream[bass.ds(it * RING + (first + i), 1)].rearrange("o p c -> (o p) c")
                                     ).then_inc(w_loaded[(first + i) % RING], 16)

            pw = PHASES["poolw"][0]
            turns = (pw - RING) // RING
            stream(RING, RING + turns * RING)
            b = RING + turns * RING
            while b < pw + RING:
                sp.wait_ge(group_done, groups_before(b - RING))
                sp.dma_start(ring[:, b % RING, :], wstream[b]).then_inc(w_loaded[b % RING], 16)
                b += 1
            turns = (NBLOCKS - b) // RING
            stream(b, b + turns * RING)
            b += turns * RING
            while b < NBLOCKS:
                sp.wait_ge(group_done, groups_before(b - RING))
                sp.dma_start(ring[:, b % RING, :], wstream[b]).then_inc(w_loaded[b % RING], 16)
                b += 1

        @block.gpsimd
        def _(pool):
            n_stored = [0]

            def store(dst, src):
                pool.dma_start(dst, src).then_inc(stored, 16)
                n_stored[0] += 16

            pool.dma_start(uT[:], xT).then_inc(x_loaded, 16)
            pool.dma_start(gs[:, 0, :], wgate).then_inc(rows_in_loaded, 16)
            pool.dma_start(seg0, segm).then_inc(rows_in_loaded, 16)
            pool.dma_start(wr[:], wrt).then_inc(rows_in_loaded, 16)
            pool.dma_start(mp[64:68, 4:NSEG], m0).then_inc(rows_in_loaded, 16)
            store(pool_old, pool_raw[:, TS * D:15 * D])
            pool.dma_start(cpad[:, 0:288].rearrange("p (i j k) -> p i j k", i=12, j=NSEQ), conv0).then_inc(conv_in_loaded, 16)
            pool.wait_ge(m_ready, 1)
            store(mm_p, G[64:68, 4, 511:512])
            store(mm_s, G[64:68, 4, 512:NT])
            pool.wait_ge(evac_xz, 20)
            store(conv_p, proj[:, 0:12, 509:512])
            store(conv_s, proj[:, 0:12, 512:NT])
            pool.wait_ge(conv_pre, 12)
            pool.dma_start(s0g[0], ssd0[0]).then_inc(s0_loaded, 16)
            pool.dma_start(s0g[1], ssd0[1]).then_inc(s0_loaded, 16)
            pool.wait_ge(ssd_stdone, 4)
            store(ssd_p, sT)
            pool.wait_ge(ssd_updone, NSEQ)
            store(ssd_s[0], s0g[0])
            store(ssd_s[1], s0g[1])
            ssd_stores = n_stored[0]
            pool.wait_ge(stored, ssd_stores)
            pool.sem_inc(ssd_stdone, 1)
            for i in range(16):
                if i >= 2:
                    pool.wait_ge(ml_updone, i - 1)
                    pool.dma_start(cm_s[i - 2], caug[:, i % 2]).then_inc(caug_s[i % 2], 16)
                    pool.wait_ge(caug_s[i % 2], 16 * (i // 2))
                else:
                    pool.wait_ge(ml_stdone, 1)
                pool.dma_start(caug[:, i % 2], caug0[i]).then_inc(caug_l[i % 2], 16)
            for i in (16, 17):
                pool.wait_ge(ml_updone, i - 1)
                pool.dma_start(cm_s[i - 2], caug[:, i % 2]).then_inc(caug_s[i % 2], 16)
            store(cm_p, CT_)
            for s in caug_s:
                pool.wait_ge(s, 16 * 8)
            pool.wait_ge(stored, n_stored[0])
            pool.sem_inc(ml_stdone, 1)
            pool.wait_ge(evac_up, 8)
            pool.dma_start(pool_hist_dst, pool0).then_inc(pool_loaded, 16)
            store(pool_p, proj[:, 0:8, 497:512])
            store(pool_s, proj[:, 0:8, 512:NT])
            pool.wait_ge(stored, n_stored[0])
            pool.sem_inc(pool_stored, 1)
            pool.wait_ge(evac_out, 8)
            pool.dma_start(proj[:, 8:16, :], xT).then_inc(xr_loaded, 16)
            pool.wait_ge(ln_done, 2)
            store(yT, merged[:])
            pool.wait_ge(stored, n_stored[0])

        @block.tensor
        def _(pe):
            mm = nc.tensor.matmul

            def wblk(slot, kt, mi):
                return ring[:, slot, kt * 256 + mi * P:kt * 256 + mi * P + P]

            def wait_block(b, it=None):
                v = 16 * (b // RING + 1)
                pe.wait_ge(w_loaded[b % RING], v if it is None else it * 16 + v)

            def dense_block(b, a, rhs, it=None):
                wait_block(b, it)
                for mi in range(2):
                    v = a // 2 + 1
                    pe.wait_ge(acc_free[mi], v if it is None else it * RING + v)
                    for kt in range(KT):
                        for h in range(2):
                            last = mm(acc(mi)[:, h, :], wblk(b % RING, kt, mi), rhs[:, kt, h * HALF:(h + 1) * HALF],
                                      start=kt == 0, stop=kt == KT - 1)
                    last.then_inc(group_done, 1)

            def dense(name, nb, rhs):
                b0, _, a0 = PHASES[name]
                if nb >= 2 * RING:
                    with pe.Fori(0, nb // RING) as it:
                        for i in range(RING):
                            dense_block(b0 + i, a0 + 2 * i, rhs, it)
                    rest = range(nb // RING * RING, nb)
                else:
                    rest = range(nb)
                for i in rest:
                    dense_block(b0 + i, a0 + 2 * i, rhs)

            def ada(name, bank):
                b0 = PHASES[name][0]
                for i in range(12):
                    wait_block(b0 + i)
                    for mi in range(2):
                        n = (2 * i + mi) * 9
                        for kt in range(KT):
                            last = mm(PS[:, bank, n:n + 9], wblk((b0 + i) % RING, kt, mi), cTs[:, kt, :],
                                      start=kt == 0, stop=kt == KT - 1)
                        last.then_inc(group_done, 1)

            pe.wait_ge(small_loaded, 48)
            ada("ada_mix", 7)

            pe.wait_ge(u_ready, 1)
            pe.wait_ge(rows_in_loaded, 64)
            for h in range(2):
                for kt in range(KT):
                    last = mm(PS[0:68, 4 + h, 0:HALF], wg[:, kt, :], uT[:, kt, h * HALF:(h + 1) * HALF],
                              start=kt == 0, stop=kt == KT - 1)
            last.then_inc(gates_psum, 1)

            dense("xbcz", 10, uT)

            pe.wait_ge(rows_ready, 1)
            for c, (t0, L) in enumerate(CHUNKS):
                for i, (g, r0, n) in enumerate(((6, 0, 16), (2, 0, 16), (3, 0, 16), (4, 0, 16),
                                                (1, 64, 4), (5, 64, 4), (0, 64, 4), (6, 64, 4))):
                    bank, col = (6, c * 64 + 16 * i) if i < 4 else (7, c * 16 + 4 * (i - 4))
                    nc.tensor.transpose(PS[0:L, bank, col:col + n], G[r0:r0 + n, g, t0:t0 + L],
                                        ident[r0:r0 + n, r0:r0 + n])
            mm(PS[:, 6, 320:512], one[0:16, :], G[0:16, 1, 0:192], start=True, stop=True)
            mm(PS[:, 7, 80:128], one[64:68, :], G[64:68, 2, 0:48], start=True, stop=True).then_inc(tok_psum, 1)

            pe.wait_ge(conv_silu, 12)
            for s in acc_free:
                pe.wait_ge(s, PHASES["merge0"][2] // 2 + 1)
            pe.wait_ge(tok_ready, 3)
            for c, (t0, L) in enumerate(CHUNKS):
                cols = slice(t0, t0 + L)
                if c:
                    pe.wait_ge(ssd_ytok, c)
                    pe.wait_ge(ssd_stdone, c)
                for i in range(8):
                    nc.tensor.transpose(banks(4, 2)[0:L, i * P:(i + 1) * P], proj[:, i, cols], ident)
                for g in range(2):
                    nc.tensor.transpose(PS[0:L, 6, g * P:(g + 1) * P], proj[:, 8 + g, cols], ident)
                for g in range(2):
                    last = mm(PS[0:L, 6, 256 + g * P:256 + g * P + L], proj[:, 8 + g, cols], proj[:, 10 + g, cols],
                              start=True, stop=True)
                last.then_inc(ssd_xb, 1)
                if c:
                    pe.wait_ge(ssd_out, c)
                for h in range(16):
                    last = mm(banks(0, 4)[0:L, h * P:h * P + L], sel[0:16, h, 0:L], G[0:16, 2, cols], start=True, stop=True)
                last.then_inc(ssd_bc, 1)
                pe.wait_ge(ssd_w, c + 1)
                for h in range(16):
                    last = mm(banks(4, 2)[0:L, h * 64:(h + 1) * 64], Es[0:L, h * P:h * P + L], xdt[0:L, h * 64:(h + 1) * 64],
                              start=True, stop=True)
                if c == 0:
                    last.then_inc(ssd_yp, 1)
                elif L == P:
                    for g in range(2):
                        last = mm(PS[0:L, 2 + g, :], proj[:, 10 + g, cols], sT[:, g * 512:(g + 1) * 512],
                                  start=True, stop=True)
                    last.then_inc(ssd_yp, 1)
                else:
                    pe.wait_ge(ssd_masks, 1)
                    pe.wait_ge(s0_loaded, 32)
                    for g in range(2):
                        for j in range(NSEQ):
                            last = mm(PS[0:L, 2 + g, :], CTm[:, (g * NSEQ + j) * 32:(g * NSEQ + j) * 32 + 32],
                                      s0g[g][:, j * 512:(j + 1) * 512], start=j == 0, stop=j == NSEQ - 1)
                    last.then_inc(ssd_yp, 1)
                if L == P:
                    pe.wait_ge(ssd_bt, c + 1)
                    for g in range(2):
                        last = mm(PS[:, 6 + g, :], Bt[0:L, g * P:(g + 1) * P], xw[0:L, g * 512:(g + 1) * 512],
                                  start=True, stop=True)
                    last.then_inc(ssd_st, 1)
                pe.wait_ge(ssd_ytok, c + 1)
                for i in range(8):
                    last = nc.tensor.transpose(banks(0, 2)[:, i * P:i * P + L], ytok[0:L, i * P:(i + 1) * P],
                                               ident[0:L, 0:L])
                last.then_inc(ssd_yTp, 1)
            for j in range(NSEQ):
                b = 4 + 2 * (j % 2)
                if j >= 2:
                    pe.wait_ge(ssd_updone, j - 1)
                for g in range(2):
                    last = mm(PS[:, b + g, :], Btm[0:32, j * 256 + g * P:j * 256 + (g + 1) * P],
                              xw[0:32, g * 512:(g + 1) * 512], start=True, stop=True)
                last.then_inc(ssd_upd, 1)

            def sum_tiles(bank, weights, src, done):
                for h in range(2):
                    for kt in range(KT):
                        last = mm(PS[:, bank + h, 0:HALF], weights, src[:, kt, h * HALF:(h + 1) * HALF],
                                  start=kt == 0, stop=kt == KT - 1)
                last.then_inc(done, 1)

            pe.wait_ge(sq_ready, 1)
            pe.wait_ge(ssd_updone, NSEQ)
            sum_tiles(4, mean, proj[:, 0:8, :], ssq_psum)

            def merge(name, y):
                b0, _, a0 = PHASES[name]
                with pe.Fori(0, 2) as it:
                    for i in range(RING):
                        dense_block(b0 + i, a0 + 2 * i, uT if i % 2 == 0 else y, it)

            pe.wait_ge(br_ready, 1)
            pe.wait_ge(ssd_out, 5)
            merge("merge0", proj[:, 12:20, :])
            dense("qkvo", 16, uT)

            for s in acc_free:
                pe.wait_ge(s, PHASES["merge1"][2] // 2 + 1)
            pe.wait_ge(evac_qk, 32)
            for c, (t0, L) in enumerate(CHUNKS):
                cols = slice(t0, t0 + L)
                if c:
                    pe.wait_ge(ml_h, c)
                for i in range(8):
                    nc.tensor.transpose(banks(0, 2)[0:L, i * P:(i + 1) * P], proj[:, 8 + i, cols], ident)
                for i in range(8):
                    last = nc.tensor.transpose(banks(2, 2)[0:L, i * P:(i + 1) * P], proj[:, 16 + i, cols], ident)
                last.then_inc(ml_kv, 1)
                if c:
                    pe.wait_ge(ml_out, c)
                    pe.wait_ge(ml_stdone, c)
                for h in range(4):
                    for k in range(2):
                        mm(PS[0:L, 4, h * P:h * P + L], proj[:, 8 + 2 * h + k, cols], proj[:, 2 * h + k, cols],
                           start=k == 0, stop=k == 1)
                for h in range(4):
                    mm(PS[0:L, 5, h * P:h * P + L], sel[64:68, h, 0:L], G[64:68, 3, cols], start=True, stop=True)
                for h in range(4):
                    last = mm(PS[:, 6, h * P:h * P + L], sel[64:68, h, :], G[64:68, 5, cols], start=True, stop=True)
                last.then_inc(ml_sc, 1)
                pe.wait_ge(ml_w, c + 1)
                pe.wait_ge(ml_va, c + 1)
                pe.wait_ge(ml_qs, c + 1)
                for h in range(4):
                    last = mm(PS[0:L, h, 0:257], Em[0:L, h * P:h * P + L], vaug[0:L, h, :], start=True, stop=c == 0)
                    if c and L == P:
                        for k in range(2):
                            last = mm(PS[0:L, h, 0:257], qs[:, (2 * h + k) * P:(2 * h + k) * P + L], CT[:, h, k, :],
                                      start=False, stop=k == 1)
                if L == P:
                    last.then_inc(ml_num, 1)
                    for i in range(8):
                        if i >= 2:
                            pe.wait_ge(ml_upd, 8 * c + i - 1)
                        h, k = i // 2, i % 2
                        mm(PS[:, 6 + i % 2, 0:257], kw[0:L, h * 256 + k * P:h * 256 + (k + 1) * P], vaug[0:L, h, :],
                           start=True, stop=True).then_inc(ml_st, 1)
                else:
                    n = 0
                    for i in range(16):
                        h, k = i // 4, i // 2 % 2
                        pe.wait_ge(caug_l[i % 2], 16 * (i // 2 + 1))
                        pe.wait_ge(ml_qm, i + 1)
                        for j in range(4):
                            last = mm(PS[0:L, h, 0:257], qm_[:, j * 32:(j + 1) * 32], caug[:, i % 2, j, :],
                                      start=False, stop=i % 4 == 3 and j == 3)
                        for j in range(4):
                            if n >= 4:
                                pe.wait_ge(ml_upd, 32 + n - 3)
                            last = mm(PS[:, 4 + n % 4, 0:257], kwm_[0:32, j * P:(j + 1) * P], vaug[0:32, h, :],
                                      start=True, stop=True)
                            last.then_inc(ml_st, 1)
                            n += 1
                    pe.wait_ge(ml_upd, 32 + n)
                    pe.sem_inc(ml_num, 1)
                pe.wait_ge(ml_hn, c + 1)
                for i in range(8):
                    last = nc.tensor.transpose(banks(4, 2)[:, i * P:i * P + L], hbuf[0:L, i * P:(i + 1) * P],
                                               ident[0:L, 0:L])
                last.then_inc(ml_hT, 1)

            pe.wait_ge(ml_out, 5)
            pe.wait_ge(ml_h, 5)
            merge("merge1", proj[:, 24:32, :])
            dense("up", 4, uT)

            b0, _, a0 = PHASES["poolw"]
            wait_block(b0)
            pe.wait_ge(pool_d, 1)
            for n in range(8):
                g, m = n // 2, n % 2
                pe.wait_ge(acc_free[n % 2], (a0 + n) // 2 + 1)
                for k in range(2):
                    for h in range(2):
                        last = mm(acc(n % 2)[:, h, :], ring[:, b0 % RING, (g * 2 + k) * 256 + m * P:(g * 2 + k) * 256 + m * P + P],
                                  dpool[:, 2 * g + k, h * HALF:(h + 1) * HALF], start=k == 0, stop=k == 1)
                last.then_inc(group_done, 1)
            pe.wait_ge(evac_pool, 8)
            merge("merge2", proj[:, 8:16, :])
            pe.wait_ge(gate_used, 2 + 24)
            dense("out", 4, merged)
            ada("ada_ffn", 7)

            def layer_norm_sums(n, src, sq):
                pe.wait_ge(r_ready, n + 1)
                sum_tiles(4, mean, src, ln_mu)
                pe.wait_ge(ln_sq, n + 1)
                sum_tiles(6, mean, sq, ln_var)

            pe.wait_ge(ada_ready, 2)
            layer_norm_sums(0, proj[:, 0:8, :], proj[:, 16:24, :])
            pe.wait_ge(u2_ready, 1)
            for c, (t0, L) in enumerate(CHUNKS):
                for kt in range(KT):
                    last = mm(PS[0:L, 4, c * 20:(c + 1) * 20], uT[:, kt, t0:t0 + L], wr[:, kt, :],
                              start=kt == 0, stop=kt == KT - 1)
            last.then_inc(rt_psum, 1)
            pe.wait_ge(wts_ready, 1)
            for c, (t0, L) in enumerate(CHUNKS):
                dst = PS[0:16, 5, t0:t0 + L] if c < 4 else PS[0:16, 6, 0:L]
                last = nc.tensor.transpose(dst, rt[0:L, c, 80:96], ident[0:L, 0:L])
            last.then_inc(wtsT_psum, 1)
            b0, _, a0 = PHASES["experts"]
            pe.wait_ge(wtsT_ready, 1)
            with pe.Fori(0, 8) as it:
                for e in range(2):
                    dense_block(b0 + 2 * e, a0 + 4 * e, uT, it)
                    pe.wait_ge(wm_ready, it * 2 + e + 1)
                    pe.wait_ge(h_used, it * 4 + (2 * e + 2))
                    for h in range(2):
                        last = mm(PS[:, 4 + 2 * e + h, 0:HALF], one[0:16, :], G[0:16, 1 + e, h * HALF:(h + 1) * HALF],
                                  start=True, stop=True)
                    last.then_inc(wbc_psum, 1)
                    dense_block(b0 + 2 * e + 1, a0 + 4 * e + 2, uT, it)
            b0, _, a0 = PHASES["down"]
            pe.wait_ge(h_used, 4 + 32)
            with pe.Fori(0, 4) as it:
                for kb in range(4):
                    wait_block(b0 + kb, it)
                    for mi in range(2):
                        if kb == 0:
                            pe.wait_ge(acc_free[mi], it + (a0 // 2 + 1))
                        for kt in range(KT):
                            for h in range(2):
                                last = mm(acc(mi)[:, h, :], wblk((b0 + kb) % RING, kt, mi),
                                          proj[:, kb * 8 + kt, h * HALF:(h + 1) * HALF],
                                          start=kb == 0 and kt == 0, stop=kb == 3 and kt == KT - 1,
                                          skip_group_check=True)
                        last.then_inc(group_done, 1)
            layer_norm_sums(1, merged, proj[:, 0:8, :])

        @block.scalar
        def _(act):
            made = {}

            def do(ins, s=act_step, n=1):
                ins.then_inc(s, 1)
                made[s] = made.get(s, 0) + 1
                act.wait_ge(s, made[s])

            for s in acc_free:
                act.sem_inc(s, 1)

            def evac(name, n, dst_tile, s, **kw_):
                _, g0, _ = PHASES[name]
                if n >= 16:
                    with act.Fori(0, n // 8) as it:
                        for i in range(8):
                            act.wait_ge(group_done, it * 8 + (g0 + i + 1))
                            nc.scalar.copy(proj[:, bass.ds(it * 8 + (dst_tile + i), 1), :].rearrange(
                                "p o (h t) -> p (o h) t", h=2), acc(i % 2)).then_inc(acc_free[i % 2], 1)
                    rest = range(n // 8 * 8, n)
                else:
                    rest = range(n)
                for i in rest:
                    act.wait_ge(group_done, g0 + i + 1)
                    nc.scalar.copy(halves(proj[:, dst_tile + i, :]), acc(i % 2)).then_inc(acc_free[i % 2], 1)
                a_end = PHASES[name][2] + n
                for x in acc_free:
                    act.wait_ge(x, a_end // 2 + 1)
                act.sem_inc(s, n)

            act.wait_ge(gates_psum, 1)
            act.wait_ge(small_loaded, 48)
            do(nc.scalar.activation(halves(G[0:68, 0, :]), PS[0:68, 4:6, 0:HALF], ACT.Identity,
                                    bias=vv("row_bias", 0)[0:68]), xrow_ready)
            do(nc.scalar.activation(exl[0:16, 0, 0:1], vv("a_log", 0)[0:16], ACT.Exp))
            act.wait_ge(rabs_ready, 1)
            do(nc.scalar.activation(G[0:68, 1, :], G[0:68, 1, :], ACT.Exp, scale=-1.0), rexp_ready)
            act.wait_ge(rw_ready, 1)
            do(nc.scalar.activation(G[0:68, 5, :], G[0:68, 2, :], ACT.Ln), rln_ready)
            act.wait_ge(cumd_ready, 1)
            do(nc.scalar.activation(G[0:16, 3, :], G[0:16, 2, :], ACT.Exp))
            do(nc.scalar.activation(G[0:16, 4, :], G[0:16, 4, :], ACT.Exp))
            do(nc.scalar.activation(G[64:68, 5, :], G[64:68, 5, :], ACT.Exp))
            do(nc.scalar.activation(G[64:68, 0, :], G[64:68, 4, :], ACT.Exp, scale=-1.0))
            do(nc.scalar.activation(G[64:68, 6, :], G[64:68, 6, :], ACT.Exp), rowexp_ready)

            evac("xbcz", 20, 0, evac_xz)
            act.wait_ge(tok_psum, 1)
            for bank, w, a0 in ((6, 64, 0), (7, 16, 64)):
                do(nc.scalar.copy(tg[:, 0:4, a0:a0 + w], PS[:, bank, 0:4 * w].rearrange("p (c n) -> p c n", c=4)))
                do(nc.scalar.copy(tg[0:32, 4, a0:a0 + w], PS[0:32, bank, 4 * w:5 * w]), tok_ready)
            do(nc.scalar.copy(exl[:], PS[:, 6, 320:512].rearrange("p (h s) -> p h s", h=16)))
            do(nc.scalar.copy(wpb[:], PS[:, 7, 80:128].rearrange("p (h s) -> p h s", h=4)), tok_ready)
            for i in range(12):
                act.wait_ge(conv_pre, i + 1)
                act.wait_ge(evac_xz, 20)
                do(nc.scalar.activation(proj[:, i, :], proj[:, i, :], ACT.Silu, bias=vv("conv_b", i)), conv_silu)
            do(nc.scalar.activation(proj[:, 12:20, :], proj[:, 12:20, :], ACT.Silu), z_silu)
            for c, (t0, L) in enumerate(CHUNKS):
                act.wait_ge(ssd_xb, c + 1)
                do(nc.scalar.copy(Bt[0:L, :], PS[0:L, 6, 0:256]), ssd_bt)
                act.wait_ge(ssd_seg, c + 1)
                e = Es[0:L, :].rearrange("p (h l) -> p h l", h=16)[:, :, 0:L]
                do(nc.scalar.activation(e, e, ACT.Exp), ssd_exp)
            act.wait_ge(ssd_out, 5)
            do(nc.scalar.activation(proj[:, 0:8, :], proj[:, 12:20, :], ACT.Square), sq_ready)
            act.wait_ge(ssq_psum, 1)
            do(nc.scalar.activation(halves(gs[:, 0, :]), PS[:, 4:6, 0:HALF], ACT.Sqrt, bias=cc("eps")[:, 1:2]), sd_ready)
            act.wait_ge(br_ready, 1)

            def gates(name, b):
                _, g0, _ = PHASES[name]
                a = VEC["gate_b"][0]
                with act.Fori(0, 2) as it:
                    for i in range(4):
                        g = 4 * (i // 2) + i % 2
                        act.wait_ge(group_done, it * 8 + (g0 + g + 1))
                        act.wait_ge(gate_used, it * 4 + (8 * b + i + 1))
                        nc.scalar.activation(halves(gs[:, i % 2, :]), acc(i % 2), ACT.Sigmoid,
                                             bias=V[:, bass.ds(it * 4 + (a + 8 * b + i), 1)]).then_inc(gate_ready, 1)

            act.sem_inc(gate_used, 2)
            gates("merge0", 0)
            evac("qkvo", 32, 0, evac_qk)
            do(nc.scalar.activation(proj[:, 24:32, :], proj[:, 24:32, :], ACT.Sigmoid), og_ready)
            for c, (t0, L) in enumerate(CHUNKS):
                act.wait_ge(ml_kv, c + 1)
                do(nc.scalar.copy(vaug[0:L, :, 0:256], banks(2, 2)[0:L, :].rearrange("p (h v) -> p h v", h=4)), ml_va)
                act.wait_ge(ml_d, c + 1)
                e = Em[0:L, :].rearrange("p (h l) -> p h l", h=4)[:, :, 0:L]
                do(nc.scalar.activation(e, e, ACT.Exp), ml_exp)
                act.wait_ge(ml_h, c + 1)
                do(nc.scalar.activation(hstat[0:L, 36:40], hstat[0:L, 36:40], ACT.Sqrt, bias=cc("eps")[0:L, 0:1]), ml_sd)
            act.wait_ge(ml_out, 5)
            gates("merge1", 1)
            evac("up", 8, 0, evac_up)
            _, g0, _ = PHASES["poolw"]
            for i in range(8):
                act.wait_ge(group_done, g0 + i + 1)
                nc.scalar.activation(halves(proj[:, 8 + i, :]), acc(i % 2), ACT.Copy,
                                     scale=vv("pool_scale", i)).then_inc(acc_free[i % 2], 1)
            for x in acc_free:
                act.wait_ge(x, PHASES["merge2"][2] // 2 + 1)
            act.sem_inc(evac_pool, 8)
            gates("merge2", 2)
            evac("out", 8, 0, evac_out)

            def layer_norm(n, cen, sq):
                act.wait_ge(ln_cen, n + 1)
                do(nc.scalar.activation(sq, cen, ACT.Square), ln_sq)
                act.wait_ge(ln_var, n + 1)
                do(nc.scalar.activation(halves(gs[:, 0, :]), PS[:, 6:8, 0:HALF], ACT.Sqrt, bias=cc("eps")[:, 0:1]), ln_sd)

            layer_norm(0, proj[:, 0:8, :], proj[:, 16:24, :])
            act.wait_ge(rt_d, 1)
            do(nc.scalar.activation(rt[:, :, 24:28], rt[:, :, 24:28], ACT.Exp), rt_e)
            act.wait_ge(rt_dd, 1)
            do(nc.scalar.activation(rt[:, :, 60:61], rt[:, :, 60:61], ACT.Exp), rt_e2)
            _, g0, _ = PHASES["experts"]
            act.wait_ge(wtsT_ready, 1)
            with act.Fori(0, 8) as it:
                for e in range(2):
                    for m in range(2):
                        act.wait_ge(group_done, it * 8 + (g0 + 4 * e + m + 1))
                        act.wait_ge(h_used, it * 4 + (2 * e + m + 3))
                        nc.scalar.activation(halves(gs[:, m, :]), acc(m), ACT.Silu).then_inc(silu_ready, 1)
            _, g0, _ = PHASES["down"]
            with act.Fori(0, 4) as it:
                for m in range(2):
                    act.wait_ge(group_done, it * 8 + (g0 + 6 + m + 1))
                    nc.scalar.copy(uT[:, bass.ds(it * 2 + m, 1), :].rearrange("p o (h t) -> p (o h) t", h=2),
                                   acc(m)).then_inc(acc_free[m], 1)
            for x in acc_free:
                act.wait_ge(x, PHASES["down"][2] // 2 + 1 + 4)
            act.sem_inc(evac_down, 1)
            layer_norm(1, merged[:], proj[:, 0:8, :])

        @block.vector
        def _(dve):
            v = nc.vector
            made = {}

            def do(ins, s=dve_step):
                ins.then_inc(s, 1)
                made[s] = made.get(s, 0) + 1
                dve.wait_ge(s, made[s])

            def bc(ap, shape):
                return ap.to_broadcast(shape)

            def smp(t):
                return t.rearrange("p a (j t) -> p a j t", j=NSEQ)

            def ada_finish(dst, name, bank):
                a, _ = VEC[name]
                do(v.tensor_tensor(dst[:], PS[:, bank, 0:216].rearrange("p (m s) -> p m s", m=24),
                                   bc(V[:, a:a + 24].unsqueeze(2), [P, 24, 9]), ALU.add))
                do(v.tensor_scalar(dst[:, 8:24, :], dst[:, 8:24, :], 1.0, None, ALU.add), ada_ready)

            def modulate(dst, src, ada_, done):
                for i in range(KT):
                    do(v.tensor_scalar(dst[:, i, 0:TP], src[:, i, 0:TP], ada_[:, 8 + i, 0:1], ada_[:, i, 0:1],
                                       ALU.mult, ALU.add))
                do(v.tensor_tensor(smp(dst[:, :, TP:NT]), smp(src[:, :, TP:NT]),
                                   bc(ada_[:, 8:16, 1:9].unsqueeze(3), [P, 8, NSEQ, TS]), ALU.mult))
                do(v.tensor_tensor(smp(dst[:, :, TP:NT]), smp(dst[:, :, TP:NT]),
                                   bc(ada_[:, 0:8, 1:9].unsqueeze(3), [P, 8, NSEQ, TS]), ALU.add), done)

            dve.wait_ge(small_loaded, 48)
            dve.wait_ge(group_done, 24)
            ada_finish(adaM, "b_ada_mix", 7)
            dve.wait_ge(x_loaded, 16)
            modulate(uT, uT, adaM, u_ready)

            r16, r4 = slice(0, 16), slice(64, 68)
            do(v.memset(mp[64:68, 0:1], 0.0))
            dve.wait_ge(rows_in_loaded, 64)
            dve.wait_ge(xrow_ready, 1)
            do(v.scalar_tensor_tensor(G[0:68, 1, :], G[0:68, 0, :], -1.0, G[0:68, 0, :], ALU.mult, ALU.max), rabs_ready)
            dve.wait_ge(rexp_ready, 1)
            do(v.tensor_scalar(G[0:68, 2, :], G[0:68, 1, :], 1.0, None, ALU.add), rw_ready)
            do(v.tensor_scalar(G[0:68, 3, :], G[0:68, 2, :], -1.0, None, ALU.add))
            do(v.tensor_scalar(G[0:68, 4, :], G[0:68, 3, :], 0.0, None, ALU.is_equal))
            do(v.tensor_tensor(G[0:68, 3, :], G[0:68, 3, :], G[0:68, 4, :], ALU.add))
            do(v.reciprocal(G[0:68, 3, :], G[0:68, 3, :]))
            dve.wait_ge(rln_ready, 1)
            do(v.tensor_tensor(G[0:68, 5, :], G[0:68, 5, :], G[0:68, 4, :], ALU.add))
            do(v.tensor_tensor(G[0:68, 5, :], G[0:68, 5, :], G[0:68, 1, :], ALU.mult))
            do(v.tensor_tensor(G[0:68, 5, :], G[0:68, 5, :], G[0:68, 3, :], ALU.mult))
            do(v.scalar_tensor_tensor(G[r16, 6, :], G[r16, 0, :], 0.0, G[r16, 5, :], ALU.max, ALU.add))
            do(v.scalar_tensor_tensor(G[r4, 6, :], G[r4, 0, :], 0.0, G[r4, 5, :], ALU.min, ALU.subtract))
            do(v.tensor_scalar(G[r16, 1, :], G[r16, 6, :], exl[0:16, 0, 0:1], -1.0, ALU.mult, ALU.mult))
            do(v.tensor_tensor_scan(G[r16, 2, :], seg0[r16, :], G[r16, 1, :], 0.0, ALU.mult, ALU.add))
            do(v.tensor_tensor_scan(G[r4, 2, :], seg0[r4, :], G[r4, 6, :], 0.0, ALU.mult, ALU.add))
            do(v.tensor_copy(G[r4, 1, :], G[32:36, 0, :]))
            do(v.tensor_tensor(G[r4, 1, :], G[r4, 1, :], G[r4, 2, :], ALU.subtract))
            for s in range(NSEG):
                a, b = (s * P, s * P + P) if s < 4 else (TP + (s - 4) * TS, TP + (s - 3) * TS)
                do(v.tensor_tensor_scan(G[r4, 3, a:b], G[r4, 1, a:b], G[r4, 1, a:b], mp[r4, s:s + 1], ALU.max, ALU.max))
                if s < 3:
                    do(v.tensor_tensor(mp[r4, s + 1:s + 2], G[r4, 3, b - 1:b], G[r4, 2, b - 1:b], ALU.add))
            do(v.tensor_tensor(G[r4, 4, :], G[r4, 3, :], G[r4, 2, :], ALU.add), m_ready)

            def segs(row, r):
                return (row[r, 0:TP].rearrange("p (s t) -> p s t", s=4),
                        row[r, TP:NT].rearrange("p (s t) -> p s t", s=NSEQ))

            for k, (n, s0, w) in enumerate(((4, 0, P), (NSEQ, 4, TS))):
                M_, a_ = segs(G[:, 3, :], r4)[k], segs(G[:, 1, :], r4)[k]
                cum_ = segs(G[:, 2, :], r16)[k]
                do(v.tensor_tensor(segs(G[:, 5, :], r4)[k], bc(mp[r4, s0:s0 + n].unsqueeze(2), [4, n, w]), M_,
                                   ALU.subtract))
                do(v.tensor_tensor(segs(G[:, 6, :], r4)[k], a_, bc(M_[:, :, w - 1:w], [4, n, w]), ALU.subtract))
                do(v.tensor_tensor(segs(G[:, 4, :], r16)[k], bc(cum_[:, :, w - 1:w], [16, n, w]), cum_, ALU.subtract))
            dve.sem_inc(cumd_ready, 1)
            dve.wait_ge(rowexp_ready, 1)
            do(v.tensor_scalar(G[r4, 6, :], G[r4, 6, :], 0.0625, None, ALU.mult))
            dg16 = G[r16, 1, 0:192].rearrange("p (h s) -> p h s", h=16)
            dg4 = G[r4, 2, 0:48].rearrange("p (h s) -> p h s", h=4)
            for k, (n, s0, w) in enumerate(((4, 0, P), (NSEQ, 4, TS))):
                ex = segs(G[:, 3, :], r16)[k][:, :, w - 1:w].rearrange("p s o -> p o s")
                do(v.tensor_tensor(dg16[:, :, s0:s0 + n], bc(ex, [16, 16, n]),
                                   bc(ident[r16, 0:16].unsqueeze(2), [16, 16, n]), ALU.mult))
                wp = segs(G[:, 5, :], r4)[k][:, :, w - 1:w].rearrange("p s o -> p o s")
                do(v.tensor_tensor(dg4[:, :, s0:s0 + n], bc(wp, [4, 4, n]),
                                   bc(ident[r4, 64:68].unsqueeze(2), [4, 4, n]), ALU.mult))
            dve.sem_inc(rows_ready, 1)

            dve.wait_ge(evac_xz, 20)
            dve.wait_ge(stored, 16 * 5)
            dve.wait_ge(conv_in_loaded, 16)
            hist = cpad[:, 0:288].rearrange("p (i j k) -> p i j k", i=12, j=NSEQ)
            sx = cpad[:, 512:512 + 12 * 56].rearrange("p (i j k) -> p i j k", i=12, j=NSEQ)
            cin = cpad[:, 1536:1536 + 2 * NT].rearrange("p (b t) -> p b t", b=2)
            do(v.tensor_copy(sx[:, :, :, 0:3], hist))
            do(v.tensor_copy(sx[:, :, :, 3:7], proj[:, 0:12, TP:NT].rearrange("p a (j t) -> p a j t", j=NSEQ)))
            for i in range(12):
                x_ = cin[:, i % 2, :]
                do(v.tensor_copy(x_, proj[:, i, :]))

                def tap(k):
                    return vv("conv_w", k * 12 + i)
                o = proj[:, i, 0:TP]
                os_ = proj[:, i, TP:NT].rearrange("p (j t) -> p j t", j=NSEQ)
                do(v.tensor_scalar(o, x_[:, 0:TP], tap(3), None, ALU.mult))
                do(v.tensor_scalar(os_, sx[:, i, :, 3:7], tap(3), None, ALU.mult))
                for k in (2, 1, 0):
                    d = 3 - k
                    do(v.scalar_tensor_tensor(o[:, d:], x_[:, 0:TP - d], tap(k), o[:, d:], ALU.mult, ALU.add))
                    do(v.scalar_tensor_tensor(os_, sx[:, i, :, k:k + 4], tap(k), os_, ALU.mult, ALU.add),
                       dve_step if k else conv_pre)

            dve.wait_ge(tok_ready, 3)
            for c, (t0, L) in enumerate(CHUNKS):
                cols = slice(t0, t0 + L)
                x16 = lambda t: t[0:L, :].rearrange("p (h d) -> p h d", h=16)
                tgc = lambda a, n=16, w=64: bc(tg[0:L, c, a:a + n].unsqueeze(2), [L, n, w])
                mk = cc("mask")[0:L, 0:L] if L == P else cc("smask")[0:L, :]
                dve.wait_ge(ssd_xb, c + 1)
                do(v.tensor_tensor(x16(xdt), banks(4, 2)[0:L, :].rearrange("p (h d) -> p h d", h=16), tgc(0), ALU.mult))
                if c and L == P:
                    dve.wait_ge(ssd_st, c)
                do(v.tensor_tensor(x16(xw), x16(xdt), tgc(48), ALU.mult))
                dve.wait_ge(ssd_bt, c + 1)
                do(v.tensor_tensor(cbm[0:L, :].rearrange("p (g l) -> p g l", g=2)[:, :, 0:L],
                                   PS[0:L, 6, 256:512].rearrange("p (g l) -> p g l", g=2)[:, :, 0:L],
                                   bc(mk.unsqueeze(1), [L, 2, L]), ALU.mult))
                dve.wait_ge(ssd_bc, c + 1)
                do(v.tensor_tensor(Es[0:L, :].rearrange("p (h l) -> p h l", h=16)[:, :, 0:L],
                                   banks(0, 4)[0:L, :].rearrange("p (h l) -> p h l", h=16)[:, :, 0:L],
                                   tgc(16, 16, L), ALU.subtract))
                e = Es[0:L, :].rearrange("p (h l) -> p h l", h=16)[:, :, 0:L]
                do(v.tensor_scalar(e, e, 0.0, None, ALU.min), ssd_seg)
                if L < P:
                    dve.wait_ge(z_silu, 1)
                    for g in range(2):
                        do(v.tensor_tensor(CTm[:, g * 256:(g + 1) * 256].rearrange("p (j t) -> p j t", j=NSEQ),
                                           bc(proj[:, 10 + g, cols].unsqueeze(1), [P, NSEQ, 32]), seqcol, ALU.mult))
                    dve.wait_ge(ssd_bt, 5)
                    do(v.tensor_tensor(Btm[0:32, :].rearrange("p (j n) -> p j n", j=NSEQ),
                                       bc(Bt[0:32, :].unsqueeze(1), [32, NSEQ, 256]),
                                       bc(cc("tokseq")[0:32, :].unsqueeze(2), [32, NSEQ, 256]), ALU.mult), ssd_masks)
                dve.wait_ge(ssd_exp, c + 1)
                e = Es[0:L, :].rearrange("p (g h l) -> p g h l", g=2, h=8)[:, :, :, 0:L]
                cb = cbm[0:L, :].rearrange("p (g l) -> p g l", g=2)[:, :, 0:L]
                do(v.tensor_tensor(e, e, bc(cb.unsqueeze(2), [L, 2, 8, L]), ALU.mult), ssd_w)
                dve.wait_ge(ssd_yp, c + 1)
                if c == 0:
                    do(v.tensor_copy(ytok[0:L, :], banks(4, 2)[0:L, :]), ssd_ytok)
                else:
                    do(v.tensor_tensor(x16(ytok), banks(2, 2)[0:L, :].rearrange("p (h d) -> p h d", h=16), tgc(32), ALU.mult))
                    do(v.tensor_tensor(ytok[0:L, :], ytok[0:L, :], banks(4, 2)[0:L, :], ALU.add), ssd_ytok)
                if L == P:
                    dve.wait_ge(ssd_st, c + 1)
                    if c == 0:
                        do(v.tensor_copy(sT, banks(6, 2)), ssd_stdone)
                    else:
                        s16 = sT.rearrange("p (h d) -> p h d", h=16)
                        do(v.tensor_tensor(s16, s16, bc(exl[:, :, c:c + 1], [P, 16, 64]), ALU.mult))
                        do(v.tensor_tensor(sT, sT, banks(6, 2), ALU.add), ssd_stdone)
                dve.wait_ge(ssd_yTp, c + 1)
                dve.wait_ge(z_silu, 1)
                for i in range(8):
                    do(v.scalar_tensor_tensor(ytok[:, i * P:i * P + L], proj[:, i, cols], vv("ssd_D", i),
                                              banks(0, 2)[:, i * P:i * P + L], ALU.mult, ALU.add))
                do(v.tensor_tensor(proj[:, 12:20, cols], proj[:, 12:20, cols],
                                   ytok.rearrange("p (i l) -> p i l", i=8)[:, :, 0:L], ALU.mult), ssd_out)
            for j in range(NSEQ):
                b = 4 + 2 * (j % 2)
                for g in range(2):
                    t = s0g[g][:, j * 512:(j + 1) * 512]
                    t8 = t.rearrange("p (h d) -> p h d", h=8)
                    do(v.tensor_tensor(t8, t8, bc(exl[:, g * 8:(g + 1) * 8, 4 + j:5 + j], [P, 8, 64]), ALU.mult))
                dve.wait_ge(ssd_upd, j + 1)
                do(v.tensor_tensor(s0g[0][:, j * 512:(j + 1) * 512], s0g[0][:, j * 512:(j + 1) * 512], PS[:, b, :], ALU.add))
                do(v.tensor_tensor(s0g[1][:, j * 512:(j + 1) * 512], s0g[1][:, j * 512:(j + 1) * 512], PS[:, b + 1, :],
                                   ALU.add), ssd_updone)
            dve.wait_ge(sd_ready, 1)
            do(v.reciprocal(gs[:, 1, :], gs[:, 0, :]))
            for i in range(8):
                do(v.scalar_tensor_tensor(proj[:, 12 + i, :], proj[:, 12 + i, :], vv("ssd_norm_w", i), gs[:, 1, :],
                                          ALU.mult, ALU.mult), dve_step if i < 7 else br_ready)
            dve.wait_ge(ssd_stdone, 5)

            def merge(name, b):
                _, g0, _ = PHASES[name]
                with dve.Fori(0, 2) as it:
                    for i in range(4):
                        g = 4 * (i // 2) + 2 + i % 2
                        m = merged[:, bass.ds(it * 4 + i, 1), :].rearrange("p o (h t) -> p (o h) t", h=2)
                        s = halves(gs[:, i % 2, :])
                        dve.wait_ge(gate_ready, it * 4 + (8 * b + i + 1))
                        dve.sem_inc(acc_free[i % 2], 1)
                        dve.wait_ge(group_done, it * 8 + (g0 + g + 1))
                        if b == 0:
                            v.tensor_tensor(m, s, acc(i % 2), ALU.mult).then_inc(gate_used, 1)
                        else:
                            v.tensor_tensor(s, s, acc(i % 2), ALU.mult).then_inc(r2_ready, 1)
                            dve.wait_ge(r2_ready, it * 4 + (8 * (b - 1) + i + 1))
                            v.tensor_tensor(m, m, s, ALU.add).then_inc(gate_used, 1)
                        dve.wait_ge(gate_used, it * 4 + (8 * b + i + 3))
                        dve.sem_inc(acc_free[i % 2], 1)

            merge("merge0", 0)

            do(v.memset(vaug[:, :, 256:257], 1.0))
            dve.wait_ge(og_ready, 1)
            for c, (t0, L) in enumerate(CHUNKS):
                cols = slice(t0, t0 + L)
                mk = cc("mask16")[0:L, 0:L] if L == P else cc("smask16")[0:L, :]
                e = Em[0:L, :].rearrange("p (h l) -> p h l", h=4)[:, :, 0:L]
                col4 = lambda b: PS[0:L, b, :].rearrange("p (h l) -> p h l", h=4)[:, :, 0:L]
                dve.wait_ge(ml_kv, c + 1)
                if c:
                    dve.wait_ge(ml_st, 8 * c)
                do(v.tensor_tensor(kw[0:L, :].rearrange("p (h d) -> p h d", h=4),
                                   banks(0, 2)[0:L, :].rearrange("p (h d) -> p h d", h=4),
                                   bc(tg[0:L, c, 76:80].unsqueeze(2), [L, 4, 256]), ALU.mult), ml_kw)
                dve.wait_ge(ml_sc, c + 1)
                do(v.tensor_tensor(e, bc(tg[0:L, c, 64:68].unsqueeze(2), [L, 4, L]), col4(5), ALU.subtract))
                do(v.tensor_scalar(e, e, 0.0, None, ALU.min), ml_d)
                if c:
                    q4 = qs.rearrange("p (h k l) -> p h k l", h=4, k=2)[:, :, :, 0:L]
                    w4 = PS[:, 6, :].rearrange("p (h l) -> p h l", h=4)[:, :, 0:L]
                    do(v.tensor_tensor(q4, proj[:, 0:8, cols].rearrange("p (h k) l -> p h k l", h=4),
                                       bc(w4.unsqueeze(2), [P, 4, 2, L]), ALU.mult), ml_qs)
                else:
                    dve.sem_inc(ml_qs, 1)
                dve.wait_ge(ml_exp, c + 1)
                do(v.tensor_tensor(e, e, bc(mk.unsqueeze(1), [L, 4, L]), ALU.mult))
                do(v.tensor_tensor(e, e, col4(4), ALU.mult), ml_w)
                if L == P:
                    for i in range(8):
                        h, k = i // 2, i % 2
                        dve.wait_ge(ml_st, 8 * c + i + 1)
                        if c:
                            if i == 0:
                                dve.wait_ge(ml_num, c + 1)
                            do(v.scalar_tensor_tensor(CT[:, h, k, :], CT[:, h, k, :], wpb[:, h, c:c + 1],
                                                      PS[:, 6 + i % 2, 0:257], ALU.mult, ALU.add), ml_upd)
                        else:
                            do(v.tensor_copy(CT[:, h, k, :], PS[:, 6 + i % 2, 0:257]), ml_upd)
                    dve.sem_inc(ml_stdone, 1)
                else:
                    for i in range(16):
                        h, k, jh = i // 4, i // 2 % 2, i % 2
                        if i:
                            dve.wait_ge(ml_st, 32 + 4 * i)
                        do(v.tensor_tensor(kwm_[0:32, :].rearrange("p (j d) -> p j d", j=4),
                                           bc(kw[0:32, h * 256 + k * P:h * 256 + (k + 1) * P].unsqueeze(1), [32, 4, P]),
                                           bc(cc("tokseq")[0:32, 4 * jh:4 * jh + 4].unsqueeze(2), [32, 4, P]), ALU.mult))
                        do(v.tensor_tensor(qm_.rearrange("p (j t) -> p j t", j=4),
                                           bc(qs[:, (2 * h + k) * P:(2 * h + k) * P + 32].unsqueeze(1), [P, 4, 32]),
                                           seqcol[:, 4 * jh:4 * jh + 4, :], ALU.mult), ml_qm)
                        for j in range(4):
                            n = 4 * i + j
                            dve.wait_ge(ml_st, 32 + n + 1)
                            t = caug[:, i % 2, j, :]
                            do(v.scalar_tensor_tensor(t, t, wpb[:, h, 4 + 4 * jh + j:5 + 4 * jh + j],
                                                      PS[:, 4 + n % 4, 0:257], ALU.mult, ALU.add), ml_upd)
                        dve.sem_inc(ml_updone, 1)
                dve.wait_ge(ml_num, c + 1)
                if c:
                    dve.wait_ge(ml_hT, c)
                den = hstat[0:L, 0:4]
                do(v.tensor_copy(den, PS[0:L, 0:4, 256]))
                do(v.scalar_tensor_tensor(den, den, -1.0, den, ALU.mult, ALU.max))
                do(v.tensor_tensor(den, den, tg[0:L, c, 72:76], ALU.max))
                do(v.reciprocal(den, den))
                h4 = hbuf[0:L, :].rearrange("p (h d) -> p h d", h=4)
                do(v.tensor_tensor(h4, PS[0:L, 0:4, 0:256], bc(den.unsqueeze(2), [L, 4, 256]), ALU.mult))
                for h in range(4):
                    do(v.bn_stats(hstat[0:L, 4 + 6 * h:10 + 6 * h], h4[:, h, :]))
                    do(v.bn_aggr(hstat[0:L, 28 + 2 * h:30 + 2 * h], hstat[0:L, 4 + 6 * h:10 + 6 * h]))
                mv = hstat[0:L, 28:36].rearrange("p (h k) -> p h k", h=4)
                do(v.tensor_copy(hstat[0:L, 36:40], mv[:, :, 1]), ml_h)
                dve.wait_ge(ml_sd, c + 1)
                do(v.reciprocal(hstat[0:L, 36:40], hstat[0:L, 36:40]))
                for h in range(4):
                    do(v.tensor_scalar(h4[:, h, :], h4[:, h, :], mv[:, h, 0:1], hstat[0:L, 36 + h:37 + h],
                                       ALU.subtract, ALU.mult), dve_step if h < 3 else ml_hn)
                dve.wait_ge(ml_hT, c + 1)
                for i in range(8):
                    do(v.scalar_tensor_tensor(proj[:, 24 + i, cols], banks(4, 2)[:, i * P:i * P + L],
                                              vv("mlstm_norm_w", i), proj[:, 24 + i, cols], ALU.mult, ALU.mult),
                       dve_step if i < 7 else ml_out)
            merge("merge1", 1)

            dve.wait_ge(ml_stdone, 5)
            dve.wait_ge(evac_up, 8)
            dve.wait_ge(pool_loaded, 16)
            dve.wait_ge(pool_stored, 1)
            do(v.memset(padP[0][:, :, 0:15], 0.0))
            do(v.tensor_copy(padP[0][:, :, 15:527], proj[:, 0:8, 0:TP]))
            do(v.tensor_copy(padS[0][:, :, :, 15:19], smp(proj[:, 0:8, TP:NT])))
            for k in range(4):
                d, lo = 1 << k, (2 << k) - 1
                src, dst = k % 2, (k + 1) % 2
                do(v.tensor_tensor(padP[dst][:, 2 * k:8, lo:527], padP[src][:, 2 * k:8, lo:527],
                                   padP[src][:, 2 * k:8, lo - d:527 - d], ALU.add))
                for i in range(2 * k, 8):
                    do(v.tensor_tensor(padS[dst][:, i, :, lo:19], padS[src][:, i, :, lo:19],
                                       padS[src][:, i, :, lo - d:19 - d], ALU.add))
            for g in range(4):
                w, b = 2 << g, (g + 1) % 2
                t2 = slice(2 * g, 2 * g + 2)
                do(v.scalar_tensor_tensor(dpool[:, t2, 0:TP], padP[b][:, t2, 15:527], 1.0 / w, proj[:, t2, 0:TP],
                                          ALU.mult, ALU.subtract))
                a, _ = CST["invcnt"]
                do(v.tensor_tensor(dpool[:, t2, 0:w - 1], padP[b][:, t2, 15:14 + w],
                                   bc(C[:, a + 16 * g:a + 16 * g + w - 1].unsqueeze(1), [P, 2, w - 1]), ALU.mult))
                do(v.tensor_tensor(dpool[:, t2, 0:w - 1], dpool[:, t2, 0:w - 1], proj[:, t2, 0:w - 1], ALU.subtract))
                for i in range(2 * g, 2 * g + 2):
                    do(v.scalar_tensor_tensor(dpool[:, i, TP:NT].rearrange("p (j t) -> p j t", j=NSEQ),
                                              padS[b][:, i, :, 15:19], 1.0 / w,
                                              proj[:, i, TP:NT].rearrange("p (j t) -> p j t", j=NSEQ),
                                              ALU.mult, ALU.subtract), dve_step if i < 7 else pool_d)
            merge("merge2", 2)

            def residual(dst, out_, x_, ada_, done):
                for i in range(KT):
                    do(v.tensor_scalar(out_[:, i, 0:TP], out_[:, i, 0:TP], ada_[:, 16 + i, 0:1], None, ALU.mult))
                do(v.tensor_tensor(smp(out_[:, :, TP:NT]), smp(out_[:, :, TP:NT]),
                                   bc(ada_[:, 16:24, 1:9].unsqueeze(3), [P, 8, NSEQ, TS]), ALU.mult))
                do(v.scalar_tensor_tensor(dst, x_, ALPHA, out_, ALU.mult, ALU.add), done)

            def layer_norm(n, r, dst, gname, bname):
                dve.wait_ge(ln_mu, n + 1)
                r4_ = r.rearrange("p k (h t) -> p k h t", h=2)
                do(v.tensor_tensor(r4_, r4_, bc(PS[:, 4:6, 0:HALF].unsqueeze(1), [P, KT, 2, HALF]), ALU.subtract), ln_cen)
                dve.wait_ge(ln_sd, n + 1)
                do(v.reciprocal(gs[:, 1, :], gs[:, 0, :]))
                dve.wait_ge(ln_sq, n + 1)
                do(v.tensor_tensor(r, r, bc(gs[:, 1:2, :], [P, KT, NT]), ALU.mult))
                for i in range(KT):
                    do(v.tensor_scalar(dst[:, i, :], r[:, i, :], vv(gname, i), vv(bname, i), ALU.mult, ALU.add),
                       dve_step if i < 7 else ln_done)

            dve.wait_ge(group_done, PHASES["experts"][1])
            ada_finish(adaF, "b_ada_ffn", 7)
            dve.wait_ge(evac_out, 8)
            dve.wait_ge(xr_loaded, 16)
            residual(proj[:, 0:8, :], proj[:, 0:8, :], proj[:, 8:16, :], adaM, r_ready)
            layer_norm(0, proj[:, 0:8, :], merged, "ln1_g", "ln1_b")
            modulate(uT, merged, adaF, u2_ready)

            R = lambda a, b: rt[:, :, a:b]
            rank = bc(cc("rank").unsqueeze(1), [P, 5, 4])
            do(v.memset(rt[:], 0.0))
            dve.wait_ge(rt_psum, 1)
            do(v.tensor_tensor(rt[:, 0:4, 0:20], PS[:, 4, 0:80].rearrange("p (c n) -> p c n", c=4),
                               bc(vv("b_rt", 0, 20).unsqueeze(1), [P, 4, 20]), ALU.add))
            do(v.tensor_tensor(rt[0:32, 4, 0:20], PS[0:32, 4, 80:100], vv("b_rt", 0, 20)[0:32, :], ALU.add))

            def one_hot(src, mx, tmp, mn, dst):
                do(v.tensor_reduce(mx, src, AX.X, ALU.max))
                do(v.tensor_tensor(tmp, src, bc(mx, [P, 5, 4]), ALU.is_equal))
                do(v.tensor_tensor(tmp, tmp, rank, ALU.mult))
                do(v.tensor_reduce(mn, tmp, AX.X, ALU.min))
                do(v.tensor_tensor(dst, rank, bc(mn, [P, 5, 4]), ALU.is_equal))

            one_hot(R(0, 4), R(20, 21), R(24, 28), R(21, 22), R(28, 32))
            do(v.tensor_tensor(R(24, 28), R(0, 4), bc(R(20, 21), [P, 5, 4]), ALU.subtract), rt_d)
            dve.wait_ge(rt_e, 1)
            do(v.tensor_reduce(R(22, 23), R(24, 28), AX.X, ALU.add))
            do(v.reciprocal(R(22, 23), R(22, 23)))
            g4 = R(32, 48).rearrange("p c (g j) -> p c g j", g=4)
            do(v.tensor_tensor(g4, R(4, 20).rearrange("p c (g j) -> p c g j", g=4),
                               bc(R(28, 32).unsqueeze(3), [P, 5, 4, 4]), ALU.mult))
            do(v.tensor_reduce(R(48, 52), R(32, 48).rearrange("p c (g j) -> p c j g", g=4), AX.X, ALU.add))
            one_hot(R(48, 52), R(20, 21), R(24, 28), R(21, 22), R(52, 56))
            do(v.tensor_scalar(R(24, 28), R(52, 56), -BIG, None, ALU.mult))
            do(v.tensor_tensor(R(48, 52), R(48, 52), R(24, 28), ALU.add))
            one_hot(R(48, 52), R(23, 24), R(24, 28), R(21, 22), R(56, 60))
            do(v.tensor_tensor(R(60, 61), R(23, 24), R(20, 21), ALU.subtract), rt_dd)
            dve.wait_ge(rt_e2, 1)
            do(v.tensor_scalar(R(61, 62), R(60, 61), 1.0, None, ALU.add))
            do(v.reciprocal(R(61, 62), R(61, 62)))
            do(v.tensor_tensor(R(61, 62), R(61, 62), R(22, 23), ALU.mult))
            do(v.tensor_tensor(R(62, 63), R(61, 62), R(60, 61), ALU.mult))
            do(v.tensor_tensor(R(52, 56), R(52, 56), bc(R(61, 62), [P, 5, 4]), ALU.mult))
            do(v.tensor_tensor(R(56, 60), R(56, 60), bc(R(62, 63), [P, 5, 4]), ALU.mult))
            do(v.tensor_tensor(R(52, 56), R(52, 56), R(56, 60), ALU.add))
            w4 = R(80, 96).rearrange("p c (g j) -> p c g j", g=4)
            do(v.tensor_tensor(w4, bc(R(28, 32).unsqueeze(3), [P, 5, 4, 4]), bc(R(52, 56).unsqueeze(2), [P, 5, 4, 4]),
                               ALU.mult), wts_ready)
            dve.wait_ge(wtsT_psum, 1)
            do(v.tensor_copy(G[0:16, 0, 0:TP], PS[0:16, 5, :]))
            do(v.tensor_copy(G[0:16, 0, TP:NT], PS[0:16, 6, 0:32]), wtsT_ready)
            dve.sem_inc(h_used, 4)
            _, g0, _ = PHASES["experts"]
            with dve.Fori(0, 8) as it:
                for e in range(2):
                    v.tensor_scalar(G[0:16, 1 + e, :], G[0:16, 0, :], ident[0:16, bass.ds(it * 2 + e, 1)], None,
                                    ALU.mult).then_inc(wm_ready, 1)
                    for m in range(2):
                        dve.wait_ge(silu_ready, it * 4 + (2 * e + m + 1))
                        dve.sem_inc(acc_free[m], 1)
                    for m in range(2):
                        s = halves(gs[:, m, :])
                        dve.wait_ge(group_done, it * 8 + (g0 + 4 * e + 2 + m + 1))
                        v.tensor_tensor(s, s, acc(m), ALU.mult).then_inc(acc_free[m], 1)
                        dve.wait_ge(acc_free[m], it * 4 + (PHASES["experts"][2] // 2 + 2 * e + 3))
                        dve.wait_ge(wbc_psum, it * 2 + e + 1)
                        v.tensor_tensor(proj[:, bass.ds(it * 4 + (2 * e + m), 1), :].rearrange("p o (h t) -> p (o h) t", h=2),
                                        s, PS[:, 4 + 2 * e:6 + 2 * e, 0:HALF], ALU.mult).then_inc(h_used, 1)
            dve.wait_ge(evac_down, 1)
            dve.wait_ge(ln_done, 1)
            residual(merged[:], uT[:], merged[:], adaF, r_ready)
            layer_norm(1, merged[:], merged, "ln2_g", "ln2_b")


INS = ("wstream", "xT", "cT", "cst", "vec", "wgate", "segm", "wrt", "ssd0", "conv0", "caug0", "m0", "pool0", "pool_raw")
OUTS = (("yT", (P, KT, NT)), ("ssd_p", (P, 1024)), ("conv_p", (P, 12, 3)), ("cm_p", (P, 2056)), ("mm_p", (4, 1)),
        ("pool_p", (P, 8, 15)), ("ssd_s", (2, P, 4096)), ("conv_s", (P, 12, 32)), ("cm_s", (16, P, 4, 257)),
        ("mm_s", (4, 32)), ("pool_s", (P, 8, 32)),
        ("pool_old", (NSEQ, 11 * D)))


def constants(np):
    c = np.zeros((P, NCST), np.float32)

    def put(name, a):
        s, w = CST[name]
        a = np.asarray(a, np.float32)
        c[:a.shape[0], s:s + w] = a.reshape(a.shape[0], w)

    i = np.arange(P)
    put("ident", np.eye(P))
    put("one", np.ones((P, P)))
    put("mean", np.full((P, P), 1.0 / D))
    mask = (i[:, None] <= i[None, :]) * 1.0
    put("mask", mask)
    put("mask16", mask / 16)
    q = np.arange(32)
    sm = ((q[:, None] <= q[None, :]) & (q[:, None] // TS == q[None, :] // TS)) * 1.0
    put("smask", sm)
    put("smask16", sm / 16)
    own = (q[:, None] // TS == np.arange(NSEQ)[None, :]) * 1.0
    put("tokseq", own)
    put("seqcol", np.broadcast_to(own.T.reshape(1, -1), (P, NSEQ * 32)))
    put("rank", np.broadcast_to(np.arange(4) - 4.0, (P, 4)))
    inv = np.stack([1.0 / np.minimum(np.arange(16) + 1, 2 << g) for g in range(4)])
    put("invcnt", np.broadcast_to(inv.reshape(1, -1), (P, 64)))
    put("eps", np.broadcast_to(np.array([1e-5, 1e-6]), (P, 2)))
    s = np.zeros((P, 16, P))
    for h in range(16):
        s[h, h] = 1.0
    for h in range(4):
        s[64 + h, h] = 1.0
    put("sel", s)
    seg = np.ones((P, NT), np.float32)
    seg[:, [0, 128, 256, 384] + [TP + TS * j for j in range(NSEQ)]] = 0.0
    return c, seg


def lay_out(np, t):
    f = np.float32
    w = {k: np.asarray(v) for k, v in t.items()}
    w = {k: (v[0] if k not in ("x_prompt", "x_sample", "c_prompt", "c_sample") else v) for k, v in w.items()}

    def blocks(m):
        n = m.shape[1] // 256
        return np.ascontiguousarray(m.reshape(KT, P, n, 256).transpose(2, 1, 0, 3)).reshape(n, P, 2048)

    def paired(a, b):
        return np.stack([blocks(a), blocks(b)], axis=1).reshape(-1, P, 2048)

    win = w["w_in"]
    o = np.cumsum([0, 1024, 1536, 16, 1024, 1024, 1024, 4, 4, 1024, 1024, 3072])
    sec = lambda i: win[:, o[i]:o[i + 1]]
    gl = sec(10).reshape(D, 3, D)
    pw = w["pool_w"].reshape(4, 2, P, 256).transpose(2, 0, 1, 3).reshape(1, P, 2048)
    eg, eu = w["w_e_gate"], w["w_e_up"]
    ex = np.concatenate([np.concatenate([blocks(eg[e]), blocks(eu[e])]) for e in range(16)])
    dn = w["w_e_down"].reshape(4, D, D)
    dn = np.stack([blocks(dn[k]) for k in range(4)], axis=1).reshape(-1, P, 2048)
    stream = np.concatenate([
        blocks(w["w_ada_mix"]), blocks(sec(1)), blocks(sec(0)), paired(gl[:, 0], w["w_br_ssd"]),
        blocks(sec(3)), blocks(sec(4)), blocks(sec(5)), blocks(sec(8)), paired(gl[:, 1], w["w_br_mlstm"]),
        blocks(sec(9)), pw, paired(gl[:, 2], w["w_br_pool"]), blocks(w["w_out"]), blocks(w["w_ada_ffn"]), ex, dn])
    tile_rows = lambda m: np.ascontiguousarray(m.reshape(m.shape[0] // P, P, -1).transpose(1, 0, 2))
    x = np.concatenate([w["x_prompt"].reshape(TP, D), w["x_sample"].reshape(-1, D)])
    c = np.concatenate([w["c_prompt"], w["c_sample"]])
    wgate = np.zeros((D, 68), f)
    wgate[:, 0:16], wgate[:, 32:36], wgate[:, 64:68] = sec(2), sec(6), sec(7)
    vec = np.zeros((P, NVEC), f)

    def put(name, a, rows=P):
        s, n = VEC[name]
        vec[:rows, s:s + n] = a

    feat = lambda v: v.reshape(-1, P).T
    for n in ("b_ada_mix", "b_ada_ffn", "gate_b", "conv_b", "ssd_norm_w", "mlstm_norm_w", "pool_scale", "ln1_g", "ln1_b",
              "ln2_g", "ln2_b"):
        put(n, feat(w[n]))
    put("conv_w", feat(w["conv_w"].reshape(-1)))
    put("ssd_D", feat(np.broadcast_to(w["ssd_D"][:, None], (16, 64)).reshape(-1)))
    s, _ = VEC["row_bias"]
    vec[0:16, s], vec[32:36, s], vec[64:68, s] = w["ssd_dt_bias"], w["mlstm_gate_b"][:4], w["mlstm_gate_b"][4:]
    put("a_log", w["ssd_A_log"][:, None], 16)
    put("b_rt", np.broadcast_to(np.concatenate([w["b_rt_group"], w["b_rt_expert"]]), (P, 20)))
    cst, seg = constants(np)
    C0, n0 = w["state_mlstm_C"], w["state_mlstm_n"]
    ca = np.concatenate([C0.transpose(0, 1, 3, 2), n0[..., None]], axis=-1)
    ca = ca.reshape(2, 4, 4, 2, P, 257).transpose(2, 3, 0, 4, 1, 5).reshape(16, P, 4, 257)
    ssd0 = w["state_ssd"].reshape(NSEQ, 2, 8 * 64, P).transpose(1, 3, 0, 2).reshape(2, P, 4096)
    return {
        "wstream": stream, "xT": tile_rows(np.ascontiguousarray(x.T)), "cT": tile_rows(np.ascontiguousarray(c.T)),
        "cst": cst, "vec": vec, "wgate": tile_rows(wgate).reshape(P, -1), "segm": seg,
        "wrt": tile_rows(np.concatenate([w["w_rt_group"], w["w_rt_expert"]], axis=1)),
        "ssd0": ssd0, "conv0": w["state_conv"].reshape(NSEQ, 3, 12, P).transpose(3, 2, 0, 1), "caug0": ca,
        "m0": w["state_mlstm_m"].T, "pool0": w["state_pool"].reshape(NSEQ, 15, 8, P).transpose(3, 2, 0, 1),
        "pool_raw": w["state_pool"].reshape(NSEQ, 15 * D),
    }


def kernel(**inputs):
    import numpy as np
    import concourse.bacc as bacc
    from concourse.bass_utils import run_bass_kernel_spmd as run

    nc = bacc.Bacc("TRN2", target_bir_lowering=False, num_devices=1)
    laid = lay_out(np, inputs)
    arrays, args = {}, []
    for name in INS:
        a = np.ascontiguousarray(laid[name])
        arrays["in_" + name] = a
        args.append(nc.dram_tensor("in_" + name, a.shape, mybir.dt.from_np(a.dtype), kind="ExternalInput").ap())
    for name, shape in OUTS:
        args.append(nc.dram_tensor("out_" + name, shape, F32, kind="ExternalOutput").ap())
    program(nc, *args)
    r = run(nc, [arrays], core_ids=[0]).results[0]
    g = {name: np.asarray(r["out_" + name]) for name, _ in OUTS}

    y = g["yT"].transpose(2, 1, 0).reshape(NT, D)
    ssd_p = g["ssd_p"].T.reshape(1, 1, 16, 64, P)
    ssd_s = g["ssd_s"].reshape(2, P, NSEQ, 512).transpose(2, 0, 3, 1).reshape(1, NSEQ, 16, 64, P)
    conv_p = g["conv_p"].transpose(2, 1, 0).reshape(1, 1, 3, 1536)
    conv_s = g["conv_s"].transpose(2, 1, 0).reshape(1, NSEQ, TS, 1536)[:, :, 1:]
    cp = g["cm_p"].reshape(P, 4, 2, 257).transpose(1, 3, 2, 0).reshape(1, 1, 4, 257, 256)
    cs = g["cm_s"].reshape(4, 2, 2, P, 4, 257).transpose(2, 4, 0, 5, 1, 3).reshape(1, NSEQ, 4, 257, 256)
    pool_p = g["pool_p"].transpose(2, 1, 0).reshape(1, 1, 15, D)
    up_s = g["pool_s"].transpose(2, 1, 0).reshape(1, NSEQ, TS, D)
    pool_s = np.concatenate([g["pool_old"].reshape(1, NSEQ, 11, D), up_s], axis=2)
    out = (y[:TP].reshape(1, TP, D), y[TP:].reshape(NSEQ, TS, D),
           ssd_p, conv_p, cp[:, :, :, :256], cp[:, :, :, 256], g["mm_p"].reshape(1, 1, 4), pool_p,
           ssd_s, conv_s, cs[:, :, :, :256], cs[:, :, :, 256], g["mm_s"][:, TS - 1::TS].T.reshape(1, NSEQ, 4), pool_s)
    return tuple(np.ascontiguousarray(a) for a in out)
```

```python
from contextlib import ExitStack

import concourse.bass as bass
from concourse import mybir

F32 = mybir.dt.float32
U32 = mybir.dt.uint32
ALU = mybir.AluOpType
ACT = mybir.ActivationFunctionType
AX = mybir.AxisListType

P = 128
D = 1024
KT = D // P
TP, NSEQ, TS = 512, 8, 4
NT = TP + NSEQ * TS
HALF = NT // 2
RING = 4
CHUNKS = [(c * P, P) for c in range(TP // P)] + [(TP, NSEQ * TS)]
NSEG = TP // P + NSEQ
ALPHA = 2 ** 0.25
BIG = 3.0e38

PHASES = {}


def plan():
    b = g = a = 0
    for name, nb, ng, na in (("ada_mix", 12, 24, 0), ("z", 4, 8, 8), ("xbc", 6, 12, 12), ("merge0", 8, 16, 16),
                             ("qkvo", 16, 32, 32), ("merge1", 8, 16, 16), ("up", 4, 8, 8), ("ada_ffn", 12, 24, 0),
                             ("poolw", 1, 8, 8), ("merge2", 8, 16, 16), ("out", 4, 8, 8),
                             ("end", 0, 0, 0)):
        PHASES[name] = (b, g, a)
        b, g, a = b + nb, g + ng, a + na
    return b


NBLOCKS = plan()

NE = 16
XB = (2 * NT - 1) // P
NB = NE + XB
NBUF = 3

CST = {}
_at = 0
for _n, _w in (("ident", P), ("one", P), ("mean", P), ("mask", P), ("mask16", P), ("smask", 32), ("smask16", 32),
               ("tokseq", NSEQ), ("seqcol", NSEQ * 32), ("rank", 4), ("invcnt", 64), ("eps", 2), ("eid", NE), ("xb", XB), ("tok", 5),
               ("sel", 16 * P)):
    CST[_n] = (_at, _w)
    _at += _w
NCST = _at

VEC = {}
_at = 0
for _n, _w in (("b_ada_mix", 24), ("b_ada_ffn", 24), ("gate_b", 24), ("conv_b", 12), ("conv_w", 48), ("ssd_norm_w", 8),
               ("mlstm_norm_w", 8), ("pool_scale", 8), ("ln1_g", 8), ("ln1_b", 8), ("ln2_g", 8), ("ln2_b", 8),
               ("ssd_D", 8), ("row_bias", 1), ("a_log", 1), ("b_rt", 20)):
    VEC[_n] = (_at, _w)
    _at += _w
NVEC = _at


def program(nc, wstream, xT, cT, cst, vec, wgate, segm, wrt, wexp, ssd0, conv0, caug0, m0, pool0, pool_raw,
            yT, ssd_p, conv_p, cm_p, mm_p, pool_p, ssd_s, conv_s, cm_s, mm_s, pool_s, pool_old,
            slots, u2rows, yrows):
    with ExitStack() as ctx:
        def sb(name, shape):
            return ctx.enter_context(nc.sbuf_tensor(name, shape, F32))

        def sem(name):
            return ctx.enter_context(nc.semaphore(name))

        C = sb("C", [P, NCST])
        V = sb("V", [P, NVEC])
        cTs = sb("cTs", [P, KT, 9])
        wr = sb("wr", [P, KT, 20])
        uT = sb("uT", [P, KT, NT])
        ring = sb("ring", [P, RING, 2048])
        proj = sb("proj", [P, 32, NT])
        merged = sb("merged", [P, KT, NT])
        G = sb("G", [P, 7, NT])
        tg = sb("tg", [P, 5, 80])
        exl = sb("exl", [P, 16, NSEG])
        wpb = sb("wpb", [P, 4, NSEG])
        adaM = sb("adaM", [P, 24, 9])
        adaF = sb("adaF", [P, 24, 9])
        gs = sb("gs", [P, 2, NT])
        mp = sb("mp", [P, NSEG])
        rt = sb("rt", [P, 5, 160])
        route = sb("route", [P, 160])
        ridx = ctx.enter_context(nc.sbuf_tensor("ridx", [P, 64], U32))
        work = sb("work", [P, 8256])
        PS = ctx.enter_context(nc.psum_tensor("PS", [P, 8, 512], F32))

        def cc(name, rows=P):
            a, w = CST[name]
            return C[0:rows, a:a + w]

        def vv(name, i, n=1):
            a, _ = VEC[name]
            return V[:, a + i:a + i + n]

        ident, one, mean = cc("ident"), cc("one"), cc("mean")
        sel = cc("sel").rearrange("p (h m) -> p h m", h=16)
        seqcol = cc("seqcol").rearrange("p (j t) -> p j t", j=NSEQ)
        wg = gs[:, 0, :].rearrange("p (k m) -> p k m", k=KT)
        seg0 = gs[:, 1, :]

        def carve(sizes):
            out, at = [], 0
            for n in sizes:
                out.append(work[:, at:at + n])
                at += n
            return out

        xdt, xw, Es, cbm, Bt, ytok, sT, CTm = carve([1024, 1024, 2048, 256, 256, 1024, 1024, 512])
        s0g = [proj[:, 20:28, :].rearrange("p a t -> p (a t)")[:, 0:4096],
               merged[:].rearrange("p a t -> p (a t)")[:, 0:4096]]
        Btm = proj[:, 28:32, :].rearrange("p a t -> p (a t)")[:, 0:2048]
        cpad = proj[:, 20:28, :].rearrange("p a t -> p (a t)")
        hist = cpad[:, 0:288].rearrange("p (i j k) -> p i j k", i=12, j=NSEQ)
        sx = cpad[:, 512:512 + 12 * 56].rearrange("p (i j k) -> p i j k", i=12, j=NSEQ)
        cin = cpad[:, 1536:1536 + 2 * NT].rearrange("p (b t) -> p b t", b=2)
        tail = cpad[:, 2700:2700 + 12 * 35].rearrange("p (i t) -> p i t", i=12)
        no_rows = Btm[:, 0:D]
        vaug_, kw, Em, qs, CT_, kwm_, caug_ = carve([1028, 1024, 512, 1024, 2056, 512, 2056])
        qm_ = route[:, 0:128]
        vaug = vaug_.rearrange("p (h v) -> p h v", h=4)
        CT = CT_.rearrange("p (h k v) -> p h k v", h=4, k=2)
        caug = caug_.rearrange("p (b j v) -> p b j v", b=2, j=4)
        CB = [caug[:, 0], caug[:, 1]] + [proj[:, 8:24, :].rearrange("p a t -> p (a t)")[:, i * 1028:(i + 1) * 1028]
                                         .rearrange("p (j v) -> p j v", j=4) for i in range(8)]
        NCB = len(CB)
        hbuf = gs[:].rearrange("p a t -> p (a t)")[:, 0:1024]
        qmask = [qm_, rt[:, 0, 0:128]]
        kwmask = [kwm_, hbuf[:, 0:512]]
        hstat = gs[:].rearrange("p a t -> p (a t)")[:, 1024:1088]

        pf = proj[:].rearrange("p a t -> p (a t)")
        at = 8 * NT
        padP, padS = [], []
        for _ in range(2):
            padP.append(pf[:, at:at + 8 * 527].rearrange("p (i t) -> p i t", i=8))
            at += 8 * 527
            padS.append(pf[:, at:at + 8 * 152].rearrange("p (i j t) -> p i j t", i=8, j=NSEQ))
            at += 8 * 152
        dpool = work[:, 0:4352].rearrange("p (i t) -> p i t", i=8)
        pool_hist_dst = padS[0][:, :, :, 0:15]

        rg = ring[:].rearrange("p r f -> p (r f)")
        E3 = [rg[:, 0:6144], pf[:, 0:6144], pf[:, 6144:12288]]
        Y3 = [pf[:, 12288 + i * 1024:12288 + (i + 1) * 1024] for i in range(3)]
        X3 = [work[:, i * 1024:(i + 1) * 1024] for i in range(3)]
        XT3 = [work[:, (3 + i) * 1024:(4 + i) * 1024].rearrange("p (k s) -> p k s", k=KT) for i in range(3)]
        H3 = [work[:, 6144 + i * 256:6400 + i * 256] for i in range(3)]
        HT3 = [work[:, 6912 + i * 256:7168 + i * 256] for i in range(3)]
        arow = work[0:9, 4352:4352 + 3 * D]
        u2r = [work[:, i * 1024:(i + 1) * 1024] for i in range(5)]
        BK = [[pf[:, (2 * c + k) * 1024:(2 * c + k + 1) * 1024] for k in range(2)] for c in range(5)]
        zeros = ridx[:, 0:NB]
        n_further = ridx[0:1, 48 + XB:49 + XB]

        def acc(p):
            return PS[:, 2 * p:2 * p + 2, 0:HALF]

        def banks(b, n):
            return PS[:, b:b + n, :].rearrange("p b f -> p (b f)")

        def halves(t):
            return t.rearrange("p (h t) -> p h t", h=2)

        w_loaded = [sem(f"w_loaded{i}") for i in range(RING)]
        group_done = sem("group_done")
        acc_free = [sem("acc_free0"), sem("acc_free1")]
        small_loaded, x_loaded, rows_in_loaded = sem("small_loaded"), sem("x_loaded"), sem("rows_in_loaded")
        dve_step, act_step = sem("dve_step"), sem("act_step")
        ada_rows, ada_psum = sem("ada_rows"), sem("ada_psum")
        ada_ready, u_ready, gates_psum, xrow_ready, rabs_ready = (
            sem("ada_ready"), sem("u_ready"), sem("gates_psum"), sem("xrow_ready"), sem("rabs_ready"))
        rexp_ready, rw_ready, rln_ready, cumd_ready, rowexp_ready, rows_ready = (
            sem("rexp_ready"), sem("rw_ready"), sem("rln_ready"), sem("cumd_ready"), sem("rowexp_ready"),
            sem("rows_ready"))
        tok_psum, tok_ready, m_ready = sem("tok_psum"), sem("tok_ready"), sem("m_ready")
        conv_x, conv_tail, conv_in_loaded, conv_pre, conv_silu, z_silu = (
            sem(n) for n in ("conv_x", "conv_tail", "conv_in_loaded", "conv_pre", "conv_silu", "z_silu"))
        ssd_xb, ssd_bc, ssd_bt, ssd_x, ssd_seg, ssd_exp, ssd_w, ssd_yp, ssd_ytok, ssd_st, ssd_stdone, ssd_yTp, ssd_out = (
            sem(n) for n in ("ssd_xb", "ssd_bc", "ssd_bt", "ssd_x", "ssd_seg", "ssd_exp", "ssd_w", "ssd_yp", "ssd_ytok",
                             "ssd_st", "ssd_stdone", "ssd_yTp", "ssd_out"))
        ssd_masks, s0_loaded, ssd_upd, ssd_updone = sem("ssd_masks"), sem("s0_loaded"), sem("ssd_upd"), sem("ssd_updone")
        sq_ready, ssq_psum, sd_ready, br_ready, gate_ready, gate_used = (
            sem("sq_ready"), sem("ssq_psum"), sem("sd_ready"), sem("br_ready"), sem("gate_ready"), sem("gate_used"))
        evac_qk, og_ready = sem("evac_qk"), sem("og_ready")
        ml_kv, ml_sc, ml_kw, ml_va, ml_d, ml_exp, ml_w, ml_qs, ml_num, ml_h, ml_sd, ml_hn, ml_hT, ml_out = (
            sem(n) for n in ("ml_kv", "ml_sc", "ml_kw", "ml_va", "ml_d", "ml_exp", "ml_w", "ml_qs", "ml_num", "ml_h",
                             "ml_sd", "ml_hn", "ml_hT", "ml_out"))
        ml_st, ml_stdone, ml_qm, ml_upd, ml_updone = (
            sem(n) for n in ("ml_st", "ml_stdone", "ml_qm", "ml_upd", "ml_updone"))
        caug_l = [sem(f"caug_loaded{i}") for i in range(NCB)]
        caug_s = [sem(f"caug_stored{i}") for i in range(NCB)]
        evac_up, pool_loaded, pool_d, evac_pool, evac_out, xr_loaded, r_ready = (
            sem(n) for n in ("evac_up", "pool_loaded", "pool_d", "evac_pool", "evac_out", "xr_loaded", "r_ready"))
        ln_mu, ln_cen, ln_sq, ln_var, ln_sd, ln_done = (
            sem(n) for n in ("ln_mu", "ln_cen", "ln_sq", "ln_var", "ln_sd", "ln_done"))
        u2_ready, rt_psum, rt_d, rt_e, rt_dd, rt_e2, wts_ready, wtsT_psum, wtsT_ready = (
            sem(n) for n in ("u2_ready", "rt_psum", "rt_d", "rt_e", "rt_dd", "rt_e2", "wts_ready", "wtsT_psum",
                             "wtsT_ready"))
        ohs_ready, cnt_psum, cnt_used, pos_ready, list_zeroed, list_written, list_loaded, u2p, u2r_ready, u2_stored = (
            sem(n) for n in ("ohs_ready", "cnt_psum", "cnt_used", "pos_ready", "list_zeroed", "list_written", "list_loaded", "u2p",
                             "u2r_ready", "u2_stored"))
        e_loaded = [sem(f"e_loaded{i}") for i in range(NBUF)]
        x_got = [sem(f"x_got{i}") for i in range(NBUF)]
        y_stored = [sem(f"y_stored{i}") for i in range(NBUF)]
        xt_psum, xt_ready, gu_psum, sg_ready, h_ready, h_psum, hT_ready, y_psum, y_ready = (
            sem(n) for n in ("xt_psum", "xt_ready", "gu_psum", "sg_ready", "h_ready", "h_psum", "hT_ready", "y_psum",
                             "y_ready"))
        back_got, moe_ready, moeT_psum, moeT_ready, zero_ready, r2_ready = (
            sem(n) for n in ("back_got", "moe_ready", "moeT_psum", "moeT_ready", "zero_ready", "r2_ready"))
        rows_zeroed = sem("rows_zeroed")
        stored, pool_stored = sem("stored"), sem("pool_stored")

        block = ctx.enter_context(nc.Block())

        def groups_before(b):
            pw = PHASES["poolw"][0]
            return 2 * (b + 1) + (6 if b >= pw else 0)

        @block.sync
        def _(sp):
            sp.dma_start(C[:], cst).then_inc(small_loaded, 16)
            sp.dma_start(V[:], vec).then_inc(small_loaded, 16)
            sp.dma_start(cTs[:], cT).then_inc(small_loaded, 16)
            for i in range(RING):
                sp.dma_start(ring[:, i, :], wstream[i]).then_inc(w_loaded[i], 16)

            def stream(first, last):
                base = groups_before(first - RING)
                with sp.Fori(0, (last - first) // RING) as it:
                    for i in range(RING):
                        sp.wait_ge(group_done, it * (2 * RING) + base + 2 * i)
                        sp.dma_start(ring[:, (first + i) % RING, :],
                                     wstream[bass.ds(it * RING + (first + i), 1)].rearrange("o p c -> (o p) c")
                                     ).then_inc(w_loaded[(first + i) % RING], 16)

            pw = PHASES["poolw"][0]
            turns = (pw - RING) // RING
            stream(RING, RING + turns * RING)
            b = RING + turns * RING
            while b < pw + RING:
                sp.wait_ge(group_done, groups_before(b - RING))
                sp.dma_start(ring[:, b % RING, :], wstream[b]).then_inc(w_loaded[b % RING], 16)
                b += 1
            turns = (NBLOCKS - b) // RING
            stream(b, b + turns * RING)
            b += turns * RING
            while b < NBLOCKS:
                sp.wait_ge(group_done, groups_before(b - RING))
                sp.dma_start(ring[:, b % RING, :], wstream[b]).then_inc(w_loaded[b % RING], 16)
                b += 1

            sp.wait_ge(ln_done, 1)
            sp.wait_ge(group_done, PHASES["end"][1])

            def expert_block(b, it=None):
                i = b % NBUF
                if b < NE:
                    src = wexp[b] if it is None else wexp[bass.ds(it * NBUF + b, 1)].rearrange("o p c -> (o p) c")
                else:
                    e = sp.value_load(ridx[0:1, 48 + b - NE:49 + b - NE], min_val=0, max_val=NE - 1)
                    src = wexp[bass.ds(e, 1)].rearrange("o p c -> (o p) c")
                sp.dma_start(E3[i], src).then_inc(e_loaded[i], 16)

            def result_block(b, it=None):
                v = b + 1
                sp.wait_ge(y_ready, v if it is None else it * NBUF + v)
                dst = yrows.rearrange("(p b) d -> p b d", b=NB)
                dst = dst[:, b, :] if it is None else dst[:, bass.ds(it * NBUF + b, 1), :].rearrange("p o d -> p (o d)")
                sp.dma_start(dst, Y3[b % NBUF]).then_inc(y_stored[b % NBUF], 16)

            for b in range(NBUF):
                expert_block(b)
            turns = (NE - NBUF) // NBUF
            with sp.Fori(0, turns) as it:
                for b in range(NBUF, 2 * NBUF):
                    sp.wait_ge(y_psum, it * NBUF + (b - NBUF + 1))
                    expert_block(b, it)
                    result_block(b - NBUF, it)
            for b in range((turns + 1) * NBUF, NE):
                sp.wait_ge(y_psum, b - NBUF + 1)
                expert_block(b)
                result_block(b - NBUF)
            for b in range(NE - NBUF, NE):
                result_block(b)
            sp.wait_ge(pos_ready, 1)
            further = sp.value_load(n_further, min_val=0, max_val=XB)
            with sp.If(further > 0):
                for b in range(NE, NB):
                    if b >= NE + NBUF:
                        sp.wait_ge(y_psum, b - NBUF + 1)
                    expert_block(b)
                    if b >= NE + NBUF:
                        result_block(b - NBUF)
                for b in range(NB - NBUF, NB):
                    result_block(b)

        @block.gpsimd
        def _(pool):
            n_stored = [0]

            def store(dst, src):
                pool.dma_start(dst, src).then_inc(stored, 16)
                n_stored[0] += 16

            pool.dma_start(uT[:], xT).then_inc(x_loaded, 16)
            pool.wait_ge(zero_ready, 1)
            pool.dma_start(slots.rearrange("(p b) o -> p (b o)", b=NB), zeros).then_inc(list_zeroed, 16)
            pool.dma_start(gs[:, 0, :], wgate).then_inc(rows_in_loaded, 16)
            pool.dma_start(seg0, segm).then_inc(rows_in_loaded, 16)
            pool.dma_start(wr[:], wrt).then_inc(rows_in_loaded, 16)
            pool.dma_start(mp[64:68, 4:NSEG], m0).then_inc(rows_in_loaded, 16)
            store(pool_old, pool_raw[:, TS * D:15 * D])
            pool.dma_start(cpad[:, 0:288].rearrange("p (i j k) -> p i j k", i=12, j=NSEQ), conv0).then_inc(conv_in_loaded, 16)
            pool.wait_ge(u_ready, 1)
            pool.dma_start(yrows.rearrange("(p b) d -> p b d", b=NB)[:, NE:NB, :],
                           no_rows.unsqueeze(1).to_broadcast([P, XB, D])).then_inc(rows_zeroed, 16)
            pool.wait_ge(m_ready, 1)
            store(mm_p, G[64:68, 4, 511:512])
            store(mm_s, G[64:68, 4, 512:NT])
            pool.wait_ge(conv_tail, 12)
            store(conv_p, tail[:, :, 0:3])
            store(conv_s, tail[:, :, 3:35])
            pool.wait_ge(stored, n_stored[0])
            pool.wait_ge(conv_pre, 12)
            pool.dma_start(s0g[0], ssd0[0]).then_inc(s0_loaded, 16)
            pool.dma_start(s0g[1], ssd0[1]).then_inc(s0_loaded, 16)
            pool.wait_ge(ssd_stdone, 4)
            store(ssd_p, sT)
            pool.wait_ge(ssd_updone, NSEQ)
            store(ssd_s[0], s0g[0])
            store(ssd_s[1], s0g[1])
            ssd_stores = n_stored[0]
            pool.wait_ge(stored, ssd_stores)
            pool.sem_inc(ssd_stdone, 1)
            for i in range(NCB):
                if i == 0:
                    pool.wait_ge(ml_stdone, 1)
                if i == 2:
                    pool.wait_ge(ml_sc, 5)
                pool.dma_start(CB[i], caug0[i]).then_inc(caug_l[i], 16)
            store(cm_p, CT_)
            for i in range(16):
                pool.wait_ge(ml_updone, i + 1)
                pool.dma_start(cm_s[i], CB[i % NCB]).then_inc(caug_s[i % NCB], 16)
                if i >= 2 and i - 2 + NCB < 16:
                    pool.wait_ge(caug_s[i - 2], 16)
                    pool.dma_start(CB[i - 2], caug0[i - 2 + NCB]).then_inc(caug_l[i - 2], 16)
            for i in range(NCB):
                pool.wait_ge(caug_s[i], 16 * len(range(i, 16, NCB)))
            pool.wait_ge(stored, n_stored[0])
            pool.sem_inc(ml_stdone, 1)
            pool.dma_start(pool_hist_dst, pool0).then_inc(pool_loaded, 16)
            pool.wait_ge(evac_up, 8)
            store(pool_p, proj[:, 0:8, 497:512])
            store(pool_s, proj[:, 0:8, 512:NT])
            pool.wait_ge(stored, n_stored[0])
            pool.sem_inc(pool_stored, 1)
            pool.wait_ge(evac_out, 8)
            pool.dma_start(proj[:, 8:16, :], xT).then_inc(xr_loaded, 16)
            for c, (t0, L) in enumerate(CHUNKS):
                pool.wait_ge(u2r_ready, c + 1)
                pool.dma_start(u2rows[t0:t0 + L, :], u2r[c][0:L, :]).then_inc(u2_stored, 16)
            pool.wait_ge(pos_ready, 1)
            pool.wait_ge(list_zeroed, 16)
            for c, (t0, L) in enumerate(CHUNKS):
                for k in range(2):
                    pool.indirect_dma_start(slots, bass.IndirectOffsetOnAxis(ap=ridx[0:L, 24 + 5 * k + c:25 + 5 * k + c], axis=0),
                                            ridx[0:L, 40 + c:41 + c], None).then_inc(list_written, 16)
            pool.wait_ge(list_written, 16 * 10)
            pool.dma_start(ridx[:, 0:NB], slots.rearrange("(p b) o -> p (b o)", b=NB)).then_inc(list_loaded, 16)
            pool.wait_ge(list_loaded, 16)
            pool.wait_ge(u2_stored, 16 * 5)

            def rows_block(b):
                if b >= NBUF:
                    pool.wait_ge(xt_psum, b - NBUF + 1)
                pool.indirect_dma_start(X3[b % NBUF], None, u2rows, bass.IndirectOffsetOnAxis(ap=ridx[:, b:b + 1], axis=0)
                                        ).then_inc(x_got[b % NBUF], 16)

            for b in range(NE):
                rows_block(b)
            further = pool.value_load(n_further, min_val=0, max_val=XB)
            for i in range(NBUF):
                pool.wait_ge(y_stored[i], 16 * len(range(i, NE, NBUF)))
            with pool.If(further > 0):
                for b in range(NE, NB):
                    rows_block(b)
                for i in range(NBUF):
                    pool.wait_ge(y_stored[i], 16 * len(range(i, NB, NBUF)))
            for c, (t0, L) in enumerate(CHUNKS):
                for k in range(2):
                    pool.indirect_dma_start(BK[c][k][0:L, :], None, yrows,
                                            bass.IndirectOffsetOnAxis(ap=ridx[0:L, 24 + 5 * k + c:25 + 5 * k + c], axis=0)
                                            ).then_inc(back_got, 16)
            pool.wait_ge(ln_done, 2)
            store(yT, merged[:])
            pool.wait_ge(stored, n_stored[0])

        @block.tensor
        def _(pe):
            mm = nc.tensor.matmul

            def wblk(slot, kt, mi):
                return ring[:, slot, kt * 256 + mi * P:kt * 256 + mi * P + P]

            def wait_block(b, it=None):
                v = 16 * (b // RING + 1)
                pe.wait_ge(w_loaded[b % RING], v if it is None else it * 16 + v)

            def dense_block(b, a, rhs, it=None):
                wait_block(b, it)
                for mi in range(2):
                    v = a // 2 + 1
                    pe.wait_ge(acc_free[mi], v if it is None else it * RING + v)
                    for kt in range(KT):
                        for h in range(2):
                            last = mm(acc(mi)[:, h, :], wblk(b % RING, kt, mi), rhs[:, kt, h * HALF:(h + 1) * HALF],
                                      start=kt == 0, stop=kt == KT - 1)
                    last.then_inc(group_done, 1)

            def dense(name, nb, rhs):
                b0, _, a0 = PHASES[name]
                if nb >= 2 * RING:
                    with pe.Fori(0, nb // RING) as it:
                        for i in range(RING):
                            dense_block(b0 + i, a0 + 2 * i, rhs, it)
                    rest = range(nb // RING * RING, nb)
                else:
                    rest = range(nb)
                for i in rest:
                    dense_block(b0 + i, a0 + 2 * i, rhs)

            def ada(name, n):
                b0 = PHASES[name][0]

                def turn(i):
                    pe.wait_ge(ada_rows, 12 * n + i + 1)
                    for m in range(2 * i, 2 * i + 2):
                        last = nc.tensor.transpose(PS[:, 7, m * 9:m * 9 + 9], arow[:, m * P:(m + 1) * P], ident[0:9, 0:9])
                    last.then_inc(ada_psum, 1)

                for i in range(12):
                    wait_block(b0 + i)
                    if i >= 2:
                        pe.wait_ge(ada_rows, 12 * n + i - 1)
                    for kt in range(KT):
                        last = mm(PS[0:9, 4 + i % 2, 0:256], cTs[:, kt, :], ring[:, (b0 + i) % RING, kt * 256:(kt + 1) * 256],
                                  start=kt == 0, stop=kt == KT - 1)
                    last.then_inc(group_done, 2)
                    if i:
                        turn(i - 1)
                turn(11)

            pe.wait_ge(small_loaded, 48)
            ada("ada_mix", 0)

            pe.wait_ge(u_ready, 1)
            pe.wait_ge(rows_in_loaded, 64)
            for h in range(2):
                for kt in range(KT):
                    last = mm(PS[0:68, 4 + h, 0:HALF], wg[:, kt, :], uT[:, kt, h * HALF:(h + 1) * HALF],
                              start=kt == 0, stop=kt == KT - 1)
            last.then_inc(gates_psum, 1)

            dense("z", 4, uT)
            for i in range(4):
                dense_block(PHASES["xbc"][0] + i, PHASES["xbc"][2] + 2 * i, uT)

            pe.wait_ge(rows_ready, 1)
            for c, (t0, L) in enumerate(CHUNKS):
                for i, (g, r0, n) in enumerate(((6, 0, 16), (2, 0, 16), (3, 0, 16), (4, 0, 16),
                                                (1, 64, 4), (5, 64, 4), (0, 64, 4), (6, 64, 4))):
                    bank, col = (6, c * 64 + 16 * i) if i < 4 else (7, c * 16 + 4 * (i - 4))
                    nc.tensor.transpose(PS[0:L, bank, col:col + n], G[r0:r0 + n, g, t0:t0 + L],
                                        ident[r0:r0 + n, r0:r0 + n])
            mm(PS[:, 6, 320:512], one[0:16, :], G[0:16, 1, 0:192], start=True, stop=True)
            mm(PS[:, 7, 80:128], one[64:68, :], G[64:68, 2, 0:48], start=True, stop=True).then_inc(tok_psum, 1)

            for i in range(4, 6):
                dense_block(PHASES["xbc"][0] + i, PHASES["xbc"][2] + 2 * i, uT)
            pe.wait_ge(conv_silu, 12)
            for s in acc_free:
                pe.wait_ge(s, PHASES["merge0"][2] // 2 + 1)
            pe.wait_ge(tok_ready, 3)
            for c, (t0, L) in enumerate(CHUNKS):
                cols = slice(t0, t0 + L)
                if c:
                    pe.wait_ge(ssd_ytok, c)
                    pe.wait_ge(ssd_stdone, c)
                for i in range(8):
                    nc.tensor.transpose(banks(4, 2)[0:L, i * P:(i + 1) * P], proj[:, i, cols], ident)
                for g in range(2):
                    nc.tensor.transpose(PS[0:L, 6, g * P:(g + 1) * P], proj[:, 8 + g, cols], ident)
                for g in range(2):
                    last = mm(PS[0:L, 6, 256 + g * P:256 + g * P + L], proj[:, 8 + g, cols], proj[:, 10 + g, cols],
                              start=True, stop=True)
                last.then_inc(ssd_xb, 1)
                if c:
                    pe.wait_ge(ssd_out, c)
                for h in range(16):
                    last = mm(banks(0, 4)[0:L, h * P:h * P + L], sel[0:16, h, 0:L], G[0:16, 2, cols], start=True, stop=True)
                last.then_inc(ssd_bc, 1)
                pe.wait_ge(ssd_w, c + 1)
                for h in range(16):
                    last = mm(banks(4, 2)[0:L, h * 64:(h + 1) * 64], Es[0:L, h * P:h * P + L], xdt[0:L, h * 64:(h + 1) * 64],
                              start=True, stop=True)
                if c == 0:
                    last.then_inc(ssd_yp, 1)
                elif L == P:
                    for g in range(2):
                        last = mm(PS[0:L, 2 + g, :], proj[:, 10 + g, cols], sT[:, g * 512:(g + 1) * 512],
                                  start=True, stop=True)
                    last.then_inc(ssd_yp, 1)
                else:
                    pe.wait_ge(ssd_masks, 1)
                    pe.wait_ge(s0_loaded, 32)
                    for g in range(2):
                        for j in range(NSEQ):
                            last = mm(PS[0:L, 2 + g, :], CTm[:, (g * NSEQ + j) * 32:(g * NSEQ + j) * 32 + 32],
                                      s0g[g][:, j * 512:(j + 1) * 512], start=j == 0, stop=j == NSEQ - 1)
                    last.then_inc(ssd_yp, 1)
                if L == P:
                    pe.wait_ge(ssd_bt, c + 1)
                    for g in range(2):
                        last = mm(PS[:, 6 + g, :], Bt[0:L, g * P:(g + 1) * P], xw[0:L, g * 512:(g + 1) * 512],
                                  start=True, stop=True)
                    last.then_inc(ssd_st, 1)
                pe.wait_ge(ssd_ytok, c + 1)
                for i in range(8):
                    last = nc.tensor.transpose(banks(0, 2)[:, i * P:i * P + L], ytok[0:L, i * P:(i + 1) * P],
                                               ident[0:L, 0:L])
                last.then_inc(ssd_yTp, 1)
            def sum_tiles(bank, weights, src, done):
                for h in range(2):
                    for kt in range(KT):
                        last = mm(PS[:, bank + h, 0:HALF], weights, src[:, kt, h * HALF:(h + 1) * HALF],
                                  start=kt == 0, stop=kt == KT - 1)
                last.then_inc(done, 1)

            for j in range(NSEQ):
                b = 4 + 2 * (j % 2)
                if j == 2:
                    pe.wait_ge(sq_ready, 1)
                    sum_tiles(0, mean, proj[:, 0:8, :], ssq_psum)
                if j >= 2:
                    pe.wait_ge(ssd_updone, j - 1)
                for g in range(2):
                    last = mm(PS[:, b + g, :], Btm[0:32, j * 256 + g * P:j * 256 + (g + 1) * P],
                              xw[0:32, g * 512:(g + 1) * 512], start=True, stop=True)
                last.then_inc(ssd_upd, 1)

            def merge(name, y, y_ready_, n):
                b0, _, a0 = PHASES[name]
                with pe.Fori(0, 2) as it:
                    for i in range(RING):
                        if i == 1:
                            pe.wait_ge(y_ready_, n)
                        dense_block(b0 + i, a0 + 2 * i, uT if i % 2 == 0 else y, it)

            pe.wait_ge(sd_ready, 1)
            merge("merge0", proj[:, 12:20, :], br_ready, 1)
            dense("qkvo", 16, uT)

            for s in acc_free:
                pe.wait_ge(s, PHASES["merge1"][2] // 2 + 1)
            pe.wait_ge(evac_qk, 32)
            for c, (t0, L) in enumerate(CHUNKS):
                cols = slice(t0, t0 + L)
                if c:
                    pe.wait_ge(ml_h, c)
                for i in range(8):
                    nc.tensor.transpose(banks(0, 2)[0:L, i * P:(i + 1) * P], proj[:, 8 + i, cols], ident)
                for i in range(8):
                    last = nc.tensor.transpose(banks(2, 2)[0:L, i * P:(i + 1) * P], proj[:, 16 + i, cols], ident)
                last.then_inc(ml_kv, 1)
                if c:
                    pe.wait_ge(ml_out, c)
                    pe.wait_ge(ml_stdone, c)
                for h in range(4):
                    for k in range(2):
                        mm(PS[0:L, 4, h * P:h * P + L], proj[:, 8 + 2 * h + k, cols], proj[:, 2 * h + k, cols],
                           start=k == 0, stop=k == 1)
                for h in range(4):
                    mm(PS[0:L, 5, h * P:h * P + L], sel[64:68, h, 0:L], G[64:68, 3, cols], start=True, stop=True)
                for h in range(4):
                    last = mm(PS[:, 6, h * P:h * P + L], sel[64:68, h, :], G[64:68, 5, cols], start=True, stop=True)
                last.then_inc(ml_sc, 1)
                pe.wait_ge(ml_w, c + 1)
                pe.wait_ge(ml_va, c + 1)
                pe.wait_ge(ml_qs, c + 1)
                for h in range(4):
                    last = mm(PS[0:L, h, 0:257], Em[0:L, h * P:h * P + L], vaug[0:L, h, :], start=True, stop=c == 0)
                    if c and L == P:
                        for k in range(2):
                            last = mm(PS[0:L, h, 0:257], qs[:, (2 * h + k) * P:(2 * h + k) * P + L], CT[:, h, k, :],
                                      start=False, stop=k == 1)
                if L == P:
                    last.then_inc(ml_num, 1)
                    for i in range(8):
                        if i >= 2:
                            pe.wait_ge(ml_upd, 8 * c + i - 1)
                        h, k = i // 2, i % 2
                        mm(PS[:, 6 + i % 2, 0:257], kw[0:L, h * 256 + k * P:h * 256 + (k + 1) * P], vaug[0:L, h, :],
                           start=True, stop=True).then_inc(ml_st, 1)
                else:
                    n = 0
                    for i in range(16):
                        h, k = i // 4, i // 2 % 2
                        pe.wait_ge(caug_l[i % NCB], 16 * (i // NCB + 1))
                        pe.wait_ge(ml_qm, i + 1)
                        for j in range(4):
                            last = mm(PS[0:L, h, 0:257], qmask[i % 2][:, j * 32:(j + 1) * 32], CB[i % NCB][:, j, :],
                                      start=False, stop=i % 4 == 3 and j == 3)
                        for j in range(4):
                            if n >= 4:
                                pe.wait_ge(ml_upd, 32 + n - 3)
                            last = mm(PS[:, 4 + n % 4, 0:257], kwmask[i % 2][0:32, j * P:(j + 1) * P], vaug[0:32, h, :],
                                      start=True, stop=True)
                            last.then_inc(ml_st, 1)
                            n += 1
                    pe.wait_ge(ml_upd, 32 + n)
                    pe.sem_inc(ml_num, 1)
                pe.wait_ge(ml_hn, c + 1)
                for i in range(8):
                    last = nc.tensor.transpose(banks(4, 2)[:, i * P:i * P + L], hbuf[0:L, i * P:(i + 1) * P],
                                               ident[0:L, 0:L])
                last.then_inc(ml_hT, 1)

            pe.wait_ge(ml_h, 5)
            merge("merge1", proj[:, 24:32, :], ml_out, 5)
            dense("up", 4, uT)
            ada("ada_ffn", 1)

            b0, _, a0 = PHASES["poolw"]
            wait_block(b0)
            pe.wait_ge(pool_d, 1)
            for n in range(8):
                g, m = n // 2, n % 2
                pe.wait_ge(acc_free[n % 2], (a0 + n) // 2 + 1)
                for k in range(2):
                    for h in range(2):
                        last = mm(acc(n % 2)[:, h, :], ring[:, b0 % RING, (g * 2 + k) * 256 + m * P:(g * 2 + k) * 256 + m * P + P],
                                  dpool[:, 2 * g + k, h * HALF:(h + 1) * HALF], start=k == 0, stop=k == 1)
                last.then_inc(group_done, 1)
            merge("merge2", proj[:, 8:16, :], evac_pool, 8)
            pe.wait_ge(gate_used, 2 + 24)
            dense("out", 4, merged)

            def layer_norm_sums(n, src, sq):
                pe.wait_ge(r_ready, n + 1)
                sum_tiles(4, mean, src, ln_mu)
                pe.wait_ge(ln_sq, n + 1)
                sum_tiles(6, mean, sq, ln_var)

            pe.wait_ge(ada_ready, 2)
            layer_norm_sums(0, proj[:, 0:8, :], proj[:, 16:24, :])
            pe.wait_ge(u2_ready, 1)
            for c, (t0, L) in enumerate(CHUNKS):
                for kt in range(KT):
                    last = mm(PS[0:L, 4, c * 20:(c + 1) * 20], uT[:, kt, t0:t0 + L], wr[:, kt, :],
                              start=kt == 0, stop=kt == KT - 1)
            last.then_inc(rt_psum, 1)
            for c, (t0, L) in enumerate(CHUNKS):
                b = 2 * (c % 2)
                if c >= 2:
                    pe.wait_ge(u2r_ready, c - 1)
                for kt in range(KT):
                    last = nc.tensor.transpose(banks(b, 2)[0:L, kt * P:(kt + 1) * P], uT[:, kt, t0:t0 + L], ident)
                last.then_inc(u2p, 1)
            pe.wait_ge(ohs_ready, 1)
            for c, (t0, L) in enumerate(CHUNKS):
                for k in range(c + 1):
                    mm(PS[0:L, 4, c * NE:(c + 1) * NE], (one if k < c else cc("mask"))[:, 0:L], rt[:, k, 96:112],
                       start=k == 0, stop=k == c)
            for k in range(5):
                last = mm(PS[:, 4, 80:96], one, rt[:, k, 96:112], start=k == 0, stop=k == 4)
            last.then_inc(cnt_psum, 1)

            def at(b, it):
                return b if it is None else it * NBUF + b

            def rows_T(b, it=None):
                pe.wait_ge(x_got[b % NBUF], 16 * (b // NBUF + 1) if it is None else it * 16 + 16 * (b // NBUF + 1))
                if b:
                    pe.wait_ge(xt_ready, at(b, it))
                for kt in range(KT):
                    last = nc.tensor.transpose(banks(0, 2)[:, kt * P:(kt + 1) * P], X3[b % NBUF][:, kt * P:(kt + 1) * P], ident)
                last.then_inc(xt_psum, 1)

            def gate_up(b, it=None):
                pe.wait_ge(e_loaded[b % NBUF], 16 * (b // NBUF + 1) if it is None else it * 16 + 16 * (b // NBUF + 1))
                pe.wait_ge(xt_ready, at(b + 1, it))
                if b:
                    pe.wait_ge(h_ready, at(b, it))
                for kt in range(KT):
                    last = mm(PS[:, 2, :], XT3[b % NBUF][:, kt, :], E3[b % NBUF][:, kt * 512:(kt + 1) * 512],
                              start=kt == 0, stop=kt == KT - 1)
                last.then_inc(gu_psum, 1)

            def hidden_T(b, it=None):
                pe.wait_ge(h_ready, at(b + 1, it))
                if b:
                    pe.wait_ge(hT_ready, at(b, it))
                for f in range(2):
                    last = nc.tensor.transpose(PS[:, 3, f * P:(f + 1) * P], H3[b % NBUF][:, f * P:(f + 1) * P], ident)
                last.then_inc(h_psum, 1)

            def down(b, it=None):
                pe.wait_ge(hT_ready, at(b + 1, it))
                if b:
                    pe.wait_ge(y_ready, at(b, it))
                for n in range(2):
                    for f in range(2):
                        last = mm(PS[:, 4 + n, :], HT3[b % NBUF][:, f * P:(f + 1) * P],
                                  E3[b % NBUF][:, 4096 + f * 1024 + n * 512:4096 + f * 1024 + (n + 1) * 512],
                                  start=f == 0, stop=f == 1)
                last.then_inc(y_psum, 1)

            def step(b, it=None, first=False, last=False):
                if not last:
                    rows_T(b + 1, it)
                gate_up(b, it)
                if not first:
                    down(b - 1, it)
                hidden_T(b, it)

            def run_blocks(first, last):
                turns = (last - first - 2) // NBUF
                rows_T(first)
                step(first, first=True)
                with pe.Fori(0, turns) as it:
                    for b in range(first + 1, first + 1 + NBUF):
                        step(b, it)
                for b in range(first + 1 + turns * NBUF, last):
                    step(b, last=b == last - 1)
                down(last - 1)

            pe.wait_ge(cnt_used, 1)
            pe.wait_ge(pos_ready, 1)
            further = pe.value_load(n_further, min_val=0, max_val=XB)
            run_blocks(0, NE)
            with pe.If(further > 0):
                run_blocks(NE, NB)
            for c, (t0, L) in enumerate(CHUNKS):
                b = 2 * (c % 2)
                pe.wait_ge(moe_ready, c + 1)
                if c >= 2:
                    pe.wait_ge(moeT_ready, c - 1)
                for kt in range(KT):
                    last = nc.tensor.transpose(banks(b, 2)[:, kt * P:kt * P + L], BK[c][0][0:L, kt * P:(kt + 1) * P],
                                               ident[0:L, 0:L])
                last.then_inc(moeT_psum, 1)
            layer_norm_sums(1, merged, proj[:, 20:28, :])

        @block.scalar
        def _(act):
            made = {}

            def do(ins, s=act_step, n=1):
                ins.then_inc(s, 1)
                made[s] = made.get(s, 0) + 1
                act.wait_ge(s, made[s])

            for s in acc_free:
                act.sem_inc(s, 1)

            def evac(name, n, dst_tile, s, **kw_):
                _, g0, _ = PHASES[name]
                if n >= 16:
                    with act.Fori(0, n // 8) as it:
                        for i in range(8):
                            act.wait_ge(group_done, it * 8 + (g0 + i + 1))
                            nc.scalar.copy(proj[:, bass.ds(it * 8 + (dst_tile + i), 1), :].rearrange(
                                "p o (h t) -> p (o h) t", h=2), acc(i % 2)).then_inc(acc_free[i % 2], 1)
                    rest = range(n // 8 * 8, n)
                else:
                    rest = range(n)
                for i in rest:
                    act.wait_ge(group_done, g0 + i + 1)
                    nc.scalar.copy(halves(proj[:, dst_tile + i, :]), acc(i % 2)).then_inc(acc_free[i % 2], 1)
                a_end = PHASES[name][2] + n
                for x in acc_free:
                    act.wait_ge(x, a_end // 2 + 1)
                act.sem_inc(s, n)

            def ada_copy(name):
                _, g0, _ = PHASES[name]
                for i in range(12):
                    act.wait_ge(group_done, g0 + 2 * i + 2)
                    nc.scalar.copy(arow[:, i * 256:(i + 1) * 256], PS[0:9, 4 + i % 2, 0:256]).then_inc(ada_rows, 1)

            ada_copy("ada_mix")
            act.wait_ge(gates_psum, 1)
            act.wait_ge(small_loaded, 48)
            do(nc.scalar.activation(halves(G[0:68, 0, :]), PS[0:68, 4:6, 0:HALF], ACT.Identity,
                                    bias=vv("row_bias", 0)[0:68]), xrow_ready)
            do(nc.scalar.activation(exl[0:16, 0, 0:1], vv("a_log", 0)[0:16], ACT.Exp))
            act.wait_ge(rabs_ready, 1)
            do(nc.scalar.activation(G[0:68, 1, :], G[0:68, 1, :], ACT.Exp, scale=-1.0), rexp_ready)
            act.wait_ge(rw_ready, 1)
            do(nc.scalar.activation(G[0:68, 5, :], G[0:68, 2, :], ACT.Ln), rln_ready)
            def z_tiles(first, last):
                for i in range(first, last):
                    act.wait_ge(group_done, PHASES["z"][1] + i + 1)
                    nc.scalar.activation(halves(proj[:, 12 + i, :]), acc(i % 2), ACT.Silu).then_inc(z_silu, 1)
                    act.wait_ge(z_silu, i + 1)
                    act.sem_inc(acc_free[i % 2], 1)

            z_tiles(0, 6)
            act.wait_ge(cumd_ready, 1)
            do(nc.scalar.activation(G[0:16, 3, :], G[0:16, 2, :], ACT.Exp))
            do(nc.scalar.activation(G[0:16, 4, :], G[0:16, 4, :], ACT.Exp))
            do(nc.scalar.activation(G[64:68, 5, :], G[64:68, 5, :], ACT.Exp))
            do(nc.scalar.activation(G[64:68, 0, :], G[64:68, 4, :], ACT.Exp, scale=-1.0))
            do(nc.scalar.activation(G[64:68, 6, :], G[64:68, 6, :], ACT.Exp), rowexp_ready)

            z_tiles(6, 8)
            _, g0, _ = PHASES["xbc"]

            def conv_in(i):
                act.wait_ge(group_done, g0 + i + 1)
                nc.scalar.copy(halves(cin[:, i % 2, :]), acc(i % 2)).then_inc(conv_x, 1)
                act.wait_ge(conv_x, i + 1)
                act.sem_inc(acc_free[i % 2], 1)

            def conv_out(i):
                act.wait_ge(conv_pre, i + 1)
                do(nc.scalar.activation(proj[:, i, :], proj[:, i, :], ACT.Silu, bias=vv("conv_b", i)), conv_silu)

            for i in range(8):
                if i >= 2:
                    conv_out(i - 2)
                conv_in(i)
            act.wait_ge(tok_psum, 1)
            for bank, w, a0 in ((6, 64, 0), (7, 16, 64)):
                do(nc.scalar.copy(tg[:, 0:4, a0:a0 + w], PS[:, bank, 0:4 * w].rearrange("p (c n) -> p c n", c=4)))
                do(nc.scalar.copy(tg[0:32, 4, a0:a0 + w], PS[0:32, bank, 4 * w:5 * w]), tok_ready)
            do(nc.scalar.copy(exl[:], PS[:, 6, 320:512].rearrange("p (h s) -> p h s", h=16)))
            do(nc.scalar.copy(wpb[:], PS[:, 7, 80:128].rearrange("p (h s) -> p h s", h=4)), tok_ready)
            for i in range(8, 12):
                conv_out(i - 2)
                conv_in(i)
            conv_out(10)
            conv_out(11)
            for c, (t0, L) in enumerate(CHUNKS):
                act.wait_ge(ssd_xb, c + 1)
                do(nc.scalar.copy(Bt[0:L, :], PS[0:L, 6, 0:256]), ssd_bt)
                act.wait_ge(ssd_seg, c + 1)
                e = Es[0:L, :].rearrange("p (h l) -> p h l", h=16)[:, :, 0:L]
                do(nc.scalar.activation(e, e, ACT.Exp), ssd_exp)
            act.wait_ge(ssd_out, 5)
            do(nc.scalar.activation(proj[:, 0:8, :], proj[:, 12:20, :], ACT.Square), sq_ready)
            act.wait_ge(ssq_psum, 1)
            do(nc.scalar.activation(halves(gs[:, 0, :]), PS[:, 0:2, 0:HALF], ACT.Sqrt, bias=cc("eps")[:, 1:2]), sd_ready)
            act.wait_ge(br_ready, 1)

            def gates(name, b):
                _, g0, _ = PHASES[name]
                a = VEC["gate_b"][0]
                with act.Fori(0, 2) as it:
                    for i in range(4):
                        g = 4 * (i // 2) + i % 2
                        act.wait_ge(group_done, it * 8 + (g0 + g + 1))
                        act.wait_ge(gate_used, it * 4 + (8 * b + i + 1))
                        nc.scalar.activation(halves(gs[:, i % 2, :]), acc(i % 2), ACT.Sigmoid,
                                             bias=V[:, bass.ds(it * 4 + (a + 8 * b + i), 1)]).then_inc(gate_ready, 1)

            act.sem_inc(gate_used, 2)
            gates("merge0", 0)
            evac("qkvo", 32, 0, evac_qk)
            do(nc.scalar.activation(proj[:, 24:32, :], proj[:, 24:32, :], ACT.Sigmoid), og_ready)
            for c, (t0, L) in enumerate(CHUNKS):
                act.wait_ge(ml_kv, c + 1)
                do(nc.scalar.copy(vaug[0:L, :, 0:256], banks(2, 2)[0:L, :].rearrange("p (h v) -> p h v", h=4)), ml_va)
                act.wait_ge(ml_d, c + 1)
                e = Em[0:L, :].rearrange("p (h l) -> p h l", h=4)[:, :, 0:L]
                do(nc.scalar.activation(e, e, ACT.Exp), ml_exp)
                act.wait_ge(ml_h, c + 1)
                do(nc.scalar.activation(hstat[0:L, 36:40], hstat[0:L, 36:40], ACT.Sqrt, bias=cc("eps")[0:L, 0:1]), ml_sd)
            act.wait_ge(ml_out, 5)
            gates("merge1", 1)
            evac("up", 8, 0, evac_up)
            act.wait_ge(ml_stdone, 5)
            ada_copy("ada_ffn")
            _, g0, _ = PHASES["poolw"]
            for i in range(8):
                act.wait_ge(group_done, g0 + i + 1)
                nc.scalar.activation(halves(proj[:, 8 + i, :]), acc(i % 2), ACT.Copy,
                                     scale=vv("pool_scale", i)).then_inc(acc_free[i % 2], 1)
            for x in acc_free:
                act.wait_ge(x, PHASES["merge2"][2] // 2 + 1)
            act.sem_inc(evac_pool, 8)
            gates("merge2", 2)
            act.wait_ge(pool_stored, 1)
            evac("out", 8, 0, evac_out)

            def layer_norm(n, cen, sq):
                act.wait_ge(ln_cen, n + 1)
                do(nc.scalar.activation(sq, cen, ACT.Square), ln_sq)
                act.wait_ge(ln_var, n + 1)
                do(nc.scalar.activation(halves(gs[:, 0, :]), PS[:, 6:8, 0:HALF], ACT.Sqrt, bias=cc("eps")[:, 0:1]), ln_sd)

            layer_norm(0, proj[:, 0:8, :], proj[:, 16:24, :])
            act.wait_ge(rt_d, 1)
            do(nc.scalar.activation(rt[:, :, 24:28], rt[:, :, 24:28], ACT.Exp), rt_e)
            act.wait_ge(rt_dd, 1)
            do(nc.scalar.activation(rt[:, :, 60:61], rt[:, :, 60:61], ACT.Exp), rt_e2)
            for c, (t0, L) in enumerate(CHUNKS):
                act.wait_ge(u2p, c + 1)
                do(nc.scalar.copy(u2r[c][0:L, :], banks(2 * (c % 2), 2)[0:L, :]), u2r_ready)
            for s in (u2_stored,):
                act.wait_ge(s, 16 * 5)

            def block_step(b, it=None):
                i = b % NBUF
                v = b + 1 if it is None else it * NBUF + (b + 1)
                act.wait_ge(xt_psum, v)
                nc.scalar.copy(XT3[i], banks(0, 2).rearrange("p (k s) -> p k s", k=KT)).then_inc(xt_ready, 1)
                act.wait_ge(gu_psum, v)
                nc.scalar.activation(H3[i], PS[:, 2, 0:256], ACT.Silu).then_inc(sg_ready, 1)

            def run_blocks(first, last):
                turns = (last - first) // NBUF
                with act.Fori(0, turns) as it:
                    for b in range(first, first + NBUF):
                        block_step(b, it)
                for b in range(first + turns * NBUF, last):
                    block_step(b)

            act.wait_ge(pos_ready, 1)
            further = act.value_load(n_further, min_val=0, max_val=XB)
            run_blocks(0, NE)
            with act.If(further > 0):
                run_blocks(NE, NB)
            for c, (t0, L) in enumerate(CHUNKS):
                act.wait_ge(moeT_psum, c + 1)
                do(nc.scalar.copy(uT[:, :, t0:t0 + L], banks(2 * (c % 2), 2).rearrange("p (k s) -> p k s", k=KT)[:, :, 0:L]),
                   moeT_ready)
            layer_norm(1, merged[:], proj[:, 20:28, :])

        @block.vector
        def _(dve):
            v = nc.vector
            made = {}

            def do(ins, s=dve_step):
                ins.then_inc(s, 1)
                made[s] = made.get(s, 0) + 1
                dve.wait_ge(s, made[s])

            def bc(ap, shape):
                return ap.to_broadcast(shape)

            def smp(t):
                return t.rearrange("p a (j t) -> p a j t", j=NSEQ)

            def ada_finish(dst, name, bank):
                a, _ = VEC[name]
                do(v.tensor_tensor(dst[:], PS[:, bank, 0:216].rearrange("p (m s) -> p m s", m=24),
                                   bc(V[:, a:a + 24].unsqueeze(2), [P, 24, 9]), ALU.add))
                do(v.tensor_scalar(dst[:, 8:24, :], dst[:, 8:24, :], 1.0, None, ALU.add), ada_ready)

            def modulate(dst, src, ada_, done):
                for i in range(KT):
                    do(v.tensor_scalar(dst[:, i, 0:TP], src[:, i, 0:TP], ada_[:, 8 + i, 0:1], ada_[:, i, 0:1],
                                       ALU.mult, ALU.add))
                do(v.tensor_tensor(smp(dst[:, :, TP:NT]), smp(src[:, :, TP:NT]),
                                   bc(ada_[:, 8:16, 1:9].unsqueeze(3), [P, 8, NSEQ, TS]), ALU.mult))
                do(v.tensor_tensor(smp(dst[:, :, TP:NT]), smp(dst[:, :, TP:NT]),
                                   bc(ada_[:, 0:8, 1:9].unsqueeze(3), [P, 8, NSEQ, TS]), ALU.add), done)

            do(v.memset(zeros, 0), zero_ready)
            do(v.memset(no_rows, 0.0))
            dve.wait_ge(small_loaded, 48)
            dve.wait_ge(ada_psum, 12)
            ada_finish(adaM, "b_ada_mix", 7)
            dve.wait_ge(x_loaded, 16)
            modulate(uT, uT, adaM, u_ready)

            r16, r4 = slice(0, 16), slice(64, 68)
            do(v.memset(mp[64:68, 0:1], 0.0))
            dve.wait_ge(rows_in_loaded, 64)
            dve.wait_ge(xrow_ready, 1)
            do(v.scalar_tensor_tensor(G[0:68, 1, :], G[0:68, 0, :], -1.0, G[0:68, 0, :], ALU.mult, ALU.max), rabs_ready)
            dve.wait_ge(rexp_ready, 1)
            do(v.tensor_scalar(G[0:68, 2, :], G[0:68, 1, :], 1.0, None, ALU.add), rw_ready)
            do(v.tensor_scalar(G[0:68, 3, :], G[0:68, 2, :], -1.0, None, ALU.add))
            do(v.tensor_scalar(G[0:68, 4, :], G[0:68, 3, :], 0.0, None, ALU.is_equal))
            do(v.tensor_tensor(G[0:68, 3, :], G[0:68, 3, :], G[0:68, 4, :], ALU.add))
            do(v.reciprocal(G[0:68, 3, :], G[0:68, 3, :]))
            dve.wait_ge(rln_ready, 1)
            do(v.tensor_tensor(G[0:68, 5, :], G[0:68, 5, :], G[0:68, 4, :], ALU.add))
            do(v.tensor_tensor(G[0:68, 5, :], G[0:68, 5, :], G[0:68, 1, :], ALU.mult))
            do(v.tensor_tensor(G[0:68, 5, :], G[0:68, 5, :], G[0:68, 3, :], ALU.mult))
            do(v.scalar_tensor_tensor(G[r16, 6, :], G[r16, 0, :], 0.0, G[r16, 5, :], ALU.max, ALU.add))
            do(v.scalar_tensor_tensor(G[r4, 6, :], G[r4, 0, :], 0.0, G[r4, 5, :], ALU.min, ALU.subtract))
            do(v.tensor_scalar(G[r16, 1, :], G[r16, 6, :], exl[0:16, 0, 0:1], -1.0, ALU.mult, ALU.mult))
            do(v.tensor_tensor_scan(G[r16, 2, :], seg0[r16, :], G[r16, 1, :], 0.0, ALU.mult, ALU.add))
            do(v.tensor_tensor_scan(G[r4, 2, :], seg0[r4, :], G[r4, 6, :], 0.0, ALU.mult, ALU.add))
            do(v.tensor_copy(G[r4, 1, :], G[32:36, 0, :]))
            do(v.tensor_tensor(G[r4, 1, :], G[r4, 1, :], G[r4, 2, :], ALU.subtract))
            for s in range(NSEG):
                a, b = (s * P, s * P + P) if s < 4 else (TP + (s - 4) * TS, TP + (s - 3) * TS)
                do(v.tensor_tensor_scan(G[r4, 3, a:b], G[r4, 1, a:b], G[r4, 1, a:b], mp[r4, s:s + 1], ALU.max, ALU.max))
                if s < 3:
                    do(v.tensor_tensor(mp[r4, s + 1:s + 2], G[r4, 3, b - 1:b], G[r4, 2, b - 1:b], ALU.add))
            do(v.tensor_tensor(G[r4, 4, :], G[r4, 3, :], G[r4, 2, :], ALU.add), m_ready)

            def segs(row, r):
                return (row[r, 0:TP].rearrange("p (s t) -> p s t", s=4),
                        row[r, TP:NT].rearrange("p (s t) -> p s t", s=NSEQ))

            for k, (n, s0, w) in enumerate(((4, 0, P), (NSEQ, 4, TS))):
                M_, a_ = segs(G[:, 3, :], r4)[k], segs(G[:, 1, :], r4)[k]
                cum_ = segs(G[:, 2, :], r16)[k]
                do(v.tensor_tensor(segs(G[:, 5, :], r4)[k], bc(mp[r4, s0:s0 + n].unsqueeze(2), [4, n, w]), M_,
                                   ALU.subtract))
                do(v.tensor_tensor(segs(G[:, 6, :], r4)[k], a_, bc(M_[:, :, w - 1:w], [4, n, w]), ALU.subtract))
                do(v.tensor_tensor(segs(G[:, 4, :], r16)[k], bc(cum_[:, :, w - 1:w], [16, n, w]), cum_, ALU.subtract))
            dve.sem_inc(cumd_ready, 1)
            dve.wait_ge(rowexp_ready, 1)
            do(v.tensor_scalar(G[r4, 6, :], G[r4, 6, :], 0.0625, None, ALU.mult))
            dg16 = G[r16, 1, 0:192].rearrange("p (h s) -> p h s", h=16)
            dg4 = G[r4, 2, 0:48].rearrange("p (h s) -> p h s", h=4)
            for k, (n, s0, w) in enumerate(((4, 0, P), (NSEQ, 4, TS))):
                ex = segs(G[:, 3, :], r16)[k][:, :, w - 1:w].rearrange("p s o -> p o s")
                do(v.tensor_tensor(dg16[:, :, s0:s0 + n], bc(ex, [16, 16, n]),
                                   bc(ident[r16, 0:16].unsqueeze(2), [16, 16, n]), ALU.mult))
                wp = segs(G[:, 5, :], r4)[k][:, :, w - 1:w].rearrange("p s o -> p o s")
                do(v.tensor_tensor(dg4[:, :, s0:s0 + n], bc(wp, [4, 4, n]),
                                   bc(ident[r4, 64:68].unsqueeze(2), [4, 4, n]), ALU.mult))
            dve.sem_inc(rows_ready, 1)

            dve.wait_ge(conv_in_loaded, 16)
            do(v.tensor_copy(sx[:, :, :, 0:3], hist))
            for i in range(12):
                x_ = cin[:, i % 2, :]
                dve.wait_ge(conv_x, i + 1)
                do(v.tensor_copy(sx[:, i, :, 3:7], x_[:, TP:NT].rearrange("p (j t) -> p j t", j=NSEQ)))
                do(v.tensor_copy(tail[:, i, :], x_[:, TP - 3:NT]), conv_tail)

                def tap(k):
                    return vv("conv_w", k * 12 + i)
                o = proj[:, i, 0:TP]
                os_ = proj[:, i, TP:NT].rearrange("p (j t) -> p j t", j=NSEQ)
                do(v.tensor_scalar(o, x_[:, 0:TP], tap(3), None, ALU.mult))
                do(v.tensor_scalar(os_, sx[:, i, :, 3:7], tap(3), None, ALU.mult))
                for k in (2, 1, 0):
                    d = 3 - k
                    do(v.scalar_tensor_tensor(o[:, d:], x_[:, 0:TP - d], tap(k), o[:, d:], ALU.mult, ALU.add))
                    do(v.scalar_tensor_tensor(os_, sx[:, i, :, k:k + 4], tap(k), os_, ALU.mult, ALU.add),
                       dve_step if k else conv_pre)

            dve.wait_ge(tok_ready, 3)
            for c, (t0, L) in enumerate(CHUNKS):
                cols = slice(t0, t0 + L)
                x16 = lambda t: t[0:L, :].rearrange("p (h d) -> p h d", h=16)
                tgc = lambda a, n=16, w=64: bc(tg[0:L, c, a:a + n].unsqueeze(2), [L, n, w])
                mk = cc("mask")[0:L, 0:L] if L == P else cc("smask")[0:L, :]
                dve.wait_ge(ssd_xb, c + 1)
                do(v.tensor_tensor(x16(xdt), banks(4, 2)[0:L, :].rearrange("p (h d) -> p h d", h=16), tgc(0), ALU.mult))
                if c and L == P:
                    dve.wait_ge(ssd_st, c)
                do(v.tensor_tensor(x16(xw), x16(xdt), tgc(48), ALU.mult))
                dve.wait_ge(ssd_bt, c + 1)
                do(v.tensor_tensor(cbm[0:L, :].rearrange("p (g l) -> p g l", g=2)[:, :, 0:L],
                                   PS[0:L, 6, 256:512].rearrange("p (g l) -> p g l", g=2)[:, :, 0:L],
                                   bc(mk.unsqueeze(1), [L, 2, L]), ALU.mult))
                dve.wait_ge(ssd_bc, c + 1)
                do(v.tensor_tensor(Es[0:L, :].rearrange("p (h l) -> p h l", h=16)[:, :, 0:L],
                                   banks(0, 4)[0:L, :].rearrange("p (h l) -> p h l", h=16)[:, :, 0:L],
                                   tgc(16, 16, L), ALU.subtract))
                e = Es[0:L, :].rearrange("p (h l) -> p h l", h=16)[:, :, 0:L]
                do(v.tensor_scalar(e, e, 0.0, None, ALU.min), ssd_seg)
                if L < P:
                    dve.wait_ge(z_silu, 8)
                    for g in range(2):
                        do(v.tensor_tensor(CTm[:, g * 256:(g + 1) * 256].rearrange("p (j t) -> p j t", j=NSEQ),
                                           bc(proj[:, 10 + g, cols].unsqueeze(1), [P, NSEQ, 32]), seqcol, ALU.mult))
                    dve.wait_ge(ssd_bt, 5)
                    dve.wait_ge(rows_zeroed, 16)
                    do(v.tensor_tensor(Btm[0:32, :].rearrange("p (j n) -> p j n", j=NSEQ),
                                       bc(Bt[0:32, :].unsqueeze(1), [32, NSEQ, 256]),
                                       bc(cc("tokseq")[0:32, :].unsqueeze(2), [32, NSEQ, 256]), ALU.mult), ssd_masks)
                dve.wait_ge(ssd_exp, c + 1)
                e = Es[0:L, :].rearrange("p (g h l) -> p g h l", g=2, h=8)[:, :, :, 0:L]
                cb = cbm[0:L, :].rearrange("p (g l) -> p g l", g=2)[:, :, 0:L]
                do(v.tensor_tensor(e, e, bc(cb.unsqueeze(2), [L, 2, 8, L]), ALU.mult), ssd_w)
                dve.wait_ge(ssd_yp, c + 1)
                if c == 0:
                    do(v.tensor_copy(ytok[0:L, :], banks(4, 2)[0:L, :]), ssd_ytok)
                else:
                    do(v.tensor_tensor(x16(ytok), banks(2, 2)[0:L, :].rearrange("p (h d) -> p h d", h=16), tgc(32), ALU.mult))
                    do(v.tensor_tensor(ytok[0:L, :], ytok[0:L, :], banks(4, 2)[0:L, :], ALU.add), ssd_ytok)
                if L == P:
                    dve.wait_ge(ssd_st, c + 1)
                    if c == 0:
                        do(v.tensor_copy(sT, banks(6, 2)), ssd_stdone)
                    else:
                        s16 = sT.rearrange("p (h d) -> p h d", h=16)
                        do(v.tensor_tensor(s16, s16, bc(exl[:, :, c:c + 1], [P, 16, 64]), ALU.mult))
                        do(v.tensor_tensor(sT, sT, banks(6, 2), ALU.add), ssd_stdone)
                dve.wait_ge(ssd_yTp, c + 1)
                dve.wait_ge(z_silu, 8)
                for i in range(8):
                    do(v.scalar_tensor_tensor(ytok[:, i * P:i * P + L], proj[:, i, cols], vv("ssd_D", i),
                                              banks(0, 2)[:, i * P:i * P + L], ALU.mult, ALU.add))
                do(v.tensor_tensor(proj[:, 12:20, cols], proj[:, 12:20, cols],
                                   ytok.rearrange("p (i l) -> p i l", i=8)[:, :, 0:L], ALU.mult), ssd_out)
            for j in range(NSEQ):
                b = 4 + 2 * (j % 2)
                for g in range(2):
                    t = s0g[g][:, j * 512:(j + 1) * 512]
                    t8 = t.rearrange("p (h d) -> p h d", h=8)
                    do(v.tensor_tensor(t8, t8, bc(exl[:, g * 8:(g + 1) * 8, 4 + j:5 + j], [P, 8, 64]), ALU.mult))
                dve.wait_ge(ssd_upd, j + 1)
                do(v.tensor_tensor(s0g[0][:, j * 512:(j + 1) * 512], s0g[0][:, j * 512:(j + 1) * 512], PS[:, b, :], ALU.add))
                do(v.tensor_tensor(s0g[1][:, j * 512:(j + 1) * 512], s0g[1][:, j * 512:(j + 1) * 512], PS[:, b + 1, :],
                                   ALU.add), ssd_updone)
            dve.wait_ge(sd_ready, 1)
            do(v.reciprocal(gs[:, 1, :], gs[:, 0, :]))
            for i in range(8):
                do(v.scalar_tensor_tensor(proj[:, 12 + i, :], proj[:, 12 + i, :], vv("ssd_norm_w", i), gs[:, 1, :],
                                          ALU.mult, ALU.mult), dve_step if i < 7 else br_ready)
            dve.wait_ge(ssd_stdone, 5)

            def merge(name, b):
                _, g0, _ = PHASES[name]
                with dve.Fori(0, 2) as it:
                    for i in range(4):
                        g = 4 * (i // 2) + 2 + i % 2
                        m = merged[:, bass.ds(it * 4 + i, 1), :].rearrange("p o (h t) -> p (o h) t", h=2)
                        s = halves(gs[:, i % 2, :])
                        dve.wait_ge(gate_ready, it * 4 + (8 * b + i + 1))
                        dve.sem_inc(acc_free[i % 2], 1)
                        dve.wait_ge(group_done, it * 8 + (g0 + g + 1))
                        if b == 0:
                            v.tensor_tensor(m, s, acc(i % 2), ALU.mult).then_inc(gate_used, 1)
                        else:
                            v.tensor_tensor(s, s, acc(i % 2), ALU.mult).then_inc(r2_ready, 1)
                            dve.wait_ge(r2_ready, it * 4 + (8 * (b - 1) + i + 1))
                            v.tensor_tensor(m, m, s, ALU.add).then_inc(gate_used, 1)
                        dve.wait_ge(gate_used, it * 4 + (8 * b + i + 3))
                        dve.sem_inc(acc_free[i % 2], 1)

            merge("merge0", 0)

            do(v.memset(vaug[:, :, 256:257], 1.0))
            dve.wait_ge(og_ready, 1)
            for c, (t0, L) in enumerate(CHUNKS):
                cols = slice(t0, t0 + L)
                mk = cc("mask16")[0:L, 0:L] if L == P else cc("smask16")[0:L, :]
                e = Em[0:L, :].rearrange("p (h l) -> p h l", h=4)[:, :, 0:L]
                col4 = lambda b: PS[0:L, b, :].rearrange("p (h l) -> p h l", h=4)[:, :, 0:L]
                dve.wait_ge(ml_kv, c + 1)
                if c:
                    dve.wait_ge(ml_st, 8 * c)
                do(v.tensor_tensor(kw[0:L, :].rearrange("p (h d) -> p h d", h=4),
                                   banks(0, 2)[0:L, :].rearrange("p (h d) -> p h d", h=4),
                                   bc(tg[0:L, c, 76:80].unsqueeze(2), [L, 4, 256]), ALU.mult), ml_kw)
                dve.wait_ge(ml_sc, c + 1)
                do(v.tensor_tensor(e, bc(tg[0:L, c, 64:68].unsqueeze(2), [L, 4, L]), col4(5), ALU.subtract))
                do(v.tensor_scalar(e, e, 0.0, None, ALU.min), ml_d)
                if c:
                    q4 = qs.rearrange("p (h k l) -> p h k l", h=4, k=2)[:, :, :, 0:L]
                    w4 = PS[:, 6, :].rearrange("p (h l) -> p h l", h=4)[:, :, 0:L]
                    do(v.tensor_tensor(q4, proj[:, 0:8, cols].rearrange("p (h k) l -> p h k l", h=4),
                                       bc(w4.unsqueeze(2), [P, 4, 2, L]), ALU.mult), ml_qs)
                else:
                    dve.sem_inc(ml_qs, 1)
                dve.wait_ge(ml_exp, c + 1)
                do(v.tensor_tensor(e, e, bc(mk.unsqueeze(1), [L, 4, L]), ALU.mult))
                do(v.tensor_tensor(e, e, col4(4), ALU.mult), ml_w)
                if L == P:
                    for i in range(8):
                        h, k = i // 2, i % 2
                        dve.wait_ge(ml_st, 8 * c + i + 1)
                        if c:
                            if i == 0:
                                dve.wait_ge(ml_num, c + 1)
                            do(v.scalar_tensor_tensor(CT[:, h, k, :], CT[:, h, k, :], wpb[:, h, c:c + 1],
                                                      PS[:, 6 + i % 2, 0:257], ALU.mult, ALU.add), ml_upd)
                        else:
                            do(v.tensor_copy(CT[:, h, k, :], PS[:, 6 + i % 2, 0:257]), ml_upd)
                    dve.sem_inc(ml_stdone, 1)
                else:
                    def own_parts(i):
                        h, k, jh = i // 4, i // 2 % 2, i % 2
                        if i >= 2:
                            dve.wait_ge(ml_st, 32 + 4 * (i - 1))
                        do(v.tensor_tensor(kwmask[i % 2][0:32, :].rearrange("p (j d) -> p j d", j=4),
                                           bc(kw[0:32, h * 256 + k * P:h * 256 + (k + 1) * P].unsqueeze(1), [32, 4, P]),
                                           bc(cc("tokseq")[0:32, 4 * jh:4 * jh + 4].unsqueeze(2), [32, 4, P]), ALU.mult))
                        do(v.tensor_tensor(qmask[i % 2].rearrange("p (j t) -> p j t", j=4),
                                           bc(qs[:, (2 * h + k) * P:(2 * h + k) * P + 32].unsqueeze(1), [P, 4, 32]),
                                           seqcol[:, 4 * jh:4 * jh + 4, :], ALU.mult), ml_qm)

                    own_parts(0)
                    for i in range(16):
                        h, jh = i // 4, i % 2
                        if i + 1 < 16:
                            own_parts(i + 1)
                        for j in range(4):
                            n = 4 * i + j
                            dve.wait_ge(ml_st, 32 + n + 1)
                            t = CB[i % NCB][:, j, :]
                            do(v.scalar_tensor_tensor(t, t, wpb[:, h, 4 + 4 * jh + j:5 + 4 * jh + j],
                                                      PS[:, 4 + n % 4, 0:257], ALU.mult, ALU.add), ml_upd)
                        dve.sem_inc(ml_updone, 1)
                dve.wait_ge(ml_num, c + 1)
                if c:
                    dve.wait_ge(ml_hT, c)
                den = hstat[0:L, 0:4]
                do(v.tensor_copy(den, PS[0:L, 0:4, 256]))
                do(v.scalar_tensor_tensor(den, den, -1.0, den, ALU.mult, ALU.max))
                do(v.tensor_tensor(den, den, tg[0:L, c, 72:76], ALU.max))
                do(v.reciprocal(den, den))
                h4 = hbuf[0:L, :].rearrange("p (h d) -> p h d", h=4)
                do(v.tensor_tensor(h4, PS[0:L, 0:4, 0:256], bc(den.unsqueeze(2), [L, 4, 256]), ALU.mult))
                for h in range(4):
                    do(v.bn_stats(hstat[0:L, 4 + 6 * h:10 + 6 * h], h4[:, h, :]))
                    do(v.bn_aggr(hstat[0:L, 28 + 2 * h:30 + 2 * h], hstat[0:L, 4 + 6 * h:10 + 6 * h]))
                mv = hstat[0:L, 28:36].rearrange("p (h k) -> p h k", h=4)
                do(v.tensor_copy(hstat[0:L, 36:40], mv[:, :, 1]), ml_h)
                dve.wait_ge(ml_sd, c + 1)
                do(v.reciprocal(hstat[0:L, 36:40], hstat[0:L, 36:40]))
                for h in range(4):
                    do(v.tensor_scalar(h4[:, h, :], h4[:, h, :], mv[:, h, 0:1], hstat[0:L, 36 + h:37 + h],
                                       ALU.subtract, ALU.mult), dve_step if h < 3 else ml_hn)
                dve.wait_ge(ml_hT, c + 1)
                for i in range(8):
                    do(v.scalar_tensor_tensor(proj[:, 24 + i, cols], banks(4, 2)[:, i * P:i * P + L],
                                              vv("mlstm_norm_w", i), proj[:, 24 + i, cols], ALU.mult, ALU.mult),
                       dve_step if i < 7 else ml_out)
            merge("merge1", 1)

            dve.wait_ge(ml_stdone, 5)
            dve.wait_ge(evac_up, 8)
            dve.wait_ge(pool_loaded, 16)
            do(v.memset(padP[0][:, :, 0:15], 0.0))
            do(v.tensor_copy(padP[0][:, :, 15:527], proj[:, 0:8, 0:TP]))
            do(v.tensor_copy(padS[0][:, :, :, 15:19], smp(proj[:, 0:8, TP:NT])))
            for k in range(4):
                d, lo = 1 << k, (2 << k) - 1
                src, dst = k % 2, (k + 1) % 2
                do(v.tensor_tensor(padP[dst][:, 2 * k:8, lo:527], padP[src][:, 2 * k:8, lo:527],
                                   padP[src][:, 2 * k:8, lo - d:527 - d], ALU.add))
                for i in range(2 * k, 8):
                    do(v.tensor_tensor(padS[dst][:, i, :, lo:19], padS[src][:, i, :, lo:19],
                                       padS[src][:, i, :, lo - d:19 - d], ALU.add))
            for g in range(4):
                w, b = 2 << g, (g + 1) % 2
                t2 = slice(2 * g, 2 * g + 2)
                do(v.scalar_tensor_tensor(dpool[:, t2, 0:TP], padP[b][:, t2, 15:527], 1.0 / w, proj[:, t2, 0:TP],
                                          ALU.mult, ALU.subtract))
                a, _ = CST["invcnt"]
                do(v.tensor_tensor(dpool[:, t2, 0:w - 1], padP[b][:, t2, 15:14 + w],
                                   bc(C[:, a + 16 * g:a + 16 * g + w - 1].unsqueeze(1), [P, 2, w - 1]), ALU.mult))
                do(v.tensor_tensor(dpool[:, t2, 0:w - 1], dpool[:, t2, 0:w - 1], proj[:, t2, 0:w - 1], ALU.subtract))
                for i in range(2 * g, 2 * g + 2):
                    do(v.scalar_tensor_tensor(dpool[:, i, TP:NT].rearrange("p (j t) -> p j t", j=NSEQ),
                                              padS[b][:, i, :, 15:19], 1.0 / w,
                                              proj[:, i, TP:NT].rearrange("p (j t) -> p j t", j=NSEQ),
                                              ALU.mult, ALU.subtract), dve_step if i < 7 else pool_d)
            dve.wait_ge(ada_psum, 24)
            ada_finish(adaF, "b_ada_ffn", 7)
            merge("merge2", 2)

            def residual(dst, out_, x_, ada_, done):
                for i in range(KT):
                    do(v.tensor_scalar(out_[:, i, 0:TP], out_[:, i, 0:TP], ada_[:, 16 + i, 0:1], None, ALU.mult))
                do(v.tensor_tensor(smp(out_[:, :, TP:NT]), smp(out_[:, :, TP:NT]),
                                   bc(ada_[:, 16:24, 1:9].unsqueeze(3), [P, 8, NSEQ, TS]), ALU.mult))
                do(v.scalar_tensor_tensor(dst, x_, ALPHA, out_, ALU.mult, ALU.add), done)

            def layer_norm(n, r, dst, gname, bname):
                dve.wait_ge(ln_mu, n + 1)
                r4_ = r.rearrange("p k (h t) -> p k h t", h=2)
                do(v.tensor_tensor(r4_, r4_, bc(PS[:, 4:6, 0:HALF].unsqueeze(1), [P, KT, 2, HALF]), ALU.subtract), ln_cen)
                dve.wait_ge(ln_sd, n + 1)
                do(v.reciprocal(gs[:, 1, :], gs[:, 0, :]))
                dve.wait_ge(ln_sq, n + 1)
                do(v.tensor_tensor(r, r, bc(gs[:, 1:2, :], [P, KT, NT]), ALU.mult))
                for i in range(KT):
                    do(v.tensor_scalar(dst[:, i, :], r[:, i, :], vv(gname, i), vv(bname, i), ALU.mult, ALU.add),
                       dve_step if i < 7 else ln_done)

            dve.wait_ge(evac_out, 8)
            dve.wait_ge(xr_loaded, 16)
            residual(proj[:, 0:8, :], proj[:, 0:8, :], proj[:, 8:16, :], adaM, r_ready)
            layer_norm(0, proj[:, 0:8, :], merged, "ln1_g", "ln1_b")
            modulate(uT, merged, adaF, u2_ready)

            R = lambda a, b: rt[:, :, a:b]
            rank = bc(cc("rank").unsqueeze(1), [P, 5, 4])
            do(v.memset(rt[:], 0.0))
            dve.wait_ge(rt_psum, 1)
            do(v.tensor_tensor(rt[:, 0:4, 0:20], PS[:, 4, 0:80].rearrange("p (c n) -> p c n", c=4),
                               bc(vv("b_rt", 0, 20).unsqueeze(1), [P, 4, 20]), ALU.add))
            do(v.tensor_tensor(rt[0:32, 4, 0:20], PS[0:32, 4, 80:100], vv("b_rt", 0, 20)[0:32, :], ALU.add))

            def one_hot(src, mx, tmp, mn, dst):
                do(v.tensor_reduce(mx, src, AX.X, ALU.max))
                do(v.tensor_tensor(tmp, src, bc(mx, [P, 5, 4]), ALU.is_equal))
                do(v.tensor_tensor(tmp, tmp, rank, ALU.mult))
                do(v.tensor_reduce(mn, tmp, AX.X, ALU.min))
                do(v.tensor_tensor(dst, rank, bc(mn, [P, 5, 4]), ALU.is_equal))

            one_hot(R(0, 4), R(20, 21), R(24, 28), R(21, 22), R(28, 32))
            do(v.tensor_tensor(R(24, 28), R(0, 4), bc(R(20, 21), [P, 5, 4]), ALU.subtract), rt_d)
            dve.wait_ge(rt_e, 1)
            do(v.tensor_reduce(R(22, 23), R(24, 28), AX.X, ALU.add))
            do(v.reciprocal(R(22, 23), R(22, 23)))
            g4 = R(32, 48).rearrange("p c (g j) -> p c g j", g=4)
            do(v.tensor_tensor(g4, R(4, 20).rearrange("p c (g j) -> p c g j", g=4),
                               bc(R(28, 32).unsqueeze(3), [P, 5, 4, 4]), ALU.mult))
            do(v.tensor_reduce(R(48, 52), R(32, 48).rearrange("p c (g j) -> p c j g", g=4), AX.X, ALU.add))
            one_hot(R(48, 52), R(20, 21), R(24, 28), R(21, 22), R(52, 56))
            do(v.tensor_scalar(R(24, 28), R(52, 56), -BIG, None, ALU.mult))
            do(v.tensor_tensor(R(48, 52), R(48, 52), R(24, 28), ALU.add))
            one_hot(R(48, 52), R(23, 24), R(24, 28), R(21, 22), R(56, 60))
            do(v.tensor_tensor(R(60, 61), R(23, 24), R(20, 21), ALU.subtract), rt_dd)
            dve.wait_ge(rt_e2, 1)
            do(v.tensor_scalar(R(61, 62), R(60, 61), 1.0, None, ALU.add))
            do(v.reciprocal(R(61, 62), R(61, 62)))
            do(v.tensor_tensor(R(61, 62), R(61, 62), R(22, 23), ALU.mult))
            do(v.tensor_tensor(R(62, 63), R(61, 62), R(60, 61), ALU.mult))
            g44 = lambda a: R(a, a + 16).rearrange("p c (g j) -> p c g j", g=4)
            for a, o in ((64, 52), (80, 56)):
                do(v.tensor_tensor(g44(a), bc(R(28, 32).unsqueeze(3), [P, 5, 4, 4]), bc(R(o, o + 4).unsqueeze(2), [P, 5, 4, 4]),
                                   ALU.mult))
            do(v.tensor_tensor(R(96, 112), R(64, 80), R(80, 96), ALU.add))
            do(v.memset(rt[32:64, 4, 96:112], 0.0))
            do(v.memset(rt[64:P, 4, 96:112], 0.0), ohs_ready)
            tot, xtra, offs, dbase = (route[:, 16 * i:16 * i + 16] for i in range(4))
            cmpx = route[:, 64:64 + 16].rearrange("p n -> p n")
            dve.wait_ge(cnt_psum, 1)
            do(v.tensor_copy(tot, PS[:, 4, 80:96]))
            do(v.memset(rt[:, 4, 112:128], 0.0))
            do(v.tensor_copy(rt[:, 0:4, 112:128], PS[:, 4, 0:64].rearrange("p (c e) -> p c e", c=4)))
            do(v.tensor_copy(rt[0:32, 4, 112:128], PS[0:32, 4, 64:80]), cnt_used)
            do(v.tensor_scalar(xtra, tot, P + 0.5, None, ALU.is_gt))
            for j in (2, 3, 4):
                do(v.scalar_tensor_tensor(xtra, tot, j * P + 0.5, xtra, ALU.is_gt, ALU.add))
            do(v.tensor_tensor_scan(offs, one[:, 0:NE], xtra, 0.0, ALU.mult, ALU.add))
            do(v.scalar_tensor_tensor(dbase, offs, NE - 1.0, xtra, ALU.add, ALU.subtract))
            do(v.tensor_tensor(dbase, dbase, cc("eid"), ALU.subtract))
            cnt, tmp = R(112, 128), R(128, 144)
            J = R(144, 160)
            do(v.tensor_scalar(J, cnt, P + 0.5, None, ALU.is_gt))
            do(v.tensor_tensor(tmp, J, bc(dbase.unsqueeze(1), [P, 5, NE]), ALU.mult))
            for j in (2, 3, 4):
                do(v.scalar_tensor_tensor(J, cnt, j * P + 0.5, J, ALU.is_gt, ALU.add))
            do(v.scalar_tensor_tensor(tmp, J, 1.0 - NB * P, tmp, ALU.mult, ALU.add))
            do(v.scalar_tensor_tensor(tmp, cnt, float(NB), tmp, ALU.mult, ALU.add))
            do(v.tensor_tensor(tmp, tmp, bc(cc("eid").unsqueeze(1), [P, 5, NE]), ALU.add))
            for k, a in enumerate((64, 80)):
                do(v.tensor_tensor(cnt, R(a, a + 16), tmp, ALU.mult))
                do(v.tensor_reduce(route[:, 80 + 5 * k:85 + 5 * k].unsqueeze(2), cnt, AX.X, ALU.add))
            do(v.tensor_scalar(route[:, 80:90], route[:, 80:90], -float(NB), None, ALU.add))
            do(v.tensor_copy(ridx[:, 24:34], route[:, 80:90]))
            do(v.tensor_copy(ridx[:, 40:45], cc("tok")))
            xbt = G[:, 0, 0:XB * NE].rearrange("p (b e) -> p b e", b=XB)
            do(v.tensor_tensor(xbt, bc(offs.unsqueeze(1), [P, XB, NE]), bc(cc("xb").unsqueeze(2), [P, XB, NE]), ALU.is_le))
            do(v.tensor_reduce(route[:, 96:96 + XB].unsqueeze(2), xbt, AX.X, ALU.add))
            do(v.tensor_scalar(route[:, 96:96 + XB], route[:, 96:96 + XB], NE - 1.0, None, ALU.min))
            do(v.tensor_copy(ridx[:, 48:48 + XB], route[:, 96:96 + XB]))
            do(v.tensor_copy(n_further, offs[0:1, NE - 1:NE]), pos_ready)

            def hidden(b, it=None):
                i, v_ = b % NBUF, (b + 1 if it is None else it * NBUF + (b + 1))
                dve.wait_ge(sg_ready, v_)
                v.tensor_tensor(H3[i], H3[i], PS[:, 2, 256:512], ALU.mult).then_inc(h_ready, 1)

            def hidden_back(b, it=None):
                i, v_ = b % NBUF, (b + 1 if it is None else it * NBUF + (b + 1))
                dve.wait_ge(h_psum, v_)
                v.tensor_copy(HT3[i], PS[:, 3, 0:256]).then_inc(hT_ready, 1)

            def result(b, it=None):
                i, v_ = b % NBUF, (b + 1 if it is None else it * NBUF + (b + 1))
                dve.wait_ge(y_psum, v_)
                if b >= NBUF:
                    k = 16 * (b // NBUF)
                    dve.wait_ge(y_stored[i], k if it is None else it * 16 + k)
                v.tensor_copy(Y3[i], banks(4, 2)).then_inc(y_ready, 1)

            def step(b, it=None, first=False):
                hidden(b, it)
                if not first:
                    result(b - 1, it)
                hidden_back(b, it)

            def run_blocks(first, last):
                peel = 1 if first else 1 + NBUF
                turns = (last - first - peel) // NBUF
                for b in range(first, first + peel):
                    step(b, first=b == first)
                with dve.Fori(0, turns) as it:
                    for b in range(first + peel, first + peel + NBUF):
                        step(b, it)
                for b in range(first + peel + turns * NBUF, last):
                    step(b)
                result(last - 1)

            further = dve.value_load(n_further, min_val=0, max_val=XB)
            run_blocks(0, NE)
            with dve.If(further > 0):
                run_blocks(NE, NB)
            for c, (t0, L) in enumerate(CHUNKS):
                if c == 0:
                    dve.wait_ge(back_got, 160)
                a, b = BK[c][0][0:L, :], BK[c][1][0:L, :]
                do(v.tensor_scalar(a, a, rt[0:L, c, 61:62], None, ALU.mult))
                do(v.scalar_tensor_tensor(a, b, rt[0:L, c, 62:63], a, ALU.mult, ALU.add), moe_ready)
            dve.wait_ge(moeT_ready, 5)
            residual(merged[:], uT[:], merged[:], adaF, r_ready)
            layer_norm(1, merged[:], merged, "ln2_g", "ln2_b")


INS = ("wstream", "xT", "cT", "cst", "vec", "wgate", "segm", "wrt", "wexp", "ssd0", "conv0", "caug0", "m0", "pool0", "pool_raw")
OUTS = (("yT", (P, KT, NT)), ("ssd_p", (P, 1024)), ("conv_p", (P, 12, 3)), ("cm_p", (P, 2056)), ("mm_p", (4, 1)),
        ("pool_p", (P, 8, 15)), ("ssd_s", (2, P, 4096)), ("conv_s", (P, 12, 32)), ("cm_s", (16, P, 4, 257)),
        ("mm_s", (4, 32)), ("pool_s", (P, 8, 32)),
        ("pool_old", (NSEQ, 11 * D)))


def constants(np):
    c = np.zeros((P, NCST), np.float32)

    def put(name, a):
        s, w = CST[name]
        a = np.asarray(a, np.float32)
        c[:a.shape[0], s:s + w] = a.reshape(a.shape[0], w)

    i = np.arange(P)
    put("ident", np.eye(P))
    put("one", np.ones((P, P)))
    put("mean", np.full((P, P), 1.0 / D))
    mask = (i[:, None] <= i[None, :]) * 1.0
    put("mask", mask)
    put("mask16", mask / 16)
    q = np.arange(32)
    sm = ((q[:, None] <= q[None, :]) & (q[:, None] // TS == q[None, :] // TS)) * 1.0
    put("smask", sm)
    put("smask16", sm / 16)
    own = (q[:, None] // TS == np.arange(NSEQ)[None, :]) * 1.0
    put("tokseq", own)
    put("seqcol", np.broadcast_to(own.T.reshape(1, -1), (P, NSEQ * 32)))
    put("rank", np.broadcast_to(np.arange(4) - 4.0, (P, 4)))
    inv = np.stack([1.0 / np.minimum(np.arange(16) + 1, 2 << g) for g in range(4)])
    put("invcnt", np.broadcast_to(inv.reshape(1, -1), (P, 64)))
    put("eid", np.broadcast_to(np.arange(NE), (P, NE)))
    put("xb", np.broadcast_to(np.arange(XB), (P, XB)))
    put("tok", np.arange(P)[:, None] + P * np.arange(5)[None, :])
    put("eps", np.broadcast_to(np.array([1e-5, 1e-6]), (P, 2)))
    s = np.zeros((P, 16, P))
    for h in range(16):
        s[h, h] = 1.0
    for h in range(4):
        s[64 + h, h] = 1.0
    put("sel", s)
    seg = np.ones((P, NT), np.float32)
    seg[:, [0, 128, 256, 384] + [TP + TS * j for j in range(NSEQ)]] = 0.0
    return c, seg


def lay_out(np, t):
    f = np.float32
    w = {k: np.asarray(v) for k, v in t.items()}
    w = {k: (v[0] if k not in ("x_prompt", "x_sample", "c_prompt", "c_sample") else v) for k, v in w.items()}

    def blocks(m):
        n = m.shape[1] // 256
        return np.ascontiguousarray(m.reshape(KT, P, n, 256).transpose(2, 1, 0, 3)).reshape(n, P, 2048)

    def paired(a, b):
        return np.stack([blocks(a), blocks(b)], axis=1).reshape(-1, P, 2048)

    win = w["w_in"]
    o = np.cumsum([0, 1024, 1536, 16, 1024, 1024, 1024, 4, 4, 1024, 1024, 3072])
    sec = lambda i: win[:, o[i]:o[i + 1]]
    gl = sec(10).reshape(D, 3, D)
    pw = w["pool_w"].reshape(4, 2, P, 256).transpose(2, 0, 1, 3).reshape(1, P, 2048)
    eg, eu = w["w_e_gate"], w["w_e_up"]
    gu = np.concatenate([eg, eu], axis=2).reshape(NE, KT, P, 512).transpose(0, 2, 1, 3).reshape(NE, P, 4096)
    wexp = np.concatenate([gu, w["w_e_down"].reshape(NE, 2, P, D).transpose(0, 2, 1, 3).reshape(NE, P, 2048)], axis=2)
    stream = np.concatenate([
        blocks(w["w_ada_mix"]), blocks(sec(0)), blocks(sec(1)), paired(gl[:, 0], w["w_br_ssd"]),
        blocks(sec(3)), blocks(sec(4)), blocks(sec(5)), blocks(sec(8)), paired(gl[:, 1], w["w_br_mlstm"]),
        blocks(sec(9)), blocks(w["w_ada_ffn"]), pw, paired(gl[:, 2], w["w_br_pool"]), blocks(w["w_out"])])
    tile_rows = lambda m: np.ascontiguousarray(m.reshape(m.shape[0] // P, P, -1).transpose(1, 0, 2))
    x = np.concatenate([w["x_prompt"].reshape(TP, D), w["x_sample"].reshape(-1, D)])
    c = np.concatenate([w["c_prompt"], w["c_sample"]])
    wgate = np.zeros((D, 68), f)
    wgate[:, 0:16], wgate[:, 32:36], wgate[:, 64:68] = sec(2), sec(6), sec(7)
    vec = np.zeros((P, NVEC), f)

    def put(name, a, rows=P):
        s, n = VEC[name]
        vec[:rows, s:s + n] = a

    feat = lambda v: v.reshape(-1, P).T
    for n in ("b_ada_mix", "b_ada_ffn", "gate_b", "conv_b", "ssd_norm_w", "mlstm_norm_w", "pool_scale", "ln1_g", "ln1_b",
              "ln2_g", "ln2_b"):
        put(n, feat(w[n]))
    put("conv_w", feat(w["conv_w"].reshape(-1)))
    put("ssd_D", feat(np.broadcast_to(w["ssd_D"][:, None], (16, 64)).reshape(-1)))
    s, _ = VEC["row_bias"]
    vec[0:16, s], vec[32:36, s], vec[64:68, s] = w["ssd_dt_bias"], w["mlstm_gate_b"][:4], w["mlstm_gate_b"][4:]
    put("a_log", w["ssd_A_log"][:, None], 16)
    put("b_rt", np.broadcast_to(np.concatenate([w["b_rt_group"], w["b_rt_expert"]]), (P, 20)))
    cst, seg = constants(np)
    C0, n0 = w["state_mlstm_C"], w["state_mlstm_n"]
    ca = np.concatenate([C0.transpose(0, 1, 3, 2), n0[..., None]], axis=-1)
    ca = ca.reshape(2, 4, 4, 2, P, 257).transpose(2, 3, 0, 4, 1, 5).reshape(16, P, 4, 257)
    ssd0 = w["state_ssd"].reshape(NSEQ, 2, 8 * 64, P).transpose(1, 3, 0, 2).reshape(2, P, 4096)
    return {
        "wstream": stream, "xT": tile_rows(np.ascontiguousarray(x.T)), "cT": tile_rows(np.ascontiguousarray(c.T)),
        "cst": cst, "vec": vec, "wgate": tile_rows(wgate).reshape(P, -1), "segm": seg,
        "wrt": tile_rows(np.concatenate([w["w_rt_group"], w["w_rt_expert"]], axis=1)),
        "wexp": wexp, "ssd0": ssd0, "conv0": w["state_conv"].reshape(NSEQ, 3, 12, P).transpose(3, 2, 0, 1), "caug0": ca,
        "m0": w["state_mlstm_m"].T, "pool0": w["state_pool"].reshape(NSEQ, 15, 8, P).transpose(3, 2, 0, 1),
        "pool_raw": w["state_pool"].reshape(NSEQ, 15 * D),
    }


def kernel(**inputs):
    import numpy as np
    import concourse.bacc as bacc
    from concourse.bass_utils import run_bass_kernel_spmd as run

    nc = bacc.Bacc("TRN2", target_bir_lowering=False, num_devices=1)
    laid = lay_out(np, inputs)
    arrays, args = {}, []
    for name in INS:
        a = np.ascontiguousarray(laid[name])
        arrays["in_" + name] = a
        args.append(nc.dram_tensor("in_" + name, a.shape, mybir.dt.from_np(a.dtype), kind="ExternalInput").ap())
    for name, shape in OUTS:
        args.append(nc.dram_tensor("out_" + name, shape, F32, kind="ExternalOutput").ap())
    args.append(nc.dram_tensor("slot_tokens", (P * NB, 1), U32).ap())
    args.append(nc.dram_tensor("u2_rows", (NT, D), F32).ap())
    args.append(nc.dram_tensor("expert_rows", (P * NB, D), F32).ap())
    program(nc, *args)
    r = run(nc, [arrays], core_ids=[0]).results[0]
    g = {name: np.asarray(r["out_" + name]) for name, _ in OUTS}

    y = g["yT"].transpose(2, 1, 0).reshape(NT, D)
    ssd_p = g["ssd_p"].T.reshape(1, 1, 16, 64, P)
    ssd_s = g["ssd_s"].reshape(2, P, NSEQ, 512).transpose(2, 0, 3, 1).reshape(1, NSEQ, 16, 64, P)
    conv_p = g["conv_p"].transpose(2, 1, 0).reshape(1, 1, 3, 1536)
    conv_s = g["conv_s"].transpose(2, 1, 0).reshape(1, NSEQ, TS, 1536)[:, :, 1:]
    cp = g["cm_p"].reshape(P, 4, 2, 257).transpose(1, 3, 2, 0).reshape(1, 1, 4, 257, 256)
    cs = g["cm_s"].reshape(4, 2, 2, P, 4, 257).transpose(2, 4, 0, 5, 1, 3).reshape(1, NSEQ, 4, 257, 256)
    pool_p = g["pool_p"].transpose(2, 1, 0).reshape(1, 1, 15, D)
    up_s = g["pool_s"].transpose(2, 1, 0).reshape(1, NSEQ, TS, D)
    pool_s = np.concatenate([g["pool_old"].reshape(1, NSEQ, 11, D), up_s], axis=2)
    out = (y[:TP].reshape(1, TP, D), y[TP:].reshape(NSEQ, TS, D),
           ssd_p, conv_p, cp[:, :, :, :256], cp[:, :, :, 256], g["mm_p"].reshape(1, 1, 4), pool_p,
           ssd_s, conv_s, cs[:, :, :, :256], cs[:, :, :, 256], g["mm_s"][:, TS - 1::TS].T.reshape(1, NSEQ, 4), pool_s)
    return tuple(np.ascontiguousarray(a) for a in out)
```

```python
from contextlib import ExitStack

import concourse.bass as bass
from concourse import mybir

F32 = mybir.dt.float32
U32 = mybir.dt.uint32
ALU = mybir.AluOpType
ACT = mybir.ActivationFunctionType
AX = mybir.AxisListType

P = 128
D = 1024
KT = D // P
TP, NSEQ, TS = 512, 8, 4
NT = TP + NSEQ * TS
HALF = NT // 2
RING = 4
CHUNKS = [(c * P, P) for c in range(TP // P)] + [(TP, NSEQ * TS)]
NSEG = TP // P + NSEQ
STEPS = [(c, g) for c in range(TP // P) for g in range(2)]
NS = len(STEPS)
ALPHA = 2 ** 0.25
BIG = 3.0e38

PHASES = {}


def plan():
    b = g = a = 0
    for name, nb, ng, na in (("ada_mix", 12, 24, 0), ("z", 4, 8, 8), ("xbc", 6, 12, 12), ("merge0", 8, 16, 16),
                             ("qkvo", 16, 32, 32), ("merge1", 8, 16, 16), ("up", 4, 8, 8), ("ada_ffn", 12, 24, 0),
                             ("poolw", 1, 8, 8), ("merge2", 8, 16, 16), ("out", 4, 8, 8),
                             ("end", 0, 0, 0)):
        PHASES[name] = (b, g, a)
        b, g, a = b + nb, g + ng, a + na
    return b


NBLOCKS = plan()

NE = 16
XB = (2 * NT - 1) // P
NB = NE + XB
NBUF = 3

CST = {}
_at = 0
for _n, _w in (("ident", P), ("one", P), ("mean", P), ("mask", P), ("mask16", P), ("smask", 32), ("smask16", 32),
               ("tokseq", NSEQ), ("seqcol", NSEQ * 32), ("rank", 4), ("invcnt", 64), ("eps", 2), ("eid", NE), ("xb", XB), ("tok", 5),
               ("sel", 16 * P)):
    CST[_n] = (_at, _w)
    _at += _w
NCST = _at

VEC = {}
_at = 0
for _n, _w in (("b_ada_mix", 24), ("b_ada_ffn", 24), ("gate_b", 24), ("conv_b", 12), ("conv_w", 48), ("ssd_norm_w", 8),
               ("mlstm_norm_w", 8), ("pool_scale", 8), ("ln1_g", 8), ("ln1_b", 8), ("ln2_g", 8), ("ln2_b", 8),
               ("ssd_D", 8), ("row_bias", 1), ("a_log", 1), ("b_rt", 20)):
    VEC[_n] = (_at, _w)
    _at += _w
NVEC = _at


def program(nc, wstream, xT, cT, cst, vec, wgate, segm, wrt, wexp, ssd0, conv0, caug0, m0, pool0, pool_raw,
            yT, ssd_p, conv_p, cm_p, mm_p, pool_p, ssd_s, conv_s, cm_s, mm_s, pool_s, pool_old,
            slots, u2rows, yrows):
    with ExitStack() as ctx:
        def sb(name, shape):
            return ctx.enter_context(nc.sbuf_tensor(name, shape, F32))

        def sem(name):
            return ctx.enter_context(nc.semaphore(name))

        C = sb("C", [P, NCST])
        V = sb("V", [P, NVEC])
        cTs = sb("cTs", [P, KT, 9])
        wr = sb("wr", [P, KT, 20])
        uT = sb("uT", [P, KT, NT])
        ring = sb("ring", [P, RING, 2048])
        proj = sb("proj", [P, 32, NT])
        merged = sb("merged", [P, KT, NT])
        G = sb("G", [P, 7, NT])
        tg = sb("tg", [P, 5, 80])
        exl = sb("exl", [P, 16, NSEG])
        wpb = sb("wpb", [P, 4, NSEG])
        adaM = sb("adaM", [P, 24, 9])
        adaF = sb("adaF", [P, 24, 9])
        gs = sb("gs", [P, 2, NT])
        mp = sb("mp", [P, NSEG])
        rt = sb("rt", [P, 5, 160])
        route = sb("route", [P, 160])
        ridx = ctx.enter_context(nc.sbuf_tensor("ridx", [P, 64], U32))
        work = sb("work", [P, 8256])
        PS = ctx.enter_context(nc.psum_tensor("PS", [P, 8, 512], F32))

        def cc(name, rows=P):
            a, w = CST[name]
            return C[0:rows, a:a + w]

        def vv(name, i, n=1):
            a, _ = VEC[name]
            return V[:, a + i:a + i + n]

        ident, one, mean = cc("ident"), cc("one"), cc("mean")
        sel = cc("sel").rearrange("p (h m) -> p h m", h=16)
        seqcol = cc("seqcol").rearrange("p (j t) -> p j t", j=NSEQ)
        wg = gs[:, 0, :].rearrange("p (k m) -> p k m", k=KT)
        seg0 = gs[:, 1, :]

        def carve(sizes):
            out, at = [], 0
            for n in sizes:
                out.append(work[:, at:at + n])
                at += n
            return out

        xdt, xw, Es, cbm, Bt, ytok, sT, CTm = carve([1024, 1024, 2048, 256, 256, 1024, 1024, 512])
        s0g = [proj[:, 20:28, :].rearrange("p a t -> p (a t)")[:, 0:4096],
               merged[:].rearrange("p a t -> p (a t)")[:, 0:4096]]
        Btm = proj[:, 28:32, :].rearrange("p a t -> p (a t)")[:, 0:2048]
        cpad = proj[:, 20:28, :].rearrange("p a t -> p (a t)")
        hist = cpad[:, 0:288].rearrange("p (i j k) -> p i j k", i=12, j=NSEQ)
        sx = cpad[:, 512:512 + 12 * 56].rearrange("p (i j k) -> p i j k", i=12, j=NSEQ)
        cin = cpad[:, 1536:1536 + 2 * NT].rearrange("p (b t) -> p b t", b=2)
        tail = cpad[:, 2700:2700 + 12 * 35].rearrange("p (i t) -> p i t", i=12)
        no_rows = Btm[:, 0:D]
        vaug_, kw, Em, qs, CT_, kwm_, caug_ = carve([1028, 1024, 512, 1024, 2056, 512, 2056])
        qm_ = route[:, 0:128]
        vaug = vaug_.rearrange("p (h v) -> p h v", h=4)
        CT = CT_.rearrange("p (h k v) -> p h k v", h=4, k=2)
        caug = caug_.rearrange("p (b j v) -> p b j v", b=2, j=4)
        CB = [caug[:, 0], caug[:, 1]] + [proj[:, 8:24, :].rearrange("p a t -> p (a t)")[:, i * 1028:(i + 1) * 1028]
                                         .rearrange("p (j v) -> p j v", j=4) for i in range(8)]
        NCB = len(CB)
        hbuf = gs[:].rearrange("p a t -> p (a t)")[:, 0:1024]
        qmask = [qm_, rt[:, 0, 0:128]]
        scores = [kwm_[:, 0:256], kwm_[:, 256:512]]
        kwmask = [kwm_, hbuf[:, 0:512]]
        hstat = gs[:].rearrange("p a t -> p (a t)")[:, 1024:1088]

        pf = proj[:].rearrange("p a t -> p (a t)")
        at = 8 * NT
        padP, padS = [], []
        for _ in range(2):
            padP.append(pf[:, at:at + 8 * 527].rearrange("p (i t) -> p i t", i=8))
            at += 8 * 527
            padS.append(pf[:, at:at + 8 * 152].rearrange("p (i j t) -> p i j t", i=8, j=NSEQ))
            at += 8 * 152
        dpool = work[:, 0:4352].rearrange("p (i t) -> p i t", i=8)
        pool_hist_dst = padS[0][:, :, :, 0:15]

        rg = ring[:].rearrange("p r f -> p (r f)")
        E3 = [rg[:, 0:6144], pf[:, 0:6144], pf[:, 6144:12288]]
        Y3 = [pf[:, 12288 + i * 1024:12288 + (i + 1) * 1024] for i in range(3)]
        X3 = [work[:, i * 1024:(i + 1) * 1024] for i in range(3)]
        XT3 = [work[:, (3 + i) * 1024:(4 + i) * 1024].rearrange("p (k s) -> p k s", k=KT) for i in range(3)]
        H3 = [work[:, 6144 + i * 256:6400 + i * 256] for i in range(3)]
        HT3 = [work[:, 6912 + i * 256:7168 + i * 256] for i in range(3)]
        arow = work[0:9, 4352:4352 + 3 * D]
        u2r = [work[:, i * 1024:(i + 1) * 1024] for i in range(5)]
        BK = [[pf[:, (2 * c + k) * 1024:(2 * c + k + 1) * 1024] for k in range(2)] for c in range(5)]
        zeros = ridx[:, 0:NB]
        n_further = ridx[0:1, 48 + XB:49 + XB]

        def acc(p):
            return PS[:, 2 * p:2 * p + 2, 0:HALF]

        def banks(b, n):
            return PS[:, b:b + n, :].rearrange("p b f -> p (b f)")

        def halves(t):
            return t.rearrange("p (h t) -> p h t", h=2)

        w_loaded = [sem(f"w_loaded{i}") for i in range(RING)]
        group_done = sem("group_done")
        acc_free = [sem("acc_free0"), sem("acc_free1")]
        small_loaded, x_loaded, rows_in_loaded = sem("small_loaded"), sem("x_loaded"), sem("rows_in_loaded")
        dve_step, act_step = sem("dve_step"), sem("act_step")
        ada_rows, ada_psum = sem("ada_rows"), sem("ada_psum")
        ada_ready, u_ready, gates_psum, xrow_ready, rabs_ready = (
            sem("ada_ready"), sem("u_ready"), sem("gates_psum"), sem("xrow_ready"), sem("rabs_ready"))
        rexp_ready, rw_ready, rln_ready, cumd_ready, rowexp_ready, rows_ready = (
            sem("rexp_ready"), sem("rw_ready"), sem("rln_ready"), sem("cumd_ready"), sem("rowexp_ready"),
            sem("rows_ready"))
        tok_psum, tok_ready, m_ready = sem("tok_psum"), sem("tok_ready"), sem("m_ready")
        conv_x, conv_tail, conv_in_loaded, conv_pre, conv_silu, z_silu = (
            sem(n) for n in ("conv_x", "conv_tail", "conv_in_loaded", "conv_pre", "conv_silu", "z_silu"))
        ssd_xb, ssd_bc, ssd_bt, ssd_seg, ssd_exp, ssd_w, ssd_yp, ssd_ytok, ssd_st, ssd_stdone, ssd_yTp, ssd_out = (
            sem(n) for n in ("ssd_xb", "ssd_bc", "ssd_bt", "ssd_seg", "ssd_exp", "ssd_w", "ssd_yp", "ssd_ytok",
                             "ssd_st", "ssd_stdone", "ssd_yTp", "ssd_out"))
        ssd_masks, s0_loaded, ssd_upd, ssd_updone = sem("ssd_masks"), sem("s0_loaded"), sem("ssd_upd"), sem("ssd_updone")
        sq_ready, ssq_psum, sd_ready, br_ready, gate_ready, gate_used = (
            sem("sq_ready"), sem("ssq_psum"), sem("sd_ready"), sem("br_ready"), sem("gate_ready"), sem("gate_used"))
        evac_qk, og_ready = sem("evac_qk"), sem("og_ready")
        ml_kv, ml_sc, ml_va, ml_d, ml_exp, ml_w, ml_qs, ml_num, ml_h, ml_sd, ml_hn, ml_hT, ml_out = (
            sem(n) for n in ("ml_kv", "ml_sc", "ml_va", "ml_d", "ml_exp", "ml_w", "ml_qs", "ml_num", "ml_h",
                             "ml_sd", "ml_hn", "ml_hT", "ml_out"))
        ml_st, ml_stdone, ml_qm, ml_upd, ml_updone = (
            sem(n) for n in ("ml_st", "ml_stdone", "ml_qm", "ml_upd", "ml_updone"))
        caug_moved = [sem(f"caug_moved{i}") for i in range(NCB)]
        evac_up, pool_loaded, pool_d, evac_pool, xr_loaded, r_ready = (
            sem(n) for n in ("evac_up", "pool_loaded", "pool_d", "evac_pool", "xr_loaded", "r_ready"))
        ln_mu, ln_cen, ln_sq, ln_var, ln_sd, ln_norm, ln_done = (
            sem(n) for n in ("ln_mu", "ln_cen", "ln_sq", "ln_var", "ln_sd", "ln_norm", "ln_done"))
        u2_ready, rt_psum, rt_d, rt_e, rt_dd, rt_e2 = (
            sem(n) for n in ("u2_ready", "rt_psum", "rt_d", "rt_e", "rt_dd", "rt_e2"))
        ohs_ready, cnt_psum, cnt_used, pos_ready, list_zeroed, list_written, list_loaded, u2p, u2r_ready, u2_stored = (
            sem(n) for n in ("ohs_ready", "cnt_psum", "cnt_used", "pos_ready", "list_zeroed", "list_written", "list_loaded", "u2p",
                             "u2r_ready", "u2_stored"))
        e_loaded = [sem(f"e_loaded{i}") for i in range(NBUF)]
        x_got = [sem(f"x_got{i}") for i in range(NBUF)]
        y_stored = [sem(f"y_stored{i}") for i in range(NBUF)]
        xt_psum, xt_ready, gu_psum, sg_ready, h_ready, h_psum, hT_ready, y_psum, y_ready = (
            sem(n) for n in ("xt_psum", "xt_ready", "gu_psum", "sg_ready", "h_ready", "h_psum", "hT_ready", "y_psum",
                             "y_ready"))
        back_got = [sem(f"back_got{c}") for c in range(len(CHUNKS))]
        moe_ready, moeT_psum, moeT_ready, zero_ready, r2_ready = (
            sem(n) for n in ("moe_ready", "moeT_psum", "moeT_ready", "zero_ready", "r2_ready"))
        rows_zeroed, cT_loaded, sel_loaded = sem("rows_zeroed"), sem("cT_loaded"), sem("sel_loaded")
        y_out, out_tile, rtT_psum, rtT_ready = sem("y_out"), sem("out_tile"), sem("rtT_psum"), sem("rtT_ready")
        stored, pool_stored = sem("stored"), sem("pool_stored")

        block = ctx.enter_context(nc.Block())

        def groups_before(b):
            pw = PHASES["poolw"][0]
            return 2 * (b + 1) + (6 if b >= pw else 0)

        @block.sync
        def _(sp):
            sp.dma_start(cTs[:], cT).then_inc(cT_loaded, 16)
            for i in range(RING):
                sp.dma_start(ring[:, i, :], wstream[i]).then_inc(w_loaded[i], 16)
                if i == 0:
                    sp.dma_start(C[:, 0:CST["sel"][0]], cst[:, 0:CST["sel"][0]]).then_inc(small_loaded, 16)
                    sp.dma_start(V[:], vec).then_inc(small_loaded, 16)

            def stream(first, last):
                base = groups_before(first - RING)
                with sp.Fori(0, (last - first) // RING) as it:
                    for i in range(RING):
                        sp.wait_ge(group_done, it * (2 * RING) + base + 2 * i)
                        sp.dma_start(ring[:, (first + i) % RING, :],
                                     wstream[bass.ds(it * RING + (first + i), 1)].rearrange("o p c -> (o p) c")
                                     ).then_inc(w_loaded[(first + i) % RING], 16)

            pw = PHASES["poolw"][0]
            turns = (pw - RING) // RING
            stream(RING, RING + turns * RING)
            b = RING + turns * RING
            while b < pw + RING:
                sp.wait_ge(group_done, groups_before(b - RING))
                sp.dma_start(ring[:, b % RING, :], wstream[b]).then_inc(w_loaded[b % RING], 16)
                b += 1
            turns = (NBLOCKS - b) // RING
            stream(b, b + turns * RING)
            b += turns * RING
            while b < NBLOCKS:
                sp.wait_ge(group_done, groups_before(b - RING))
                sp.dma_start(ring[:, b % RING, :], wstream[b]).then_inc(w_loaded[b % RING], 16)
                b += 1

            sp.wait_ge(group_done, PHASES["end"][1])

            def expert_block(b, it=None):
                i = b % NBUF
                if b < NE:
                    src = wexp[b] if it is None else wexp[bass.ds(it * NBUF + b, 1)].rearrange("o p c -> (o p) c")
                else:
                    e = sp.value_load(ridx[0:1, 48 + b - NE:49 + b - NE], min_val=0, max_val=NE - 1)
                    src = wexp[bass.ds(e, 1)].rearrange("o p c -> (o p) c")
                sp.dma_start(E3[i], src).then_inc(e_loaded[i], 16)

            def result_block(b, it=None):
                v = b + 1
                sp.wait_ge(y_ready, v if it is None else it * NBUF + v)
                dst = yrows.rearrange("(p b) d -> p b d", b=NB)
                dst = dst[:, b, :] if it is None else dst[:, bass.ds(it * NBUF + b, 1), :].rearrange("p o d -> p (o d)")
                sp.dma_start(dst, Y3[b % NBUF]).then_inc(y_stored[b % NBUF], 16)

            expert_block(0)
            sp.wait_ge(ln_done, KT)
            for b in range(1, NBUF):
                expert_block(b)
            turns = (NE - NBUF) // NBUF
            with sp.Fori(0, turns) as it:
                for b in range(NBUF, 2 * NBUF):
                    sp.wait_ge(y_psum, it * NBUF + (b - NBUF + 1))
                    expert_block(b, it)
                    result_block(b - NBUF, it)
            for b in range((turns + 1) * NBUF, NE):
                sp.wait_ge(y_psum, b - NBUF + 1)
                expert_block(b)
                result_block(b - NBUF)
            for b in range(NE - NBUF, NE):
                result_block(b)
            sp.wait_ge(pos_ready, 1)
            further = sp.value_load(n_further, min_val=0, max_val=XB)
            with sp.If(further > 0):
                for b in range(NE, NB):
                    if b >= NE + NBUF:
                        sp.wait_ge(y_psum, b - NBUF + 1)
                    expert_block(b)
                    if b >= NE + NBUF:
                        result_block(b - NBUF)
                for b in range(NB - NBUF, NB):
                    result_block(b)
            for i in range(0, KT, 2):
                sp.wait_ge(ln_done, KT + i + 2)
                sp.dma_start(yT[:, i:i + 2, :], merged[:, i:i + 2, :]).then_inc(y_out, 16)
            sp.wait_ge(y_out, 16 * KT // 2)

        @block.gpsimd
        def _(pool):
            n_stored = [0]

            def store(dst, src):
                pool.dma_start(dst, src).then_inc(stored, 16)
                n_stored[0] += 16

            pool.dma_start(uT[:], xT).then_inc(x_loaded, 16)
            pool.wait_ge(zero_ready, 1)
            pool.dma_start(slots.rearrange("(p b) o -> p (b o)", b=NB), zeros).then_inc(list_zeroed, 16)
            pool.dma_start(gs[:, 0, :], wgate).then_inc(rows_in_loaded, 16)
            pool.dma_start(seg0, segm).then_inc(rows_in_loaded, 16)
            pool.dma_start(wr[:], wrt).then_inc(rows_in_loaded, 16)
            pool.dma_start(mp[64:68, 4:NSEG], m0).then_inc(rows_in_loaded, 16)
            pool.dma_start(cpad[:, 0:288].rearrange("p (i j k) -> p i j k", i=12, j=NSEQ), conv0).then_inc(conv_in_loaded, 16)
            pool.wait_ge(u_ready, 1)
            pool.dma_start(C[:, CST["sel"][0]:NCST], cst[:, CST["sel"][0]:NCST]).then_inc(sel_loaded, 16)
            pool.dma_start(yrows.rearrange("(p b) d -> p b d", b=NB)[:, NE:NB, :],
                           no_rows.unsqueeze(1).to_broadcast([P, XB, D])).then_inc(rows_zeroed, 16)
            store(pool_old, pool_raw[:, TS * D:15 * D])
            pool.wait_ge(m_ready, 1)
            store(mm_p, G[64:68, 4, 511:512])
            store(mm_s, G[64:68, 4, 512:NT])
            pool.wait_ge(conv_tail, 12)
            store(conv_p, tail[:, :, 0:3])
            store(conv_s, tail[:, :, 3:35])
            pool.wait_ge(stored, n_stored[0])
            pool.wait_ge(conv_pre, 12)
            pool.dma_start(s0g[0], ssd0[0]).then_inc(s0_loaded, 16)
            pool.dma_start(s0g[1], ssd0[1]).then_inc(s0_loaded, 16)
            pool.wait_ge(ssd_stdone, NS)
            store(ssd_p, sT)
            pool.wait_ge(ssd_updone, NSEQ)
            store(ssd_s[0], s0g[0])
            store(ssd_s[1], s0g[1])
            ssd_stores = n_stored[0]
            pool.wait_ge(stored, ssd_stores)
            pool.sem_inc(ssd_stdone, 1)
            for i in range(NCB):
                if i == 0:
                    pool.wait_ge(ml_stdone, 1)
                if i == 2:
                    pool.wait_ge(ml_sc, NS + 1)
                pool.dma_start(CB[i], caug0[i]).then_inc(caug_moved[i], 16)
            store(cm_p, CT_)
            for i in range(16):
                pool.wait_ge(ml_updone, i + 1)
                pool.dma_start(cm_s[i], CB[i % NCB]).then_inc(caug_moved[i % NCB], 16)
                if i >= 2 and i - 2 + NCB < 16:
                    pool.wait_ge(caug_moved[i - 2], 32)
                    pool.dma_start(CB[i - 2], caug0[i - 2 + NCB]).then_inc(caug_moved[i - 2], 16)
            for i in range(NCB):
                pool.wait_ge(caug_moved[i], 32 * len(range(i, 16, NCB)))
            pool.wait_ge(stored, n_stored[0])
            pool.sem_inc(ml_stdone, 1)
            pool.dma_start(pool_hist_dst, pool0).then_inc(pool_loaded, 16)
            pool.wait_ge(evac_up, 8)
            store(pool_p, proj[:, 0:8, 497:512])
            store(pool_s, proj[:, 0:8, 512:NT])
            pool.wait_ge(stored, n_stored[0])
            pool.sem_inc(pool_stored, 1)
            pool.wait_ge(gate_used, 2 + 24)
            pool.dma_start(proj[:, 8:16, :], xT).then_inc(xr_loaded, 16)
            for c, (t0, L) in enumerate(CHUNKS):
                pool.wait_ge(u2r_ready, c + 1)
                pool.dma_start(u2rows[t0:t0 + L, :], u2r[c][0:L, :]).then_inc(u2_stored, 16)
            pool.wait_ge(pos_ready, 1)
            pool.wait_ge(list_zeroed, 16)
            for c, (t0, L) in enumerate(CHUNKS):
                for k in range(2):
                    pool.indirect_dma_start(slots, bass.IndirectOffsetOnAxis(ap=ridx[0:L, 24 + 5 * k + c:25 + 5 * k + c], axis=0),
                                            ridx[0:L, 40 + c:41 + c], None).then_inc(list_written, 16)
            pool.wait_ge(list_written, 16 * 10)
            pool.dma_start(ridx[:, 0:NB], slots.rearrange("(p b) o -> p (b o)", b=NB)).then_inc(list_loaded, 16)
            pool.wait_ge(list_loaded, 16)
            pool.wait_ge(u2_stored, 16 * 5)

            def rows_block(b):
                if b >= NBUF:
                    pool.wait_ge(xt_psum, b - NBUF + 1)
                pool.indirect_dma_start(X3[b % NBUF], None, u2rows, bass.IndirectOffsetOnAxis(ap=ridx[:, b:b + 1], axis=0)
                                        ).then_inc(x_got[b % NBUF], 16)

            for b in range(NE):
                rows_block(b)
            further = pool.value_load(n_further, min_val=0, max_val=XB)
            for i in range(NBUF):
                pool.wait_ge(y_stored[i], 16 * len(range(i, NE, NBUF)))
            with pool.If(further > 0):
                for b in range(NE, NB):
                    rows_block(b)
                for i in range(NBUF):
                    pool.wait_ge(y_stored[i], 16 * len(range(i, NB, NBUF)))
            for c, (t0, L) in enumerate(CHUNKS):
                for k in range(2):
                    pool.indirect_dma_start(BK[c][k][0:L, :], None, yrows,
                                            bass.IndirectOffsetOnAxis(ap=ridx[0:L, 24 + 5 * k + c:25 + 5 * k + c], axis=0)
                                            ).then_inc(back_got[c], 16)
            pool.wait_ge(stored, n_stored[0])

        @block.tensor
        def _(pe):
            mm = nc.tensor.matmul

            def wblk(slot, kt, mi):
                return ring[:, slot, kt * 256 + mi * P:kt * 256 + mi * P + P]

            def wait_block(b, it=None):
                v = 16 * (b // RING + 1)
                pe.wait_ge(w_loaded[b % RING], v if it is None else it * 16 + v)

            def dense_block(b, a, rhs, it=None):
                wait_block(b, it)
                for mi in range(2):
                    v = a // 2 + 1
                    pe.wait_ge(acc_free[mi], v if it is None else it * RING + v)
                    for kt in range(KT):
                        for h in range(2):
                            last = mm(acc(mi)[:, h, :], wblk(b % RING, kt, mi), rhs[:, kt, h * HALF:(h + 1) * HALF],
                                      start=kt == 0, stop=kt == KT - 1)
                    last.then_inc(group_done, 1)

            def dense(name, nb, rhs):
                b0, _, a0 = PHASES[name]
                if nb >= 2 * RING:
                    with pe.Fori(0, nb // RING) as it:
                        for i in range(RING):
                            dense_block(b0 + i, a0 + 2 * i, rhs, it)
                    rest = range(nb // RING * RING, nb)
                else:
                    rest = range(nb)
                for i in rest:
                    dense_block(b0 + i, a0 + 2 * i, rhs)

            def ada(name, n):
                b0 = PHASES[name][0]

                def turn(i):
                    pe.wait_ge(ada_rows, 12 * n + i + 1)
                    pe.wait_ge(small_loaded, 32)
                    for m in range(2 * i, 2 * i + 2):
                        last = nc.tensor.transpose(PS[:, 7, m * 9:m * 9 + 9], arow[:, m * P:(m + 1) * P], ident[0:9, 0:9])
                    last.then_inc(ada_psum, 1)

                for i in range(12):
                    wait_block(b0 + i)
                    if i >= 2:
                        pe.wait_ge(ada_rows, 12 * n + i - 1)
                    for kt in range(KT):
                        last = mm(PS[0:9, 4 + i % 2, 0:256], cTs[:, kt, :], ring[:, (b0 + i) % RING, kt * 256:(kt + 1) * 256],
                                  start=kt == 0, stop=kt == KT - 1)
                    last.then_inc(group_done, 2)
                    if i:
                        turn(i - 1)
                turn(11)

            pe.wait_ge(cT_loaded, 16)
            ada("ada_mix", 0)

            pe.wait_ge(u_ready, 1)
            pe.wait_ge(rows_in_loaded, 64)
            for h in range(2):
                for kt in range(KT):
                    last = mm(PS[0:68, 4 + h, 0:HALF], wg[:, kt, :], uT[:, kt, h * HALF:(h + 1) * HALF],
                              start=kt == 0, stop=kt == KT - 1)
            last.then_inc(gates_psum, 1)

            dense("z", 4, uT)
            for i in range(4):
                dense_block(PHASES["xbc"][0] + i, PHASES["xbc"][2] + 2 * i, uT)

            pe.wait_ge(rows_ready, 1)
            for c, (t0, L) in enumerate(CHUNKS):
                for i, (g, r0, n) in enumerate(((6, 0, 16), (2, 0, 16), (3, 0, 16), (4, 0, 16),
                                                (1, 64, 4), (5, 64, 4), (0, 64, 4), (6, 64, 4))):
                    bank, col = (6, c * 64 + 16 * i) if i < 4 else (7, c * 16 + 4 * (i - 4))
                    nc.tensor.transpose(PS[0:L, bank, col:col + n], G[r0:r0 + n, g, t0:t0 + L],
                                        ident[r0:r0 + n, r0:r0 + n])
            mm(PS[:, 6, 320:512], one[0:16, :], G[0:16, 1, 0:192], start=True, stop=True)
            mm(PS[:, 7, 80:128], one[64:68, :], G[64:68, 2, 0:48], start=True, stop=True).then_inc(tok_psum, 1)

            for i in range(4, 6):
                dense_block(PHASES["xbc"][0] + i, PHASES["xbc"][2] + 2 * i, uT)
            pe.wait_ge(conv_silu, 12)
            for s in acc_free:
                pe.wait_ge(s, PHASES["merge0"][2] // 2 + 1)
            pe.wait_ge(tok_ready, 3)

            def keep_warm(bank, n):
                for _ in range(n):
                    mm(PS[:, bank, :], ident, C[:, 0:512], start=True, stop=True)

            def ssd_front(s):
                c, g = STEPS[s]
                cols = slice(c * P, c * P + P)
                if s >= 2:
                    pe.wait_ge(ssd_ytok, s - 1)
                    pe.wait_ge(ssd_stdone, s - 1)
                    pe.wait_ge(ssd_out, s - 1)
                for i in range(4):
                    nc.tensor.transpose(PS[:, 4 + g, i * P:(i + 1) * P], proj[:, 4 * g + i, cols], ident)
                nc.tensor.transpose(PS[:, 6 + g, 0:P], proj[:, 8 + g, cols], ident)
                mm(PS[:, 6 + g, 256:256 + P], proj[:, 8 + g, cols], proj[:, 10 + g, cols],
                   start=True, stop=True).then_inc(ssd_xb, 1)
                for h in range(8):
                    last = mm(banks(2 * g, 2)[:, h * P:(h + 1) * P], sel[0:16, 8 * g + h, :], G[0:16, 2, cols],
                              start=True, stop=True)
                last.then_inc(ssd_bc, 1)

            def ssd_mid(s):
                c, g = STEPS[s]
                cols = slice(c * P, c * P + P)
                keep_warm(2 * (1 - g) + 1, 2)
                pe.wait_ge(ssd_w, s + 1)
                for h in range(8 * g, 8 * g + 8):
                    last = mm(PS[:, 4 + g, (h - 8 * g) * 64:(h - 8 * g + 1) * 64], Es[:, h * P:(h + 1) * P],
                              xdt[:, h * 64:(h + 1) * 64], start=True, stop=True)
                if c:
                    last = mm(PS[:, 2 * g + 1, :], proj[:, 10 + g, cols], sT[:, g * 512:(g + 1) * 512],
                              start=True, stop=True)
                last.then_inc(ssd_yp, 1)
                pe.wait_ge(ssd_bt, s + 1)
                mm(PS[:, 6 + g, :], Bt[:, g * P:(g + 1) * P], xw[:, g * 512:(g + 1) * 512],
                   start=True, stop=True).then_inc(ssd_st, 1)

            def ssd_back(s):
                _, g = STEPS[s]
                keep_warm(2 * g, 1)
                pe.wait_ge(ssd_ytok, s + 1)
                for i in range(4):
                    last = nc.tensor.transpose(PS[:, 2 * g, i * P:(i + 1) * P],
                                               ytok[:, (4 * g + i) * P:(4 * g + i + 1) * P], ident)
                last.then_inc(ssd_yTp, 1)

            pe.wait_ge(sel_loaded, 16)
            ssd_front(0)
            for s in range(NS):
                ssd_mid(s)
                if s + 1 < NS:
                    ssd_front(s + 1)
                ssd_back(s)

            L, cols = NT - TP, slice(TP, NT)
            pe.wait_ge(ssd_ytok, NS)
            pe.wait_ge(ssd_stdone, NS)
            for i in range(8):
                nc.tensor.transpose(banks(4, 2)[0:L, i * P:(i + 1) * P], proj[:, i, cols], ident)
            for g in range(2):
                nc.tensor.transpose(PS[0:L, 6, g * P:(g + 1) * P], proj[:, 8 + g, cols], ident)
            for g in range(2):
                last = mm(PS[0:L, 6, 256 + g * P:256 + g * P + L], proj[:, 8 + g, cols], proj[:, 10 + g, cols],
                          start=True, stop=True)
            last.then_inc(ssd_xb, 1)
            pe.wait_ge(ssd_out, NS)
            for h in range(16):
                last = mm(banks(0, 4)[0:L, h * P:h * P + L], sel[0:16, h, 0:L], G[0:16, 2, cols], start=True, stop=True)
            last.then_inc(ssd_bc, 1)
            keep_warm(7, 3)
            pe.wait_ge(ssd_w, NS + 1)
            for h in range(16):
                mm(banks(4, 2)[0:L, h * 64:(h + 1) * 64], Es[0:L, h * P:h * P + L], xdt[0:L, h * 64:(h + 1) * 64],
                   start=True, stop=True)
            pe.wait_ge(ssd_masks, 1)
            pe.wait_ge(s0_loaded, 32)
            for g in range(2):
                for j in range(NSEQ):
                    last = mm(PS[0:L, 2 + g, :], CTm[:, (g * NSEQ + j) * 32:(g * NSEQ + j) * 32 + 32],
                              s0g[g][:, j * 512:(j + 1) * 512], start=j == 0, stop=j == NSEQ - 1)
            last.then_inc(ssd_yp, 1)
            pe.wait_ge(ssd_ytok, NS + 1)
            for i in range(8):
                last = nc.tensor.transpose(banks(0, 2)[:, i * P:i * P + L], ytok[0:L, i * P:(i + 1) * P],
                                           ident[0:L, 0:L])
            last.then_inc(ssd_yTp, 1)

            def sum_tiles(bank, weights, src, done):
                for h in range(2):
                    for kt in range(KT):
                        last = mm(PS[:, bank + h, 0:HALF], weights, src[:, kt, h * HALF:(h + 1) * HALF],
                                  start=kt == 0, stop=kt == KT - 1)
                last.then_inc(done, 1)

            for j in range(NSEQ):
                b = 4 + 2 * (j % 2)
                if j == 2:
                    pe.wait_ge(sq_ready, 1)
                    sum_tiles(0, mean, proj[:, 0:8, :], ssq_psum)
                if j >= 2:
                    pe.wait_ge(ssd_updone, j - 1)
                for g in range(2):
                    last = mm(PS[:, b + g, :], Btm[0:32, j * 256 + g * P:j * 256 + (g + 1) * P],
                              xw[0:32, g * 512:(g + 1) * 512], start=True, stop=True)
                last.then_inc(ssd_upd, 1)

            def merge(name, y, y_ready_, n):
                b0, _, a0 = PHASES[name]
                with pe.Fori(0, 2) as it:
                    for i in range(RING):
                        if i == 1:
                            pe.wait_ge(y_ready_, n)
                        dense_block(b0 + i, a0 + 2 * i, uT if i % 2 == 0 else y, it)

            pe.wait_ge(sd_ready, 1)
            merge("merge0", proj[:, 12:20, :], br_ready, 1)
            dense("qkvo", 16, uT)

            for s in acc_free:
                pe.wait_ge(s, PHASES["merge1"][2] // 2 + 1)
            pe.wait_ge(evac_qk, 24)

            def ml_front(s):
                c, g = STEPS[s]
                b, cols = 4 * g, slice(c * P, c * P + P)
                if s >= 2:
                    pe.wait_ge(ml_h, s - 1)
                    pe.wait_ge(ml_out, s - 1)
                    pe.wait_ge(ml_stdone, s - 1)
                for i in range(4):
                    nc.tensor.transpose(PS[:, b, i * P:(i + 1) * P], proj[:, 8 + 4 * g + i, cols], ident)
                for i in range(4):
                    last = nc.tensor.transpose(PS[:, b + 1, i * P:(i + 1) * P], proj[:, 16 + 4 * g + i, cols], ident)
                last.then_inc(ml_kv, 1)
                for j in range(2):
                    for k in range(2):
                        t = 2 * (2 * g + j) + k
                        mm(PS[:, b + 2, j * P:(j + 1) * P], proj[:, 8 + t, cols], proj[:, t, cols], start=k == 0, stop=k == 1)
                for r in range(2):
                    for j in range(2):
                        last = mm(PS[:, b + 3, (2 * r + j) * P:(2 * r + j + 1) * P], sel[64:68, 2 * g + j, :],
                                  G[64:68, 3 + 2 * r, cols], start=True, stop=True)
                last.then_inc(ml_sc, 1)

            def ml_mid(s):
                c, g = STEPS[s]
                b = 4 * g
                keep_warm(4 * (1 - g), 1)
                pe.wait_ge(ml_w, s + 1)
                pe.wait_ge(ml_va, s + 1)
                pe.wait_ge(ml_qs, s + 1)
                for j in range(2):
                    h = 2 * g + j
                    last = mm(PS[:, b + j, 0:257], Em[:, h * P:(h + 1) * P], vaug[:, h, :], start=True, stop=c == 0)
                    if c:
                        for k in range(2):
                            last = mm(PS[:, b + j, 0:257], qs[:, (2 * h + k) * P:(2 * h + k + 1) * P], CT[:, h, k, :],
                                      start=False, stop=k == 1)
                last.then_inc(ml_num, 1)
                for i in range(4):
                    if i >= 2:
                        pe.wait_ge(ml_upd, 4 * s + i - 1)
                    h, k = 2 * g + i // 2, i % 2
                    mm(PS[:, b + 2 + i % 2, 0:257], kw[:, h * 256 + k * P:h * 256 + (k + 1) * P], vaug[:, h, :],
                       start=True, stop=True).then_inc(ml_st, 1)

            def ml_back(s):
                _, g = STEPS[s]
                pe.wait_ge(ml_upd, 4 * s + 4)
                keep_warm(4 * g + 3, 3)
                pe.wait_ge(ml_hn, s + 1)
                for i in range(4):
                    last = nc.tensor.transpose(PS[:, 4 * g + 2, i * P:(i + 1) * P],
                                               hbuf[:, (4 * g + i) * P:(4 * g + i + 1) * P], ident)
                last.then_inc(ml_hT, 1)

            ml_front(0)
            for s in range(NS):
                ml_mid(s)
                if s + 1 < NS:
                    ml_front(s + 1)
                ml_back(s)

            L, cols = NT - TP, slice(TP, NT)
            pe.wait_ge(ml_h, NS)
            for i in range(8):
                nc.tensor.transpose(banks(0, 2)[0:L, i * P:(i + 1) * P], proj[:, 8 + i, cols], ident)
            pe.wait_ge(ml_out, NS)
            for i in range(8):
                last = nc.tensor.transpose(banks(2, 2)[0:L, i * P:(i + 1) * P], proj[:, 16 + i, cols], ident)
            last.then_inc(ml_kv, 1)
            pe.wait_ge(ml_stdone, NS)
            for h in range(4):
                for k in range(2):
                    mm(PS[0:L, 4, h * P:h * P + L], proj[:, 8 + 2 * h + k, cols], proj[:, 2 * h + k, cols],
                       start=k == 0, stop=k == 1)
            for h in range(4):
                mm(PS[0:L, 5, h * P:h * P + L], sel[64:68, h, 0:L], G[64:68, 3, cols], start=True, stop=True)
            for h in range(4):
                last = mm(PS[:, 6, h * P:h * P + L], sel[64:68, h, :], G[64:68, 5, cols], start=True, stop=True)
            last.then_inc(ml_sc, 1)
            keep_warm(7, 4)
            pe.wait_ge(ml_w, NS + 1)
            pe.wait_ge(ml_va, NS + 1)
            pe.wait_ge(ml_qs, NS + 1)
            for h in range(4):
                mm(PS[0:L, h, 0:257], Em[0:L, h * P:h * P + L], vaug[0:L, h, :], start=True, stop=False)
            n = 0
            for i in range(16):
                h = i // 4
                pe.wait_ge(caug_moved[i % NCB], 32 * (i // NCB) + 16)
                pe.wait_ge(ml_qm, i + 1)
                for j in range(4):
                    mm(PS[0:L, h, 0:257], qmask[i % 2][:, j * 32:(j + 1) * 32], CB[i % NCB][:, j, :],
                       start=False, stop=i % 4 == 3 and j == 3)
                for j in range(4):
                    if n >= 4:
                        pe.wait_ge(ml_upd, 4 * NS + n - 3)
                    mm(PS[:, 4 + n % 4, 0:257], kwmask[i % 2][0:32, j * P:(j + 1) * P], vaug[0:32, h, :],
                       start=True, stop=True).then_inc(ml_st, 1)
                    n += 1
            pe.wait_ge(ml_upd, 4 * NS + n)
            pe.sem_inc(ml_num, 1)
            pe.wait_ge(ml_hn, NS + 1)
            for i in range(8):
                last = nc.tensor.transpose(banks(4, 2)[:, i * P:i * P + L], hbuf[0:L, i * P:(i + 1) * P],
                                           ident[0:L, 0:L])
            last.then_inc(ml_hT, 1)

            pe.wait_ge(ml_h, NS + 1)
            merge("merge1", proj[:, 24:32, :], ml_out, NS + 1)
            dense("up", 4, uT)
            ada("ada_ffn", 1)

            b0, _, a0 = PHASES["poolw"]
            wait_block(b0)
            pe.wait_ge(pool_d, 1)
            for n in range(8):
                g, m = n // 2, n % 2
                pe.wait_ge(acc_free[n % 2], (a0 + n) // 2 + 1)
                for k in range(2):
                    for h in range(2):
                        last = mm(acc(n % 2)[:, h, :], ring[:, b0 % RING, (g * 2 + k) * 256 + m * P:(g * 2 + k) * 256 + m * P + P],
                                  dpool[:, 2 * g + k, h * HALF:(h + 1) * HALF], start=k == 0, stop=k == 1)
                last.then_inc(group_done, 1)
            merge("merge2", proj[:, 8:16, :], evac_pool, 8)
            pe.wait_ge(gate_used, 2 + 24)

            def mean_tile(n, kt, src):
                pe.wait_ge(r_ready, KT * n + kt + 1)
                for h in range(2):
                    last = mm(PS[:, 4 + h, 0:HALF], mean, src[:, kt, h * HALF:(h + 1) * HALF], start=kt == 0, stop=kt == KT - 1)
                if kt == KT - 1:
                    last.then_inc(ln_mu, 1)

            def variance(n, sq):
                for kt in range(KT):
                    pe.wait_ge(ln_sq, KT * n + kt + 1)
                    for h in range(2):
                        last = mm(PS[:, 6 + h, 0:HALF], mean, sq[:, kt, h * HALF:(h + 1) * HALF], start=kt == 0, stop=kt == KT - 1)
                last.then_inc(ln_var, 1)

            pe.wait_ge(ada_ready, 2)
            for i in range(4):
                dense_block(PHASES["out"][0] + i, PHASES["out"][2] + 2 * i, merged)
                if i:
                    mean_tile(0, 2 * i - 2, proj)
                    mean_tile(0, 2 * i - 1, proj)
            mean_tile(0, 6, proj)
            mean_tile(0, 7, proj)
            variance(0, proj[:, 16:24, :])

            for kt in range(KT):
                pe.wait_ge(u2_ready, kt + 1)
                for h in range(2):
                    last = mm(PS[0:20, 4 + h, 0:HALF], wr[:, kt, :], uT[:, kt, h * HALF:(h + 1) * HALF],
                              start=kt == 0, stop=kt == KT - 1)
            last.then_inc(rtT_psum, 1)
            pe.wait_ge(rtT_ready, 1)
            for c, (t0, L) in enumerate(CHUNKS):
                last = nc.tensor.transpose(PS[0:L, 4, c * 20:(c + 1) * 20], gs[0:20, 0, t0:t0 + L], ident[0:20, 0:20])
            last.then_inc(rt_psum, 1)
            for c, (t0, L) in enumerate(CHUNKS):
                b = 2 * (c % 2)
                if c >= 2:
                    pe.wait_ge(u2r_ready, c - 1)
                for kt in range(KT):
                    last = nc.tensor.transpose(banks(b, 2)[0:L, kt * P:(kt + 1) * P], uT[:, kt, t0:t0 + L], ident)
                last.then_inc(u2p, 1)
            pe.wait_ge(ohs_ready, 1)
            for c, (t0, L) in enumerate(CHUNKS):
                for k in range(c + 1):
                    mm(PS[0:L, 4, c * NE:(c + 1) * NE], (one if k < c else cc("mask"))[:, 0:L], rt[:, k, 96:112],
                       start=k == 0, stop=k == c)
            for k in range(5):
                last = mm(PS[:, 4, 80:96], one, rt[:, k, 96:112], start=k == 0, stop=k == 4)
            last.then_inc(cnt_psum, 1)

            def at(b, it):
                return b if it is None else it * NBUF + b

            def rows_T(b, it=None):
                pe.wait_ge(x_got[b % NBUF], 16 * (b // NBUF + 1) if it is None else it * 16 + 16 * (b // NBUF + 1))
                if b:
                    pe.wait_ge(xt_ready, at(b, it))
                for kt in range(KT):
                    last = nc.tensor.transpose(banks(0, 2)[:, kt * P:(kt + 1) * P], X3[b % NBUF][:, kt * P:(kt + 1) * P], ident)
                last.then_inc(xt_psum, 1)

            def gate_up(b, it=None):
                pe.wait_ge(e_loaded[b % NBUF], 16 * (b // NBUF + 1) if it is None else it * 16 + 16 * (b // NBUF + 1))
                pe.wait_ge(xt_ready, at(b + 1, it))
                if b:
                    pe.wait_ge(h_ready, at(b, it))
                for kt in range(KT):
                    last = mm(PS[:, 2, :], XT3[b % NBUF][:, kt, :], E3[b % NBUF][:, kt * 512:(kt + 1) * 512],
                              start=kt == 0, stop=kt == KT - 1)
                last.then_inc(gu_psum, 1)

            def hidden_T(b, it=None):
                pe.wait_ge(h_ready, at(b + 1, it))
                if b:
                    pe.wait_ge(hT_ready, at(b, it))
                for f in range(2):
                    last = nc.tensor.transpose(PS[:, 3, f * P:(f + 1) * P], H3[b % NBUF][:, f * P:(f + 1) * P], ident)
                last.then_inc(h_psum, 1)

            def down(b, it=None):
                pe.wait_ge(hT_ready, at(b + 1, it))
                if b:
                    pe.wait_ge(y_ready, at(b, it))
                for n in range(2):
                    for f in range(2):
                        last = mm(PS[:, 4 + n, :], HT3[b % NBUF][:, f * P:(f + 1) * P],
                                  E3[b % NBUF][:, 4096 + f * 1024 + n * 512:4096 + f * 1024 + (n + 1) * 512],
                                  start=f == 0, stop=f == 1)
                last.then_inc(y_psum, 1)

            def step(b, it=None, first=False, last=False):
                if not last:
                    rows_T(b + 1, it)
                gate_up(b, it)
                if not first:
                    down(b - 1, it)
                hidden_T(b, it)

            def run_blocks(first, last):
                turns = (last - first - 2) // NBUF
                rows_T(first)
                step(first, first=True)
                with pe.Fori(0, turns) as it:
                    for b in range(first + 1, first + 1 + NBUF):
                        step(b, it)
                for b in range(first + 1 + turns * NBUF, last):
                    step(b, last=b == last - 1)
                down(last - 1)

            pe.wait_ge(cnt_used, 1)
            pe.wait_ge(pos_ready, 1)
            further = pe.value_load(n_further, min_val=0, max_val=XB)
            run_blocks(0, NE)
            with pe.If(further > 0):
                run_blocks(NE, NB)
            for c, (t0, L) in enumerate(CHUNKS):
                b = 2 * (c % 2)
                pe.wait_ge(moe_ready, c + 1)
                if c >= 2:
                    pe.wait_ge(moeT_ready, c - 1)
                for kt in range(KT):
                    last = nc.tensor.transpose(banks(b, 2)[:, kt * P:kt * P + L], BK[c][0][0:L, kt * P:(kt + 1) * P],
                                               ident[0:L, 0:L])
                last.then_inc(moeT_psum, 1)
            for kt in range(KT):
                mean_tile(1, kt, merged)
            variance(1, proj[:, 20:28, :])

        @block.scalar
        def _(act):
            made = {}

            def do(ins, s=act_step, n=1):
                ins.then_inc(s, 1)
                made[s] = made.get(s, 0) + 1
                act.wait_ge(s, made[s])

            for s in acc_free:
                act.sem_inc(s, 1)

            def evac(name, n, dst_tile, s):
                _, g0, _ = PHASES[name]
                if n >= 16:
                    with act.Fori(0, n // 8) as it:
                        for i in range(8):
                            act.wait_ge(group_done, it * 8 + (g0 + i + 1))
                            nc.scalar.copy(proj[:, bass.ds(it * 8 + (dst_tile + i), 1), :].rearrange(
                                "p o (h t) -> p (o h) t", h=2), acc(i % 2)).then_inc(acc_free[i % 2], 1)
                    rest = range(n // 8 * 8, n)
                else:
                    rest = range(n)
                for i in rest:
                    act.wait_ge(group_done, g0 + i + 1)
                    nc.scalar.copy(halves(proj[:, dst_tile + i, :]), acc(i % 2)).then_inc(acc_free[i % 2], 1)
                a_end = PHASES[name][2] + n
                for x in acc_free:
                    act.wait_ge(x, a_end // 2 + 1)
                act.sem_inc(s, n)

            def ada_copy(name):
                _, g0, _ = PHASES[name]
                for i in range(12):
                    act.wait_ge(group_done, g0 + 2 * i + 2)
                    nc.scalar.copy(arow[:, i * 256:(i + 1) * 256], PS[0:9, 4 + i % 2, 0:256]).then_inc(ada_rows, 1)

            ada_copy("ada_mix")
            act.wait_ge(gates_psum, 1)
            act.wait_ge(small_loaded, 32)
            do(nc.scalar.activation(halves(G[0:68, 0, :]), PS[0:68, 4:6, 0:HALF], ACT.Identity,
                                    bias=vv("row_bias", 0)[0:68]), xrow_ready)
            do(nc.scalar.activation(exl[0:16, 0, 0:1], vv("a_log", 0)[0:16], ACT.Exp))
            act.wait_ge(rabs_ready, 1)
            do(nc.scalar.activation(G[0:68, 1, :], G[0:68, 1, :], ACT.Exp, scale=-1.0), rexp_ready)
            act.wait_ge(rw_ready, 1)
            do(nc.scalar.activation(G[0:68, 5, :], G[0:68, 2, :], ACT.Ln), rln_ready)
            def z_tiles(first, last):
                for i in range(first, last):
                    act.wait_ge(group_done, PHASES["z"][1] + i + 1)
                    nc.scalar.activation(halves(proj[:, 12 + i, :]), acc(i % 2), ACT.Silu).then_inc(z_silu, 1)
                    act.wait_ge(z_silu, i + 1)
                    act.sem_inc(acc_free[i % 2], 1)

            z_tiles(0, 6)
            act.wait_ge(cumd_ready, 1)
            do(nc.scalar.activation(G[0:16, 3, :], G[0:16, 2, :], ACT.Exp))
            do(nc.scalar.activation(G[0:16, 4, :], G[0:16, 4, :], ACT.Exp))
            do(nc.scalar.activation(G[64:68, 5, :], G[64:68, 5, :], ACT.Exp))
            do(nc.scalar.activation(G[64:68, 0, :], G[64:68, 4, :], ACT.Exp, scale=-1.0))
            do(nc.scalar.activation(G[64:68, 6, :], G[64:68, 6, :], ACT.Exp), rowexp_ready)

            z_tiles(6, 8)
            _, g0, _ = PHASES["xbc"]

            def conv_in(i):
                act.wait_ge(group_done, g0 + i + 1)
                nc.scalar.copy(halves(cin[:, i % 2, :]), acc(i % 2)).then_inc(conv_x, 1)
                act.wait_ge(conv_x, i + 1)
                act.sem_inc(acc_free[i % 2], 1)

            def conv_out(i):
                act.wait_ge(conv_pre, i + 1)
                do(nc.scalar.activation(proj[:, i, :], proj[:, i, :], ACT.Silu, bias=vv("conv_b", i)), conv_silu)

            for i in range(8):
                if i >= 2:
                    conv_out(i - 2)
                conv_in(i)
            act.wait_ge(tok_psum, 1)
            for bank, w, a0 in ((6, 64, 0), (7, 16, 64)):
                do(nc.scalar.copy(tg[:, 0:4, a0:a0 + w], PS[:, bank, 0:4 * w].rearrange("p (c n) -> p c n", c=4)))
                do(nc.scalar.copy(tg[0:32, 4, a0:a0 + w], PS[0:32, bank, 4 * w:5 * w]), tok_ready)
            do(nc.scalar.copy(exl[:], PS[:, 6, 320:512].rearrange("p (h s) -> p h s", h=16)))
            do(nc.scalar.copy(wpb[:], PS[:, 7, 80:128].rearrange("p (h s) -> p h s", h=4)), tok_ready)
            for i in range(8, 12):
                conv_out(i - 2)
                conv_in(i)
            conv_out(10)
            conv_out(11)
            for s, (c, g) in enumerate(STEPS):
                act.wait_ge(ssd_xb, s + 1)
                do(nc.scalar.copy(Bt[:, g * P:(g + 1) * P], PS[:, 6 + g, 0:P]), ssd_bt)
                act.wait_ge(ssd_seg, s + 1)
                e = Es[:, g * 1024:(g + 1) * 1024]
                do(nc.scalar.activation(e, e, ACT.Exp), ssd_exp)
            L = NT - TP
            act.wait_ge(ssd_xb, NS + 1)
            do(nc.scalar.copy(Bt[0:L, :], PS[0:L, 6, 0:256]), ssd_bt)
            act.wait_ge(ssd_seg, NS + 1)
            e = Es[0:L, :].rearrange("p (h l) -> p h l", h=16)[:, :, 0:L]
            do(nc.scalar.activation(e, e, ACT.Exp), ssd_exp)
            act.wait_ge(ssd_out, NS + 1)
            do(nc.scalar.activation(proj[:, 0:8, :], proj[:, 12:20, :], ACT.Square), sq_ready)
            act.wait_ge(ssq_psum, 1)
            do(nc.scalar.activation(halves(gs[:, 0, :]), PS[:, 0:2, 0:HALF], ACT.Sqrt, bias=cc("eps")[:, 1:2]), sd_ready)
            act.wait_ge(br_ready, 1)

            def gates(name, b):
                _, g0, _ = PHASES[name]
                a = VEC["gate_b"][0]
                with act.Fori(0, 2) as it:
                    for i in range(4):
                        g = 4 * (i // 2) + i % 2
                        act.wait_ge(group_done, it * 8 + (g0 + g + 1))
                        act.wait_ge(gate_used, it * 4 + (8 * b + i + 1))
                        nc.scalar.activation(halves(gs[:, i % 2, :]), acc(i % 2), ACT.Sigmoid,
                                             bias=V[:, bass.ds(it * 4 + (a + 8 * b + i), 1)]).then_inc(gate_ready, 1)

            act.sem_inc(gate_used, 2)
            gates("merge0", 0)
            evac("qkvo", 24, 0, evac_qk)
            for i in range(24, 32):
                act.wait_ge(group_done, PHASES["qkvo"][1] + i + 1)
                nc.scalar.activation(halves(proj[:, i, :]), acc(i % 2), ACT.Sigmoid).then_inc(og_ready, 1)
                act.wait_ge(og_ready, i - 23)
                act.sem_inc(acc_free[i % 2], 1)

            def values(s):
                g = STEPS[s][1]
                act.wait_ge(ml_kv, s + 1)
                do(nc.scalar.copy(vaug[:, 2 * g:2 * g + 2, 0:256], PS[:, 4 * g + 1, :].rearrange("p (h v) -> p h v", h=2)), ml_va)

            values(0)
            for s, (c, g) in enumerate(STEPS):
                act.wait_ge(ml_d, s + 1)
                e = Em[:, g * 256:(g + 1) * 256]
                do(nc.scalar.activation(e, e, ACT.Exp), ml_exp)
                if s + 1 < NS:
                    values(s + 1)
                act.wait_ge(ml_h, s + 1)
                sd = hstat[:, 32 * g + 18:32 * g + 20]
                do(nc.scalar.activation(sd, sd, ACT.Sqrt, bias=cc("eps")[:, 0:1]), ml_sd)
            L = NT - TP
            act.wait_ge(ml_kv, NS + 1)
            do(nc.scalar.copy(vaug[0:L, :, 0:256], banks(2, 2)[0:L, :].rearrange("p (h v) -> p h v", h=4)), ml_va)
            act.wait_ge(ml_d, NS + 1)
            e = Em[0:L, :].rearrange("p (h l) -> p h l", h=4)[:, :, 0:L]
            do(nc.scalar.activation(e, e, ACT.Exp), ml_exp)
            act.wait_ge(ml_h, NS + 1)
            do(nc.scalar.activation(hstat[0:L, 36:40], hstat[0:L, 36:40], ACT.Sqrt, bias=cc("eps")[0:L, 0:1]), ml_sd)
            act.wait_ge(ml_out, NS + 1)
            gates("merge1", 1)
            evac("up", 8, 0, evac_up)
            act.wait_ge(ml_stdone, NS + 1)
            ada_copy("ada_ffn")
            _, g0, _ = PHASES["poolw"]
            for i in range(8):
                act.wait_ge(group_done, g0 + i + 1)
                nc.scalar.activation(halves(proj[:, 8 + i, :]), acc(i % 2), ACT.Copy,
                                     scale=vv("pool_scale", i)).then_inc(acc_free[i % 2], 1)
            for x in acc_free:
                act.wait_ge(x, PHASES["merge2"][2] // 2 + 1)
            act.sem_inc(evac_pool, 8)
            gates("merge2", 2)
            act.wait_ge(pool_stored, 1)
            _, g0, _ = PHASES["out"]
            for i in range(8):
                act.wait_ge(group_done, g0 + i + 1)
                do(nc.scalar.activation(halves(proj[:, i, :]), acc(i % 2), ACT.Copy, scale=adaM[:, 16 + i, 0:1]))
                do(nc.scalar.copy(proj[:, i, TP:NT], PS[:, 2 * (i % 2) + 1, TP - HALF:HALF]), out_tile)
                act.sem_inc(acc_free[i % 2], 1)

            def layer_norm(n, cen, sq, gname, bname):
                for kt in range(KT):
                    act.wait_ge(ln_cen, KT * n + kt + 1)
                    nc.scalar.activation(sq[:, kt, :], cen[:, kt, :], ACT.Square).then_inc(ln_sq, 1)
                act.wait_ge(ln_var, n + 1)
                do(nc.scalar.activation(halves(gs[:, 0, :]), PS[:, 6:8, 0:HALF], ACT.Sqrt, bias=cc("eps")[:, 0:1]), ln_sd)
                for kt in range(KT):
                    act.wait_ge(ln_norm, KT * n + kt + 1)
                    nc.scalar.activation(merged[:, kt, :], cen[:, kt, :], ACT.Identity, scale=vv(gname, kt),
                                         bias=vv(bname, kt)).then_inc(ln_done, 1)

            layer_norm(0, proj[:, 0:8, :], proj[:, 16:24, :], "ln1_g", "ln1_b")
            act.wait_ge(rtT_psum, 1)
            do(nc.scalar.copy(halves(gs[0:20, 0, :]), PS[0:20, 4:6, 0:HALF]), rtT_ready)
            act.wait_ge(rt_d, 1)
            do(nc.scalar.activation(rt[:, :, 24:28], rt[:, :, 24:28], ACT.Exp), rt_e)
            act.wait_ge(rt_dd, 1)
            do(nc.scalar.activation(rt[:, :, 60:61], rt[:, :, 60:61], ACT.Exp), rt_e2)
            for c, (t0, L) in enumerate(CHUNKS):
                act.wait_ge(u2p, c + 1)
                do(nc.scalar.copy(u2r[c][0:L, :], banks(2 * (c % 2), 2)[0:L, :]), u2r_ready)
            act.wait_ge(u2_stored, 16 * len(CHUNKS))

            def block_step(b, it=None):
                i = b % NBUF
                v = b + 1 if it is None else it * NBUF + (b + 1)
                act.wait_ge(xt_psum, v)
                nc.scalar.copy(XT3[i], banks(0, 2).rearrange("p (k s) -> p k s", k=KT)).then_inc(xt_ready, 1)
                act.wait_ge(gu_psum, v)
                nc.scalar.activation(H3[i], PS[:, 2, 0:256], ACT.Silu).then_inc(sg_ready, 1)

            def run_blocks(first, last):
                turns = (last - first) // NBUF
                with act.Fori(0, turns) as it:
                    for b in range(first, first + NBUF):
                        block_step(b, it)
                for b in range(first + turns * NBUF, last):
                    block_step(b)

            act.wait_ge(pos_ready, 1)
            further = act.value_load(n_further, min_val=0, max_val=XB)
            run_blocks(0, NE)
            with act.If(further > 0):
                run_blocks(NE, NB)
            for c, (t0, L) in enumerate(CHUNKS):
                act.wait_ge(moeT_psum, c + 1)
                do(nc.scalar.copy(uT[:, :, t0:t0 + L], banks(2 * (c % 2), 2).rearrange("p (k s) -> p k s", k=KT)[:, :, 0:L]),
                   moeT_ready)
            layer_norm(1, merged[:], proj[:, 20:28, :], "ln2_g", "ln2_b")

        @block.vector
        def _(dve):
            v = nc.vector
            made = {}

            def do(ins, s=dve_step):
                ins.then_inc(s, 1)
                made[s] = made.get(s, 0) + 1
                dve.wait_ge(s, made[s])

            def bc(ap, shape):
                return ap.to_broadcast(shape)

            def smp(t):
                return t.rearrange("p a (j t) -> p a j t", j=NSEQ)

            def ada_finish(dst, name, bank):
                a, _ = VEC[name]
                do(v.tensor_tensor(dst[:], PS[:, bank, 0:216].rearrange("p (m s) -> p m s", m=24),
                                   bc(V[:, a:a + 24].unsqueeze(2), [P, 24, 9]), ALU.add))
                do(v.tensor_scalar(dst[:, 8:24, :], dst[:, 8:24, :], 1.0, None, ALU.add), ada_ready)

            def modulate(dst, src, ada_, done):
                for i in range(KT):
                    do(v.tensor_scalar(dst[:, i, 0:TP], src[:, i, 0:TP], ada_[:, 8 + i, 0:1], ada_[:, i, 0:1],
                                       ALU.mult, ALU.add))
                do(v.tensor_tensor(smp(dst[:, :, TP:NT]), smp(src[:, :, TP:NT]),
                                   bc(ada_[:, 8:16, 1:9].unsqueeze(3), [P, 8, NSEQ, TS]), ALU.mult))
                do(v.tensor_tensor(smp(dst[:, :, TP:NT]), smp(dst[:, :, TP:NT]),
                                   bc(ada_[:, 0:8, 1:9].unsqueeze(3), [P, 8, NSEQ, TS]), ALU.add), done)

            do(v.memset(zeros, 0), zero_ready)
            do(v.memset(no_rows, 0.0))
            dve.wait_ge(small_loaded, 32)
            dve.wait_ge(ada_psum, 12)
            ada_finish(adaM, "b_ada_mix", 7)
            dve.wait_ge(x_loaded, 16)
            modulate(uT, uT, adaM, u_ready)

            r16, r4 = slice(0, 16), slice(64, 68)
            do(v.memset(mp[64:68, 0:1], 0.0))
            dve.wait_ge(rows_in_loaded, 64)
            dve.wait_ge(xrow_ready, 1)
            do(v.scalar_tensor_tensor(G[0:68, 1, :], G[0:68, 0, :], -1.0, G[0:68, 0, :], ALU.mult, ALU.max), rabs_ready)
            dve.wait_ge(rexp_ready, 1)
            do(v.tensor_scalar(G[0:68, 2, :], G[0:68, 1, :], 1.0, None, ALU.add), rw_ready)
            do(v.tensor_scalar(G[0:68, 3, :], G[0:68, 2, :], -1.0, None, ALU.add))
            do(v.tensor_scalar(G[0:68, 4, :], G[0:68, 3, :], 0.0, None, ALU.is_equal))
            do(v.tensor_tensor(G[0:68, 3, :], G[0:68, 3, :], G[0:68, 4, :], ALU.add))
            do(v.reciprocal(G[0:68, 3, :], G[0:68, 3, :]))
            dve.wait_ge(rln_ready, 1)
            do(v.tensor_tensor(G[0:68, 5, :], G[0:68, 5, :], G[0:68, 4, :], ALU.add))
            do(v.tensor_tensor(G[0:68, 5, :], G[0:68, 5, :], G[0:68, 1, :], ALU.mult))
            do(v.tensor_tensor(G[0:68, 5, :], G[0:68, 5, :], G[0:68, 3, :], ALU.mult))
            do(v.scalar_tensor_tensor(G[r16, 6, :], G[r16, 0, :], 0.0, G[r16, 5, :], ALU.max, ALU.add))
            do(v.scalar_tensor_tensor(G[r4, 6, :], G[r4, 0, :], 0.0, G[r4, 5, :], ALU.min, ALU.subtract))
            do(v.tensor_scalar(G[r16, 1, :], G[r16, 6, :], exl[0:16, 0, 0:1], -1.0, ALU.mult, ALU.mult))
            do(v.tensor_tensor_scan(G[r16, 2, :], seg0[r16, :], G[r16, 1, :], 0.0, ALU.mult, ALU.add))
            do(v.tensor_tensor_scan(G[r4, 2, :], seg0[r4, :], G[r4, 6, :], 0.0, ALU.mult, ALU.add))
            do(v.tensor_copy(G[r4, 1, :], G[32:36, 0, :]))
            do(v.tensor_tensor(G[r4, 1, :], G[r4, 1, :], G[r4, 2, :], ALU.subtract))
            for s in range(NSEG):
                a, b = (s * P, s * P + P) if s < 4 else (TP + (s - 4) * TS, TP + (s - 3) * TS)
                do(v.tensor_tensor_scan(G[r4, 3, a:b], G[r4, 1, a:b], G[r4, 1, a:b], mp[r4, s:s + 1], ALU.max, ALU.max))
                if s < 3:
                    do(v.tensor_tensor(mp[r4, s + 1:s + 2], G[r4, 3, b - 1:b], G[r4, 2, b - 1:b], ALU.add))
            do(v.tensor_tensor(G[r4, 4, :], G[r4, 3, :], G[r4, 2, :], ALU.add), m_ready)

            def segs(row, r):
                return (row[r, 0:TP].rearrange("p (s t) -> p s t", s=4),
                        row[r, TP:NT].rearrange("p (s t) -> p s t", s=NSEQ))

            for k, (n, s0, w) in enumerate(((4, 0, P), (NSEQ, 4, TS))):
                M_, a_ = segs(G[:, 3, :], r4)[k], segs(G[:, 1, :], r4)[k]
                cum_ = segs(G[:, 2, :], r16)[k]
                do(v.tensor_tensor(segs(G[:, 5, :], r4)[k], bc(mp[r4, s0:s0 + n].unsqueeze(2), [4, n, w]), M_,
                                   ALU.subtract))
                do(v.tensor_tensor(segs(G[:, 6, :], r4)[k], a_, bc(M_[:, :, w - 1:w], [4, n, w]), ALU.subtract))
                do(v.tensor_tensor(segs(G[:, 4, :], r16)[k], bc(cum_[:, :, w - 1:w], [16, n, w]), cum_, ALU.subtract))
            dve.sem_inc(cumd_ready, 1)
            dve.wait_ge(rowexp_ready, 1)
            do(v.tensor_scalar(G[r4, 6, :], G[r4, 6, :], 0.0625, None, ALU.mult))
            dg16 = G[r16, 1, 0:192].rearrange("p (h s) -> p h s", h=16)
            dg4 = G[r4, 2, 0:48].rearrange("p (h s) -> p h s", h=4)
            for k, (n, s0, w) in enumerate(((4, 0, P), (NSEQ, 4, TS))):
                ex = segs(G[:, 3, :], r16)[k][:, :, w - 1:w].rearrange("p s o -> p o s")
                do(v.tensor_tensor(dg16[:, :, s0:s0 + n], bc(ex, [16, 16, n]),
                                   bc(ident[r16, 0:16].unsqueeze(2), [16, 16, n]), ALU.mult))
                wp = segs(G[:, 5, :], r4)[k][:, :, w - 1:w].rearrange("p s o -> p o s")
                do(v.tensor_tensor(dg4[:, :, s0:s0 + n], bc(wp, [4, 4, n]),
                                   bc(ident[r4, 64:68].unsqueeze(2), [4, 4, n]), ALU.mult))
            dve.sem_inc(rows_ready, 1)

            dve.wait_ge(conv_in_loaded, 16)
            do(v.tensor_copy(sx[:, :, :, 0:3], hist))
            for i in range(12):
                x_ = cin[:, i % 2, :]
                dve.wait_ge(conv_x, i + 1)
                do(v.tensor_copy(sx[:, i, :, 3:7], x_[:, TP:NT].rearrange("p (j t) -> p j t", j=NSEQ)))
                do(v.tensor_copy(tail[:, i, :], x_[:, TP - 3:NT]), conv_tail)

                def tap(k):
                    return vv("conv_w", k * 12 + i)
                o = proj[:, i, 0:TP]
                os_ = proj[:, i, TP:NT].rearrange("p (j t) -> p j t", j=NSEQ)
                do(v.tensor_scalar(o, x_[:, 0:TP], tap(3), None, ALU.mult))
                do(v.tensor_scalar(os_, sx[:, i, :, 3:7], tap(3), None, ALU.mult))
                for k in (2, 1, 0):
                    d = 3 - k
                    do(v.scalar_tensor_tensor(o[:, d:], x_[:, 0:TP - d], tap(k), o[:, d:], ALU.mult, ALU.add))
                    do(v.scalar_tensor_tensor(os_, sx[:, i, :, k:k + 4], tap(k), os_, ALU.mult, ALU.add),
                       dve_step if k else conv_pre)

            dve.wait_ge(tok_ready, 3)

            def ssd_exponents(s):
                c, g = STEPS[s]
                hs = slice(g * 512, (g + 1) * 512)
                x8 = lambda t: t.rearrange("p (h d) -> p h d", h=8)
                col = lambda a, w: bc(tg[:, c, a + 8 * g:a + 8 * g + 8].unsqueeze(2), [P, 8, w])
                dve.wait_ge(ssd_xb, s + 1)
                do(v.tensor_tensor(x8(xdt[:, hs]), x8(PS[:, 4 + g, :]), col(0, 64), ALU.mult))
                do(v.tensor_tensor(x8(xw[:, hs]), x8(xdt[:, hs]), col(48, 64), ALU.mult))
                dve.wait_ge(ssd_bt, s + 1)
                do(v.tensor_tensor(cbm[:, g * P:(g + 1) * P], PS[:, 6 + g, 256:256 + P], cc("mask"), ALU.mult))
                dve.wait_ge(ssd_bc, s + 1)
                e = Es[:, g * 1024:(g + 1) * 1024]
                do(v.tensor_tensor(x8(e), x8(banks(2 * g, 2)), col(16, P), ALU.subtract))
                do(v.tensor_scalar(e, e, 0.0, None, ALU.min), ssd_seg)

            def ssd_weights(s):
                _, g = STEPS[s]
                dve.wait_ge(ssd_exp, s + 1)
                e = Es[:, g * 1024:(g + 1) * 1024].rearrange("p (h l) -> p h l", h=8)
                do(v.tensor_tensor(e, e, bc(cbm[:, g * P:(g + 1) * P].unsqueeze(1), [P, 8, P]), ALU.mult), ssd_w)

            def ssd_results(s):
                c, g = STEPS[s]
                hs = slice(g * 512, (g + 1) * 512)
                x8 = lambda t: t.rearrange("p (h d) -> p h d", h=8)
                dve.wait_ge(ssd_yp, s + 1)
                if c == 0:
                    do(v.tensor_copy(ytok[:, hs], PS[:, 4 + g, :]), ssd_ytok)
                else:
                    do(v.tensor_tensor(x8(ytok[:, hs]), x8(PS[:, 2 * g + 1, :]),
                                       bc(tg[:, c, 32 + 8 * g:40 + 8 * g].unsqueeze(2), [P, 8, 64]), ALU.mult))
                    do(v.tensor_tensor(ytok[:, hs], ytok[:, hs], PS[:, 4 + g, :], ALU.add), ssd_ytok)
                dve.wait_ge(ssd_st, s + 1)
                if c == 0:
                    do(v.tensor_copy(sT[:, hs], PS[:, 6 + g, :]), ssd_stdone)
                else:
                    do(v.tensor_tensor(x8(sT[:, hs]), x8(sT[:, hs]), bc(exl[:, 8 * g:8 * g + 8, c:c + 1], [P, 8, 64]), ALU.mult))
                    do(v.tensor_tensor(sT[:, hs], sT[:, hs], PS[:, 6 + g, :], ALU.add), ssd_stdone)

            def ssd_finish(s):
                c, g = STEPS[s]
                cols = slice(c * P, c * P + P)
                dve.wait_ge(ssd_yTp, s + 1)
                for i in range(4 * g, 4 * g + 4):
                    do(v.scalar_tensor_tensor(ytok[:, i * P:(i + 1) * P], proj[:, i, cols], vv("ssd_D", i),
                                              PS[:, 2 * g, (i - 4 * g) * P:(i - 4 * g + 1) * P], ALU.mult, ALU.add))
                z = proj[:, 12 + 4 * g:16 + 4 * g, cols]
                do(v.tensor_tensor(z, z, ytok[:, g * 512:(g + 1) * 512].rearrange("p (i l) -> p i l", i=4), ALU.mult), ssd_out)

            dve.wait_ge(z_silu, 8)
            ssd_exponents(0)
            for s in range(NS):
                ssd_weights(s)
                if s:
                    ssd_finish(s - 1)
                ssd_results(s)
                if s + 1 < NS:
                    ssd_exponents(s + 1)
            ssd_finish(NS - 1)

            c, t0, L = TP // P, TP, NT - TP
            cols = slice(t0, t0 + L)
            x16 = lambda t: t[0:L, :].rearrange("p (h d) -> p h d", h=16)
            tgc = lambda a, n=16, w=64: bc(tg[0:L, c, a:a + n].unsqueeze(2), [L, n, w])
            dve.wait_ge(ssd_xb, NS + 1)
            do(v.tensor_tensor(x16(xdt), banks(4, 2)[0:L, :].rearrange("p (h d) -> p h d", h=16), tgc(0), ALU.mult))
            do(v.tensor_tensor(x16(xw), x16(xdt), tgc(48), ALU.mult))
            dve.wait_ge(ssd_bt, NS + 1)
            do(v.tensor_tensor(cbm[0:L, :].rearrange("p (g l) -> p g l", g=2)[:, :, 0:L],
                               PS[0:L, 6, 256:512].rearrange("p (g l) -> p g l", g=2)[:, :, 0:L],
                               bc(cc("smask")[0:L, :].unsqueeze(1), [L, 2, L]), ALU.mult))
            dve.wait_ge(ssd_bc, NS + 1)
            e = Es[0:L, :].rearrange("p (h l) -> p h l", h=16)[:, :, 0:L]
            do(v.tensor_tensor(e, banks(0, 4)[0:L, :].rearrange("p (h l) -> p h l", h=16)[:, :, 0:L],
                               tgc(16, 16, L), ALU.subtract))
            do(v.tensor_scalar(e, e, 0.0, None, ALU.min), ssd_seg)
            for g in range(2):
                do(v.tensor_tensor(CTm[:, g * 256:(g + 1) * 256].rearrange("p (j t) -> p j t", j=NSEQ),
                                   bc(proj[:, 10 + g, cols].unsqueeze(1), [P, NSEQ, 32]), seqcol, ALU.mult))
            dve.wait_ge(rows_zeroed, 16)
            do(v.tensor_tensor(Btm[0:32, :].rearrange("p (j n) -> p j n", j=NSEQ),
                               bc(Bt[0:32, :].unsqueeze(1), [32, NSEQ, 256]),
                               bc(cc("tokseq")[0:32, :].unsqueeze(2), [32, NSEQ, 256]), ALU.mult), ssd_masks)
            dve.wait_ge(ssd_exp, NS + 1)
            e = Es[0:L, :].rearrange("p (g h l) -> p g h l", g=2, h=8)[:, :, :, 0:L]
            cb = cbm[0:L, :].rearrange("p (g l) -> p g l", g=2)[:, :, 0:L]
            do(v.tensor_tensor(e, e, bc(cb.unsqueeze(2), [L, 2, 8, L]), ALU.mult), ssd_w)
            dve.wait_ge(ssd_yp, NS + 1)
            do(v.tensor_tensor(x16(ytok), banks(2, 2)[0:L, :].rearrange("p (h d) -> p h d", h=16), tgc(32), ALU.mult))
            do(v.tensor_tensor(ytok[0:L, :], ytok[0:L, :], banks(4, 2)[0:L, :], ALU.add), ssd_ytok)
            dve.wait_ge(ssd_yTp, NS + 1)
            for i in range(8):
                do(v.scalar_tensor_tensor(ytok[:, i * P:i * P + L], proj[:, i, cols], vv("ssd_D", i),
                                          banks(0, 2)[:, i * P:i * P + L], ALU.mult, ALU.add))
            do(v.tensor_tensor(proj[:, 12:20, cols], proj[:, 12:20, cols],
                               ytok.rearrange("p (i l) -> p i l", i=8)[:, :, 0:L], ALU.mult), ssd_out)
            for j in range(NSEQ):
                b = 4 + 2 * (j % 2)
                for g in range(2):
                    t = s0g[g][:, j * 512:(j + 1) * 512]
                    t8 = t.rearrange("p (h d) -> p h d", h=8)
                    do(v.tensor_tensor(t8, t8, bc(exl[:, g * 8:(g + 1) * 8, 4 + j:5 + j], [P, 8, 64]), ALU.mult))
                dve.wait_ge(ssd_upd, j + 1)
                do(v.tensor_tensor(s0g[0][:, j * 512:(j + 1) * 512], s0g[0][:, j * 512:(j + 1) * 512], PS[:, b, :], ALU.add))
                do(v.tensor_tensor(s0g[1][:, j * 512:(j + 1) * 512], s0g[1][:, j * 512:(j + 1) * 512], PS[:, b + 1, :],
                                   ALU.add), ssd_updone)
            dve.wait_ge(sd_ready, 1)
            do(v.reciprocal(gs[:, 1, :], gs[:, 0, :]))
            for i in range(8):
                do(v.scalar_tensor_tensor(proj[:, 12 + i, :], proj[:, 12 + i, :], vv("ssd_norm_w", i), gs[:, 1, :],
                                          ALU.mult, ALU.mult), dve_step if i < 7 else br_ready)
            dve.wait_ge(ssd_stdone, NS + 1)

            def merge(name, b):
                _, g0, _ = PHASES[name]
                with dve.Fori(0, 2) as it:
                    for i in range(4):
                        g = 4 * (i // 2) + 2 + i % 2
                        m = merged[:, bass.ds(it * 4 + i, 1), :].rearrange("p o (h t) -> p (o h) t", h=2)
                        s = halves(gs[:, i % 2, :])
                        dve.wait_ge(gate_ready, it * 4 + (8 * b + i + 1))
                        dve.sem_inc(acc_free[i % 2], 1)
                        dve.wait_ge(group_done, it * 8 + (g0 + g + 1))
                        if b == 0:
                            v.tensor_tensor(m, s, acc(i % 2), ALU.mult).then_inc(gate_used, 1)
                        else:
                            v.tensor_tensor(s, s, acc(i % 2), ALU.mult).then_inc(r2_ready, 1)
                            dve.wait_ge(r2_ready, it * 4 + (8 * (b - 1) + i + 1))
                            v.tensor_tensor(m, m, s, ALU.add).then_inc(gate_used, 1)
                        dve.wait_ge(gate_used, it * 4 + (8 * b + i + 3))
                        dve.sem_inc(acc_free[i % 2], 1)

            merge("merge0", 0)

            do(v.memset(vaug[:, :, 256:257], 1.0))
            dve.wait_ge(og_ready, 8)

            def ml_exponents(s):
                c, g = STEPS[s]
                b, cols = 4 * g, slice(c * P, c * P + P)
                dve.wait_ge(ml_kv, s + 1)
                do(v.tensor_tensor(kw[:, g * 512:(g + 1) * 512].rearrange("p (h d) -> p h d", h=2),
                                   PS[:, b, :].rearrange("p (h d) -> p h d", h=2),
                                   bc(tg[:, c, 76 + 2 * g:78 + 2 * g].unsqueeze(2), [P, 2, 256]), ALU.mult))
                e = Em[:, g * 256:(g + 1) * 256]
                two = lambda a: PS[:, b + 3, a:a + 256].rearrange("p (h l) -> p h l", h=2)
                dve.wait_ge(ml_sc, s + 1)
                do(v.tensor_tensor(e.rearrange("p (h l) -> p h l", h=2),
                                   bc(tg[:, c, 64 + 2 * g:66 + 2 * g].unsqueeze(2), [P, 2, P]), two(0), ALU.subtract))
                do(v.tensor_scalar(e, e, 0.0, None, ALU.min), ml_d)
                if c:
                    do(v.tensor_tensor(qs[:, g * 512:(g + 1) * 512].rearrange("p (h k l) -> p h k l", h=2, k=2),
                                       proj[:, 4 * g:4 * g + 4, cols].rearrange("p (h k) l -> p h k l", h=2),
                                       bc(two(256).unsqueeze(2), [P, 2, 2, P]), ALU.mult), ml_qs)
                else:
                    dve.sem_inc(ml_qs, 1)
                do(v.tensor_tensor(scores[g].rearrange("p (h l) -> p h l", h=2),
                                   PS[:, b + 2, 0:256].rearrange("p (h l) -> p h l", h=2),
                                   bc(cc("mask16").unsqueeze(1), [P, 2, P]), ALU.mult))

            def ml_weights(s):
                _, g = STEPS[s]
                e = Em[:, g * 256:(g + 1) * 256]
                dve.wait_ge(ml_exp, s + 1)
                do(v.tensor_tensor(e, e, scores[g], ALU.mult), ml_w)

            def head_outputs(n, L, h0, nh, bank, c, hs):
                dve.wait_ge(ml_num, n + 1)
                den = hs[0:L, 0:nh]
                do(v.tensor_copy(den, PS[0:L, bank:bank + nh, 256]))
                do(v.scalar_tensor_tensor(den, den, -1.0, den, ALU.mult, ALU.max))
                do(v.tensor_tensor(den, den, tg[0:L, c, 72 + h0:72 + h0 + nh], ALU.max))
                do(v.reciprocal(den, den))
                h_ = hbuf[0:L, h0 * 256:(h0 + nh) * 256].rearrange("p (h d) -> p h d", h=nh)
                do(v.tensor_tensor(h_, PS[0:L, bank:bank + nh, 0:256], bc(den.unsqueeze(2), [L, nh, 256]), ALU.mult))
                for h in range(nh):
                    st = hs[0:L, nh + 6 * h:nh + 6 * h + 6]
                    do(v.bn_stats(st, h_[:, h, :]))
                    do(v.bn_aggr(hs[0:L, 7 * nh + 2 * h:7 * nh + 2 * h + 2], st))
                mv = hs[0:L, 7 * nh:9 * nh].rearrange("p (h k) -> p h k", h=nh)
                do(v.tensor_copy(hs[0:L, 9 * nh:10 * nh], mv[:, :, 1]), ml_h)

            def head_norm(n, L, h0, nh, hs):
                dve.wait_ge(ml_sd, n + 1)
                sd = hs[0:L, 9 * nh:10 * nh]
                do(v.reciprocal(sd, sd))
                for h in range(nh):
                    t = hbuf[0:L, (h0 + h) * 256:(h0 + h + 1) * 256]
                    do(v.tensor_scalar(t, t, hs[0:L, 7 * nh + 2 * h:7 * nh + 2 * h + 1], sd[:, h:h + 1],
                                       ALU.subtract, ALU.mult), dve_step if h < nh - 1 else ml_hn)

            def ml_results(s):
                c, g = STEPS[s]
                for i in range(4):
                    h, k = 2 * g + i // 2, i % 2
                    dve.wait_ge(ml_st, 4 * s + i + 1)
                    if c:
                        do(v.scalar_tensor_tensor(CT[:, h, k, :], CT[:, h, k, :], wpb[:, h, c:c + 1],
                                                  PS[:, 4 * g + 2 + i % 2, 0:257], ALU.mult, ALU.add), ml_upd)
                    else:
                        do(v.tensor_copy(CT[:, h, k, :], PS[:, 4 * g + 2 + i % 2, 0:257]), ml_upd)
                dve.sem_inc(ml_stdone, 1)
                head_outputs(s, P, 2 * g, 2, 4 * g, c, hstat[:, 32 * g:32 * g + 32])

            def ml_finish(s):
                c, g = STEPS[s]
                cols = slice(c * P, c * P + P)
                dve.wait_ge(ml_hT, s + 1)
                for i in range(4 * g, 4 * g + 4):
                    do(v.scalar_tensor_tensor(proj[:, 24 + i, cols], PS[:, 4 * g + 2, (i - 4 * g) * P:(i - 4 * g + 1) * P],
                                              vv("mlstm_norm_w", i), proj[:, 24 + i, cols], ALU.mult, ALU.mult),
                       dve_step if i < 4 * g + 3 else ml_out)

            ml_exponents(0)
            for s, (c, g) in enumerate(STEPS):
                ml_weights(s)
                if s:
                    ml_finish(s - 1)
                ml_results(s)
                if s + 1 < NS:
                    ml_exponents(s + 1)
                head_norm(s, P, 2 * g, 2, hstat[:, 32 * g:32 * g + 32])
            ml_finish(NS - 1)

            c, L = TP // P, NT - TP
            cols = slice(TP, NT)
            e = Em[0:L, :].rearrange("p (h l) -> p h l", h=4)[:, :, 0:L]
            col4 = lambda b: PS[0:L, b, :].rearrange("p (h l) -> p h l", h=4)[:, :, 0:L]
            dve.wait_ge(ml_kv, NS + 1)
            do(v.tensor_tensor(kw[0:L, :].rearrange("p (h d) -> p h d", h=4),
                               banks(0, 2)[0:L, :].rearrange("p (h d) -> p h d", h=4),
                               bc(tg[0:L, c, 76:80].unsqueeze(2), [L, 4, 256]), ALU.mult))
            dve.wait_ge(ml_sc, NS + 1)
            do(v.tensor_tensor(e, bc(tg[0:L, c, 64:68].unsqueeze(2), [L, 4, L]), col4(5), ALU.subtract))
            do(v.tensor_scalar(e, e, 0.0, None, ALU.min), ml_d)
            q4 = qs.rearrange("p (h k l) -> p h k l", h=4, k=2)[:, :, :, 0:L]
            w4 = PS[:, 6, :].rearrange("p (h l) -> p h l", h=4)[:, :, 0:L]
            do(v.tensor_tensor(q4, proj[:, 0:8, cols].rearrange("p (h k) l -> p h k l", h=4),
                               bc(w4.unsqueeze(2), [P, 4, 2, L]), ALU.mult), ml_qs)
            dve.wait_ge(ml_exp, NS + 1)
            do(v.tensor_tensor(e, e, bc(cc("smask16")[0:L, :].unsqueeze(1), [L, 4, L]), ALU.mult))
            do(v.tensor_tensor(e, e, col4(4), ALU.mult), ml_w)

            def own_parts(i):
                h, k, jh = i // 4, i // 2 % 2, i % 2
                if i >= 2:
                    dve.wait_ge(ml_st, 4 * NS + 4 * (i - 1))
                do(v.tensor_tensor(kwmask[i % 2][0:32, :].rearrange("p (j d) -> p j d", j=4),
                                   bc(kw[0:32, h * 256 + k * P:h * 256 + (k + 1) * P].unsqueeze(1), [32, 4, P]),
                                   bc(cc("tokseq")[0:32, 4 * jh:4 * jh + 4].unsqueeze(2), [32, 4, P]), ALU.mult))
                do(v.tensor_tensor(qmask[i % 2].rearrange("p (j t) -> p j t", j=4),
                                   bc(qs[:, (2 * h + k) * P:(2 * h + k) * P + 32].unsqueeze(1), [P, 4, 32]),
                                   seqcol[:, 4 * jh:4 * jh + 4, :], ALU.mult), ml_qm)

            own_parts(0)
            for i in range(16):
                h, jh = i // 4, i % 2
                if i + 1 < 16:
                    own_parts(i + 1)
                for j in range(4):
                    n = 4 * i + j
                    dve.wait_ge(ml_st, 4 * NS + n + 1)
                    t = CB[i % NCB][:, j, :]
                    do(v.scalar_tensor_tensor(t, t, wpb[:, h, 4 + 4 * jh + j:5 + 4 * jh + j],
                                              PS[:, 4 + n % 4, 0:257], ALU.mult, ALU.add), ml_upd)
                dve.sem_inc(ml_updone, 1)
            head_outputs(NS, L, 0, 4, 0, c, hstat)
            head_norm(NS, L, 0, 4, hstat)
            dve.wait_ge(ml_hT, NS + 1)
            for i in range(8):
                do(v.scalar_tensor_tensor(proj[:, 24 + i, cols], banks(4, 2)[:, i * P:i * P + L],
                                          vv("mlstm_norm_w", i), proj[:, 24 + i, cols], ALU.mult, ALU.mult),
                   dve_step if i < 7 else ml_out)
            merge("merge1", 1)

            dve.wait_ge(ml_stdone, NS + 1)
            dve.wait_ge(evac_up, 8)
            dve.wait_ge(pool_loaded, 16)
            do(v.memset(padP[0][:, :, 0:15], 0.0))
            do(v.tensor_copy(padP[0][:, :, 15:527], proj[:, 0:8, 0:TP]))
            do(v.tensor_copy(padS[0][:, :, :, 15:19], smp(proj[:, 0:8, TP:NT])))
            for k in range(4):
                d, lo = 1 << k, (2 << k) - 1
                src, dst = k % 2, (k + 1) % 2
                do(v.tensor_tensor(padP[dst][:, 2 * k:8, lo:527], padP[src][:, 2 * k:8, lo:527],
                                   padP[src][:, 2 * k:8, lo - d:527 - d], ALU.add))
                for i in range(2 * k, 8):
                    do(v.tensor_tensor(padS[dst][:, i, :, lo:19], padS[src][:, i, :, lo:19],
                                       padS[src][:, i, :, lo - d:19 - d], ALU.add))
            for g in range(4):
                w, b = 2 << g, (g + 1) % 2
                t2 = slice(2 * g, 2 * g + 2)
                do(v.scalar_tensor_tensor(dpool[:, t2, 0:TP], padP[b][:, t2, 15:527], 1.0 / w, proj[:, t2, 0:TP],
                                          ALU.mult, ALU.subtract))
                a, _ = CST["invcnt"]
                do(v.tensor_tensor(dpool[:, t2, 0:w - 1], padP[b][:, t2, 15:14 + w],
                                   bc(C[:, a + 16 * g:a + 16 * g + w - 1].unsqueeze(1), [P, 2, w - 1]), ALU.mult))
                do(v.tensor_tensor(dpool[:, t2, 0:w - 1], dpool[:, t2, 0:w - 1], proj[:, t2, 0:w - 1], ALU.subtract))
                for i in range(2 * g, 2 * g + 2):
                    do(v.scalar_tensor_tensor(dpool[:, i, TP:NT].rearrange("p (j t) -> p j t", j=NSEQ),
                                              padS[b][:, i, :, 15:19], 1.0 / w,
                                              proj[:, i, TP:NT].rearrange("p (j t) -> p j t", j=NSEQ),
                                              ALU.mult, ALU.subtract), dve_step if i < 7 else pool_d)
            dve.wait_ge(ada_psum, 24)
            ada_finish(adaF, "b_ada_ffn", 7)
            merge("merge2", 2)

            def seq(t):
                return t[:, TP:NT].rearrange("p (j t) -> p j t", j=NSEQ)

            def per_seq(ada_, m):
                return bc(ada_[:, m, 1:9].unsqueeze(2), [P, NSEQ, TS])

            def layer_norm(n, r):
                dve.wait_ge(ln_mu, n + 1)
                for i in range(KT):
                    t = halves(r[:, i, :])
                    do(v.tensor_tensor(t, t, PS[:, 4:6, 0:HALF], ALU.subtract), ln_cen)
                dve.wait_ge(ln_sd, n + 1)
                do(v.reciprocal(gs[:, 1, :], gs[:, 0, :]))
                do(v.tensor_tensor(r[:, 0, :], r[:, 0, :], gs[:, 1, :], ALU.mult), ln_norm)
                for i in range(KT):
                    if i + 1 < KT:
                        do(v.tensor_tensor(r[:, i + 1, :], r[:, i + 1, :], gs[:, 1, :], ALU.mult), ln_norm)
                    if n == 0:
                        m = merged[:, i, :]
                        dve.wait_ge(ln_done, i + 1)
                        do(v.tensor_scalar(uT[:, i, 0:TP], m[:, 0:TP], adaF[:, 8 + i, 0:1], adaF[:, i, 0:1],
                                           ALU.mult, ALU.add))
                        do(v.tensor_tensor(seq(uT[:, i, :]), seq(m), per_seq(adaF, 8 + i), ALU.mult))
                        do(v.tensor_tensor(seq(uT[:, i, :]), seq(uT[:, i, :]), per_seq(adaF, i), ALU.add), u2_ready)

            dve.wait_ge(xr_loaded, 16)
            for i in range(KT):
                t = proj[:, i, :]
                dve.wait_ge(out_tile, i + 1)
                do(v.tensor_tensor(seq(t), seq(t), per_seq(adaM, 16 + i), ALU.mult))
                do(v.scalar_tensor_tensor(t, proj[:, 8 + i, :], ALPHA, t, ALU.mult, ALU.add), r_ready)
            layer_norm(0, proj[:, 0:8, :])

            R = lambda a, b: rt[:, :, a:b]
            rank = bc(cc("rank").unsqueeze(1), [P, 5, 4])
            do(v.memset(rt[:], 0.0))
            dve.wait_ge(rt_psum, 1)
            do(v.tensor_tensor(rt[:, 0:4, 0:20], PS[:, 4, 0:80].rearrange("p (c n) -> p c n", c=4),
                               bc(vv("b_rt", 0, 20).unsqueeze(1), [P, 4, 20]), ALU.add))
            do(v.tensor_tensor(rt[0:32, 4, 0:20], PS[0:32, 4, 80:100], vv("b_rt", 0, 20)[0:32, :], ALU.add))

            def one_hot(src, mx, tmp, mn, dst):
                do(v.tensor_reduce(mx, src, AX.X, ALU.max))
                do(v.tensor_tensor(tmp, src, bc(mx, [P, 5, 4]), ALU.is_equal))
                do(v.tensor_tensor(tmp, tmp, rank, ALU.mult))
                do(v.tensor_reduce(mn, tmp, AX.X, ALU.min))
                do(v.tensor_tensor(dst, rank, bc(mn, [P, 5, 4]), ALU.is_equal))

            one_hot(R(0, 4), R(20, 21), R(24, 28), R(21, 22), R(28, 32))
            do(v.tensor_tensor(R(24, 28), R(0, 4), bc(R(20, 21), [P, 5, 4]), ALU.subtract), rt_d)
            dve.wait_ge(rt_e, 1)
            do(v.tensor_reduce(R(22, 23), R(24, 28), AX.X, ALU.add))
            do(v.reciprocal(R(22, 23), R(22, 23)))
            g4 = R(32, 48).rearrange("p c (g j) -> p c g j", g=4)
            do(v.tensor_tensor(g4, R(4, 20).rearrange("p c (g j) -> p c g j", g=4),
                               bc(R(28, 32).unsqueeze(3), [P, 5, 4, 4]), ALU.mult))
            do(v.tensor_reduce(R(48, 52), R(32, 48).rearrange("p c (g j) -> p c j g", g=4), AX.X, ALU.add))
            one_hot(R(48, 52), R(20, 21), R(24, 28), R(21, 22), R(52, 56))
            do(v.tensor_scalar(R(24, 28), R(52, 56), -BIG, None, ALU.mult))
            do(v.tensor_tensor(R(48, 52), R(48, 52), R(24, 28), ALU.add))
            one_hot(R(48, 52), R(23, 24), R(24, 28), R(21, 22), R(56, 60))
            do(v.tensor_tensor(R(60, 61), R(23, 24), R(20, 21), ALU.subtract), rt_dd)
            dve.wait_ge(rt_e2, 1)
            do(v.tensor_scalar(R(61, 62), R(60, 61), 1.0, None, ALU.add))
            do(v.reciprocal(R(61, 62), R(61, 62)))
            do(v.tensor_tensor(R(61, 62), R(61, 62), R(22, 23), ALU.mult))
            do(v.tensor_tensor(R(62, 63), R(61, 62), R(60, 61), ALU.mult))
            g44 = lambda a: R(a, a + 16).rearrange("p c (g j) -> p c g j", g=4)
            for a, o in ((64, 52), (80, 56)):
                do(v.tensor_tensor(g44(a), bc(R(28, 32).unsqueeze(3), [P, 5, 4, 4]), bc(R(o, o + 4).unsqueeze(2), [P, 5, 4, 4]),
                                   ALU.mult))
            do(v.tensor_tensor(R(96, 112), R(64, 80), R(80, 96), ALU.add))
            do(v.memset(rt[32:64, 4, 96:112], 0.0))
            do(v.memset(rt[64:P, 4, 96:112], 0.0), ohs_ready)
            tot, xtra, offs, dbase = (route[:, 16 * i:16 * i + 16] for i in range(4))
            dve.wait_ge(cnt_psum, 1)
            do(v.tensor_copy(tot, PS[:, 4, 80:96]))
            do(v.memset(rt[:, 4, 112:128], 0.0))
            do(v.tensor_copy(rt[:, 0:4, 112:128], PS[:, 4, 0:64].rearrange("p (c e) -> p c e", c=4)))
            do(v.tensor_copy(rt[0:32, 4, 112:128], PS[0:32, 4, 64:80]), cnt_used)
            do(v.tensor_scalar(xtra, tot, P + 0.5, None, ALU.is_gt))
            for j in (2, 3, 4):
                do(v.scalar_tensor_tensor(xtra, tot, j * P + 0.5, xtra, ALU.is_gt, ALU.add))
            do(v.tensor_tensor_scan(offs, one[:, 0:NE], xtra, 0.0, ALU.mult, ALU.add))
            do(v.scalar_tensor_tensor(dbase, offs, NE - 1.0, xtra, ALU.add, ALU.subtract))
            do(v.tensor_tensor(dbase, dbase, cc("eid"), ALU.subtract))
            cnt, tmp = R(112, 128), R(128, 144)
            J = R(144, 160)
            do(v.tensor_scalar(J, cnt, P + 0.5, None, ALU.is_gt))
            do(v.tensor_tensor(tmp, J, bc(dbase.unsqueeze(1), [P, 5, NE]), ALU.mult))
            for j in (2, 3, 4):
                do(v.scalar_tensor_tensor(J, cnt, j * P + 0.5, J, ALU.is_gt, ALU.add))
            do(v.scalar_tensor_tensor(tmp, J, 1.0 - NB * P, tmp, ALU.mult, ALU.add))
            do(v.scalar_tensor_tensor(tmp, cnt, float(NB), tmp, ALU.mult, ALU.add))
            do(v.tensor_tensor(tmp, tmp, bc(cc("eid").unsqueeze(1), [P, 5, NE]), ALU.add))
            for k, a in enumerate((64, 80)):
                do(v.tensor_tensor(cnt, R(a, a + 16), tmp, ALU.mult))
                do(v.tensor_reduce(route[:, 80 + 5 * k:85 + 5 * k].unsqueeze(2), cnt, AX.X, ALU.add))
            do(v.tensor_scalar(route[:, 80:90], route[:, 80:90], -float(NB), None, ALU.add))
            do(v.tensor_copy(ridx[:, 24:34], route[:, 80:90]))
            do(v.tensor_copy(ridx[:, 40:45], cc("tok")))
            xbt = G[:, 0, 0:XB * NE].rearrange("p (b e) -> p b e", b=XB)
            do(v.tensor_tensor(xbt, bc(offs.unsqueeze(1), [P, XB, NE]), bc(cc("xb").unsqueeze(2), [P, XB, NE]), ALU.is_le))
            do(v.tensor_reduce(route[:, 96:96 + XB].unsqueeze(2), xbt, AX.X, ALU.add))
            do(v.tensor_scalar(route[:, 96:96 + XB], route[:, 96:96 + XB], NE - 1.0, None, ALU.min))
            do(v.tensor_copy(ridx[:, 48:48 + XB], route[:, 96:96 + XB]))
            do(v.tensor_copy(n_further, offs[0:1, NE - 1:NE]), pos_ready)

            def hidden(b, it=None):
                i, v_ = b % NBUF, (b + 1 if it is None else it * NBUF + (b + 1))
                dve.wait_ge(sg_ready, v_)
                v.tensor_tensor(H3[i], H3[i], PS[:, 2, 256:512], ALU.mult).then_inc(h_ready, 1)

            def hidden_back(b, it=None):
                i, v_ = b % NBUF, (b + 1 if it is None else it * NBUF + (b + 1))
                dve.wait_ge(h_psum, v_)
                v.tensor_copy(HT3[i], PS[:, 3, 0:256]).then_inc(hT_ready, 1)

            def result(b, it=None):
                i, v_ = b % NBUF, (b + 1 if it is None else it * NBUF + (b + 1))
                dve.wait_ge(y_psum, v_)
                if b >= NBUF:
                    k = 16 * (b // NBUF)
                    dve.wait_ge(y_stored[i], k if it is None else it * 16 + k)
                v.tensor_copy(Y3[i], banks(4, 2)).then_inc(y_ready, 1)

            def step(b, it=None, first=False):
                hidden(b, it)
                if not first:
                    result(b - 1, it)
                hidden_back(b, it)

            def run_blocks(first, last):
                peel = 1 if first else 1 + NBUF
                turns = (last - first - peel) // NBUF
                for b in range(first, first + peel):
                    step(b, first=b == first)
                with dve.Fori(0, turns) as it:
                    for b in range(first + peel, first + peel + NBUF):
                        step(b, it)
                for b in range(first + peel + turns * NBUF, last):
                    step(b)
                result(last - 1)

            further = dve.value_load(n_further, min_val=0, max_val=XB)
            run_blocks(0, NE)
            with dve.If(further > 0):
                run_blocks(NE, NB)
            for c, (t0, L) in enumerate(CHUNKS):
                dve.wait_ge(back_got[c], 32)
                a, b = BK[c][0][0:L, :], BK[c][1][0:L, :]
                do(v.tensor_scalar(a, a, rt[0:L, c, 61:62], None, ALU.mult))
                do(v.scalar_tensor_tensor(a, b, rt[0:L, c, 62:63], a, ALU.mult, ALU.add), moe_ready)
            dve.wait_ge(moeT_ready, 5)
            for i in range(KT):
                t = uT[:, i, :]
                do(v.tensor_scalar(t[:, 0:TP], t[:, 0:TP], adaF[:, 16 + i, 0:1], None, ALU.mult))
                do(v.tensor_tensor(seq(t), seq(t), per_seq(adaF, 16 + i), ALU.mult))
                do(v.scalar_tensor_tensor(merged[:, i, :], merged[:, i, :], ALPHA, t, ALU.mult, ALU.add), r_ready)
            layer_norm(1, merged[:])


INS = ("wstream", "xT", "cT", "cst", "vec", "wgate", "segm", "wrt", "wexp", "ssd0", "conv0", "caug0", "m0", "pool0", "pool_raw")
OUTS = (("yT", (P, KT, NT)), ("ssd_p", (P, 1024)), ("conv_p", (P, 12, 3)), ("cm_p", (P, 2056)), ("mm_p", (4, 1)),
        ("pool_p", (P, 8, 15)), ("ssd_s", (2, P, 4096)), ("conv_s", (P, 12, 32)), ("cm_s", (16, P, 4, 257)),
        ("mm_s", (4, 32)), ("pool_s", (P, 8, 32)),
        ("pool_old", (NSEQ, 11 * D)))


def constants(np):
    c = np.zeros((P, NCST), np.float32)

    def put(name, a):
        s, w = CST[name]
        a = np.asarray(a, np.float32)
        c[:a.shape[0], s:s + w] = a.reshape(a.shape[0], w)

    i = np.arange(P)
    put("ident", np.eye(P))
    put("one", np.ones((P, P)))
    put("mean", np.full((P, P), 1.0 / D))
    mask = (i[:, None] <= i[None, :]) * 1.0
    put("mask", mask)
    put("mask16", mask / 16)
    q = np.arange(32)
    sm = ((q[:, None] <= q[None, :]) & (q[:, None] // TS == q[None, :] // TS)) * 1.0
    put("smask", sm)
    put("smask16", sm / 16)
    own = (q[:, None] // TS == np.arange(NSEQ)[None, :]) * 1.0
    put("tokseq", own)
    put("seqcol", np.broadcast_to(own.T.reshape(1, -1), (P, NSEQ * 32)))
    put("rank", np.broadcast_to(np.arange(4) - 4.0, (P, 4)))
    inv = np.stack([1.0 / np.minimum(np.arange(16) + 1, 2 << g) for g in range(4)])
    put("invcnt", np.broadcast_to(inv.reshape(1, -1), (P, 64)))
    put("eid", np.broadcast_to(np.arange(NE), (P, NE)))
    put("xb", np.broadcast_to(np.arange(XB), (P, XB)))
    put("tok", np.arange(P)[:, None] + P * np.arange(5)[None, :])
    put("eps", np.broadcast_to(np.array([1e-5, 1e-6]), (P, 2)))
    s = np.zeros((P, 16, P))
    for h in range(16):
        s[h, h] = 1.0
    for h in range(4):
        s[64 + h, h] = 1.0
    put("sel", s)
    seg = np.ones((P, NT), np.float32)
    seg[:, [0, 128, 256, 384] + [TP + TS * j for j in range(NSEQ)]] = 0.0
    return c, seg


def lay_out(np, t):
    f = np.float32
    w = {k: np.asarray(v) for k, v in t.items()}
    w = {k: (v[0] if k not in ("x_prompt", "x_sample", "c_prompt", "c_sample") else v) for k, v in w.items()}

    def blocks(m):
        n = m.shape[1] // 256
        return np.ascontiguousarray(m.reshape(KT, P, n, 256).transpose(2, 1, 0, 3)).reshape(n, P, 2048)

    def paired(a, b):
        return np.stack([blocks(a), blocks(b)], axis=1).reshape(-1, P, 2048)

    win = w["w_in"]
    o = np.cumsum([0, 1024, 1536, 16, 1024, 1024, 1024, 4, 4, 1024, 1024, 3072])
    sec = lambda i: win[:, o[i]:o[i + 1]]
    gl = sec(10).reshape(D, 3, D)
    pw = w["pool_w"].reshape(4, 2, P, 256).transpose(2, 0, 1, 3).reshape(1, P, 2048)
    eg, eu = w["w_e_gate"], w["w_e_up"]
    gu = np.concatenate([eg, eu], axis=2).reshape(NE, KT, P, 512).transpose(0, 2, 1, 3).reshape(NE, P, 4096)
    wexp = np.concatenate([gu, w["w_e_down"].reshape(NE, 2, P, D).transpose(0, 2, 1, 3).reshape(NE, P, 2048)], axis=2)
    stream = np.concatenate([
        blocks(w["w_ada_mix"]), blocks(sec(0)), blocks(sec(1)), paired(gl[:, 0], w["w_br_ssd"]),
        blocks(sec(3)), blocks(sec(4)), blocks(sec(5)), blocks(sec(8)), paired(gl[:, 1], w["w_br_mlstm"]),
        blocks(sec(9)), blocks(w["w_ada_ffn"]), pw, paired(gl[:, 2], w["w_br_pool"]), blocks(w["w_out"])])
    tile_rows = lambda m: np.ascontiguousarray(m.reshape(m.shape[0] // P, P, -1).transpose(1, 0, 2))
    x = np.concatenate([w["x_prompt"].reshape(TP, D), w["x_sample"].reshape(-1, D)])
    c = np.concatenate([w["c_prompt"], w["c_sample"]])
    wgate = np.zeros((D, 68), f)
    wgate[:, 0:16], wgate[:, 32:36], wgate[:, 64:68] = sec(2), sec(6), sec(7)
    vec = np.zeros((P, NVEC), f)

    def put(name, a, rows=P):
        s, n = VEC[name]
        vec[:rows, s:s + n] = a

    feat = lambda v: v.reshape(-1, P).T
    for n in ("b_ada_mix", "b_ada_ffn", "gate_b", "conv_b", "ssd_norm_w", "mlstm_norm_w", "pool_scale", "ln1_g", "ln1_b",
              "ln2_g", "ln2_b"):
        put(n, feat(w[n]))
    put("conv_w", feat(w["conv_w"].reshape(-1)))
    put("ssd_D", feat(np.broadcast_to(w["ssd_D"][:, None], (16, 64)).reshape(-1)))
    s, _ = VEC["row_bias"]
    vec[0:16, s], vec[32:36, s], vec[64:68, s] = w["ssd_dt_bias"], w["mlstm_gate_b"][:4], w["mlstm_gate_b"][4:]
    put("a_log", w["ssd_A_log"][:, None], 16)
    put("b_rt", np.broadcast_to(np.concatenate([w["b_rt_group"], w["b_rt_expert"]]), (P, 20)))
    cst, seg = constants(np)
    C0, n0 = w["state_mlstm_C"], w["state_mlstm_n"]
    ca = np.concatenate([C0.transpose(0, 1, 3, 2), n0[..., None]], axis=-1)
    ca = ca.reshape(2, 4, 4, 2, P, 257).transpose(2, 3, 0, 4, 1, 5).reshape(16, P, 4, 257)
    ssd0 = w["state_ssd"].reshape(NSEQ, 2, 8 * 64, P).transpose(1, 3, 0, 2).reshape(2, P, 4096)
    return {
        "wstream": stream, "xT": tile_rows(np.ascontiguousarray(x.T)), "cT": tile_rows(np.ascontiguousarray(c.T)),
        "cst": cst, "vec": vec, "wgate": tile_rows(wgate).reshape(P, -1), "segm": seg,
        "wrt": tile_rows(np.concatenate([w["w_rt_group"], w["w_rt_expert"]], axis=1)),
        "wexp": wexp, "ssd0": ssd0, "conv0": w["state_conv"].reshape(NSEQ, 3, 12, P).transpose(3, 2, 0, 1), "caug0": ca,
        "m0": w["state_mlstm_m"].T, "pool0": w["state_pool"].reshape(NSEQ, 15, 8, P).transpose(3, 2, 0, 1),
        "pool_raw": w["state_pool"].reshape(NSEQ, 15 * D),
    }


def kernel(**inputs):
    import numpy as np
    import concourse.bacc as bacc
    from concourse.bass_utils import run_bass_kernel_spmd as run

    nc = bacc.Bacc("TRN2", target_bir_lowering=False, num_devices=1)
    laid = lay_out(np, inputs)
    arrays, args = {}, []
    for name in INS:
        a = np.ascontiguousarray(laid[name])
        arrays["in_" + name] = a
        args.append(nc.dram_tensor("in_" + name, a.shape, mybir.dt.from_np(a.dtype), kind="ExternalInput").ap())
    for name, shape in OUTS:
        args.append(nc.dram_tensor("out_" + name, shape, F32, kind="ExternalOutput").ap())
    args.append(nc.dram_tensor("slot_tokens", (P * NB, 1), U32).ap())
    args.append(nc.dram_tensor("u2_rows", (NT, D), F32).ap())
    args.append(nc.dram_tensor("expert_rows", (P * NB, D), F32).ap())
    program(nc, *args)
    r = run(nc, [arrays], core_ids=[0]).results[0]
    g = {name: np.asarray(r["out_" + name]) for name, _ in OUTS}

    y = g["yT"].transpose(2, 1, 0).reshape(NT, D)
    ssd_p = g["ssd_p"].T.reshape(1, 1, 16, 64, P)
    ssd_s = g["ssd_s"].reshape(2, P, NSEQ, 512).transpose(2, 0, 3, 1).reshape(1, NSEQ, 16, 64, P)
    conv_p = g["conv_p"].transpose(2, 1, 0).reshape(1, 1, 3, 1536)
    conv_s = g["conv_s"].transpose(2, 1, 0).reshape(1, NSEQ, TS, 1536)[:, :, 1:]
    cp = g["cm_p"].reshape(P, 4, 2, 257).transpose(1, 3, 2, 0).reshape(1, 1, 4, 257, 256)
    cs = g["cm_s"].reshape(4, 2, 2, P, 4, 257).transpose(2, 4, 0, 5, 1, 3).reshape(1, NSEQ, 4, 257, 256)
    pool_p = g["pool_p"].transpose(2, 1, 0).reshape(1, 1, 15, D)
    up_s = g["pool_s"].transpose(2, 1, 0).reshape(1, NSEQ, TS, D)
    pool_s = np.concatenate([g["pool_old"].reshape(1, NSEQ, 11, D), up_s], axis=2)
    out = (y[:TP].reshape(1, TP, D), y[TP:].reshape(NSEQ, TS, D),
           ssd_p, conv_p, cp[:, :, :, :256], cp[:, :, :, 256], g["mm_p"].reshape(1, 1, 4), pool_p,
           ssd_s, conv_s, cs[:, :, :, :256], cs[:, :, :, 256], g["mm_s"][:, TS - 1::TS].T.reshape(1, NSEQ, 4), pool_s)
    return tuple(np.ascontiguousarray(a) for a in out)
```
